# Optimizing a Trainium2 kernel written in Bass

```python
import math
import jax, jax.numpy as jnp
from jax import lax
import numpy as np

D_MODEL = 1024
BATCH = 1
SEQ = 256
DEPTH = 1

CHUNK = 64
EPS = 1e-6
NEG = -1e30

A_HEADS = 4
A_DH = 128
A_WIDTH = A_HEADS * A_DH
CONV_W = 4
GATE_CAP = 15.0

B_HEADS = 8
B_DH = 64
B_WIDTH = B_HEADS * B_DH
B_LEFT_CHUNKS = 8
B_BAND = (B_LEFT_CHUNKS + 1) * CHUNK
B_MAX_REL = 256
B_REL_SIZE = 2 * B_MAX_REL + 1

C_HEADS = 4
C_DQK = 64
C_DV = 2 * C_DQK
C_WIDTH = C_HEADS * C_DV
Q_BLOCK = 128

T5_BUCKETS = 32
T5_MAX_DIST = 1024

N_BRANCH = 3
BRANCH_WIDTH = 512

N_GROUPS = 4
EXPERTS_PER_GROUP = 8
N_EXPERTS = N_GROUPS * EXPERTS_PER_GROUP
TOP_K = 2
D_EXPERT = D_MODEL // 4

IN_SIZES = (A_WIDTH, A_WIDTH, A_WIDTH, A_WIDTH, A_HEADS, A_HEADS,
            B_WIDTH, B_WIDTH, B_WIDTH,
            2 * C_HEADS * C_DQK, 2 * C_HEADS * C_DQK, C_WIDTH,
            N_BRANCH * D_MODEL)
IN_COLS = sum(IN_SIZES)
IN_SPLITS = tuple(int(v) for v in np.cumsum(IN_SIZES)[:-1])

kernel_name = 'hybrid_mlstm_bandattn_diffattn_hiermoe'

def rmsnorm(x, g):
    xf = x.astype(jnp.float32)
    xf = xf * lax.rsqrt(jnp.mean(xf * xf, axis=-1, keepdims=True) + EPS)
    return xf.astype(x.dtype) * g

def causal_conv(u, w, b):
    K = w.shape[0]
    S = u.shape[1]
    up = jnp.pad(u, ((0, 0), (K - 1, 0), (0, 0)))
    y = b + w[0] * u
    for j in range(1, K):
        y = y + w[j] * up[:, K - 1 - j:K - 1 - j + S]
    return y

def to_chunks(t):
    Bn, S, H = t.shape[:3]
    t = t.reshape((Bn, S // CHUNK, CHUNK, H) + t.shape[3:])
    return jnp.moveaxis(t, (1, 3), (0, 2))

def mlstm_chunkwise(q, k, v, ig, lf):
    Bn, S, H, D = q.shape
    in_dtype = v.dtype
    f32 = jnp.float32
    q = q.astype(f32)
    k = k.astype(f32) * (D ** -0.5)
    v = v.astype(f32)
    causal = jnp.tril(jnp.ones((CHUNK, CHUNK), dtype=bool))

    def step(carry, inp):
        C, n, m = carry
        qc, kc, vc, igc, lfc = inp
        b = jnp.cumsum(lfc, axis=-1)
        b_last = b[..., -1]
        dmat = jnp.where(causal, b[..., :, None] - b[..., None, :] + igc[..., None, :], NEG)
        inter = b + m[..., None]
        m_t = jnp.maximum(inter, jnp.max(dmat, axis=-1))
        w_inter = jnp.exp(inter - m_t)
        s = jnp.einsum('bhld,bhsd->bhls', qc, kc) * jnp.exp(dmat - m_t[..., None])
        num = w_inter[..., None] * jnp.einsum('bhld,bhde->bhle', qc, C) + jnp.einsum('bhls,bhse->bhle', s, vc)
        den = w_inter * jnp.einsum('bhld,bhd->bhl', qc, n) + jnp.sum(s, axis=-1)
        h = num / jnp.maximum(jnp.abs(den), jnp.exp(-m_t))[..., None]
        g_end = b_last[..., None] - b + igc
        m_new = jnp.maximum(b_last + m, jnp.max(g_end, axis=-1))
        dec = jnp.exp(b_last + m - m_new)
        w_end = jnp.exp(g_end - m_new[..., None])
        C_new = dec[..., None, None] * C + jnp.einsum('bhl,bhld,bhle->bhde', w_end, kc, vc)
        n_new = dec[..., None] * n + jnp.einsum('bhl,bhld->bhd', w_end, kc)
        return (C_new, n_new, m_new), h

    init = (jnp.zeros((Bn, H, D, D), f32), jnp.zeros((Bn, H, D), f32), jnp.zeros((Bn, H), f32))
    xs = (to_chunks(q), to_chunks(k), to_chunks(v), to_chunks(ig), to_chunks(lf))
    _, h = lax.scan(step, init, xs)
    h = jnp.moveaxis(h, (0, 2), (1, 3))
    return h.reshape(Bn, S, H, D).astype(in_dtype)

def chunk_band_attention(q, k, v, rel_table):
    Bn, S, H, D = q.shape
    nc = S // CHUNK
    pad = B_LEFT_CHUNKS * CHUNK
    kp = jnp.pad(k, ((0, 0), (pad, 0), (0, 0), (0, 0)))
    vp = jnp.pad(v, ((0, 0), (pad, 0), (0, 0), (0, 0)))
    qpos = jnp.arange(CHUNK)
    kpos = jnp.arange(B_BAND) - pad
    rel = jnp.clip(qpos[:, None] - kpos[None, :], -B_MAX_REL, B_MAX_REL) + B_MAX_REL
    bias = jnp.transpose(rel_table[rel], (2, 0, 1)).astype(jnp.float32)
    scale = D ** -0.5

    def one_chunk(c):
        start = c * CHUNK
        qc = lax.dynamic_slice_in_dim(q, start, CHUNK, axis=1)
        kc = lax.dynamic_slice_in_dim(kp, start, B_BAND, axis=1)
        vc = lax.dynamic_slice_in_dim(vp, start, B_BAND, axis=1)
        s = jnp.einsum('blhd,bkhd->bhlk', qc, kc).astype(jnp.float32) * scale + bias
        s = jnp.where((start + kpos) >= 0, s, NEG)
        p = jax.nn.softmax(s, axis=-1).astype(v.dtype)
        return jnp.einsum('bhlk,bkhd->blhd', p, vc)

    out = lax.map(one_chunk, jnp.arange(nc))
    return jnp.moveaxis(out, 0, 1).reshape(Bn, S, H * D)

def t5_bucket(rel):
    nb = T5_BUCKETS // 2
    max_exact = nb // 2
    ret = (rel > 0).astype(jnp.int32) * nb
    n = jnp.abs(rel)
    large = max_exact + (jnp.log(jnp.maximum(n, max_exact).astype(jnp.float32) / max_exact)
                         / math.log(T5_MAX_DIST / max_exact) * (nb - max_exact)).astype(jnp.int32)
    large = jnp.minimum(large, nb - 1)
    return ret + jnp.where(n < max_exact, n, large)

def diff_attention(q1, q2, k1, k2, v, t5_table, lam):
    Bn, S, H, D = q1.shape
    nblk = S // Q_BLOCK
    kpos = jnp.arange(S)
    scale = D ** -0.5

    def one_block(i):
        start = i * Q_BLOCK
        qp = start + jnp.arange(Q_BLOCK)
        bias = jnp.moveaxis(t5_table[t5_bucket(kpos[None, :] - qp[:, None])], -1, 0).astype(jnp.float32)
        allowed = (kpos[None, :] // CHUNK) <= (qp[:, None] // CHUNK)

        def probs(qf, kf):
            qb = lax.dynamic_slice_in_dim(qf, start, Q_BLOCK, axis=1)
            s = jnp.einsum('bqhd,bkhd->bhqk', qb, kf).astype(jnp.float32) * scale + bias
            return jax.nn.softmax(jnp.where(allowed, s, NEG), axis=-1)

        a = (probs(q1, k1) - lam * probs(q2, k2)).astype(v.dtype)
        return jnp.einsum('bhqk,bkhe->bqhe', a, v)

    out = lax.map(one_block, jnp.arange(nblk))
    return jnp.moveaxis(out, 0, 1).reshape(Bn, S, H, v.shape[-1])

def token_mixers(x, layer, norm_g, w_in, conv_w, conv_b, gate_bias, a_norm_g,
                 b_qk_g, b_rel, c_qk_g, c_lam, c_sub_g, t5_table, w_br, w_o):
    Bn, S, _ = x.shape
    h = rmsnorm(x, norm_g)
    aq, ak, av, ao, ai, af, bq, bk, bv, cq, ck, cv, gates = jnp.split(h @ w_in, IN_SPLITS, axis=-1)

    def heads(t, n):
        return t.reshape(Bn, S, n, -1)

    qk = jax.nn.silu(causal_conv(jnp.concatenate([aq, ak], axis=-1), conv_w, conv_b))
    aq, ak = jnp.split(qk, 2, axis=-1)
    ig = GATE_CAP * jnp.tanh((ai + gate_bias[:A_HEADS]).astype(jnp.float32) / GATE_CAP)
    lf = jax.nn.log_sigmoid((af + gate_bias[A_HEADS:]).astype(jnp.float32))
    ha = mlstm_chunkwise(heads(aq, A_HEADS), heads(ak, A_HEADS), heads(av, A_HEADS), ig, lf)
    ha = rmsnorm(ha, a_norm_g).reshape(Bn, S, A_WIDTH) * jax.nn.sigmoid(ao)

    bq = rmsnorm(heads(bq, B_HEADS), b_qk_g[0])
    bk = rmsnorm(heads(bk, B_HEADS), b_qk_g[1])
    hb = chunk_band_attention(bq, bk, heads(bv, B_HEADS), b_rel)

    cq = rmsnorm(cq.reshape(Bn, S, C_HEADS, 2, C_DQK), c_qk_g[0])
    ck = rmsnorm(ck.reshape(Bn, S, C_HEADS, 2, C_DQK), c_qk_g[1])
    lam_init = 0.8 - 0.6 * math.exp(-0.3 * layer)
    lf32 = c_lam.astype(jnp.float32)
    lam = jnp.exp(jnp.sum(lf32[0] * lf32[1])) - jnp.exp(jnp.sum(lf32[2] * lf32[3])) + lam_init
    hc = diff_attention(cq[..., 0, :], cq[..., 1, :], ck[..., 0, :], ck[..., 1, :],
                        heads(cv, C_HEADS), t5_table, lam)
    hc = (rmsnorm(hc, c_sub_g) * (1.0 - lam_init)).reshape(Bn, S, C_WIDTH)

    g = jax.nn.sigmoid(gates).reshape(Bn, S, N_BRANCH, D_MODEL)
    y = g[..., 0, :] * (ha @ w_br[0]) + g[..., 1, :] * (hb @ w_br[1]) + g[..., 2, :] * (hc @ w_br[2])
    return y @ w_o

def hier_moe(h, w_group, b_group, w_router, b_router, w_gate, w_up, w_down):
    Bn, S, D = h.shape
    N = Bn * S
    t = h.reshape(N, D)
    rows = jnp.arange(N)
    glog = (t @ w_group + b_group).astype(jnp.float32)
    g_idx = jnp.argmax(glog, axis=-1)
    p_g = jax.nn.softmax(glog, axis=-1)[rows, g_idx]
    elog = (t @ w_router + b_router).astype(jnp.float32).reshape(N, N_GROUPS, EXPERTS_PER_GROUP)
    ep = jax.nn.softmax(elog[rows, g_idx], axis=-1)
    top_p, top_i = lax.top_k(ep, TOP_K)
    top_p = top_p / jnp.sum(top_p, axis=-1, keepdims=True)
    weights = p_g[:, None] * top_p
    expert_id = g_idx[:, None] * EXPERTS_PER_GROUP + top_i
    combine = jnp.sum(jax.nn.one_hot(expert_id, N_EXPERTS, dtype=jnp.float32) * weights[..., None], axis=1)
    combine = combine.astype(t.dtype)
    out = jnp.zeros_like(t)
    for e in range(N_EXPERTS):
        he = jax.nn.silu(t @ w_gate[e]) * (t @ w_up[e])
        out = out + combine[:, e:e + 1] * (he @ w_down[e])
    return out.reshape(Bn, S, D)

def setup_inputs(seed: int = 0) -> dict:
    key = jax.random.key(seed)
    ks = jax.random.split(key, 26)
    L = DEPTH

    def nrm(k, shape, scale):
        return scale * jax.random.normal(k, shape, jnp.float32)

    def gain(k, shape):
        return 1.0 + nrm(k, shape, 0.02)

    i_bias = nrm(ks[5], (L, A_HEADS), 0.1) - 1.0
    f_bias = jnp.linspace(3.0, 6.0, A_HEADS)[None, :] + nrm(ks[6], (L, A_HEADS), 0.1)
    return {
        'x': nrm(ks[0], (BATCH, SEQ, D_MODEL), 1.0),
        'norm1_g': gain(ks[1], (L, D_MODEL)),
        'w_in': nrm(ks[2], (L, D_MODEL, IN_COLS), D_MODEL ** -0.5),
        'a_conv_w': nrm(ks[3], (L, CONV_W, 2 * A_WIDTH), CONV_W ** -0.5),
        'a_conv_b': nrm(ks[4], (L, 2 * A_WIDTH), 0.02),
        'a_gate_bias': jnp.concatenate([i_bias, f_bias], axis=-1),
        'a_out_norm_g': gain(ks[7], (L, A_HEADS, A_DH)),
        'b_qk_norm_g': gain(ks[8], (L, 2, B_DH)),
        'b_rel_bias': nrm(ks[9], (L, B_REL_SIZE, B_HEADS), 0.2),
        'c_qk_norm_g': gain(ks[10], (L, 2, C_DQK)),
        'c_lambda': nrm(ks[11], (L, 4, C_DQK), 0.1),
        'c_sub_norm_g': gain(ks[12], (L, C_DV)),
        't5_bias': nrm(ks[13], (T5_BUCKETS, C_HEADS), 0.2),
        'w_branch': nrm(ks[14], (L, N_BRANCH, BRANCH_WIDTH, D_MODEL), BRANCH_WIDTH ** -0.5),
        'w_out': nrm(ks[15], (L, D_MODEL, D_MODEL), D_MODEL ** -0.5),
        'norm2_g': gain(ks[16], (L, D_MODEL)),
        'w_group': nrm(ks[17], (L, D_MODEL, N_GROUPS), D_MODEL ** -0.5),
        'b_group': nrm(ks[18], (L, N_GROUPS), 0.01),
        'w_router': nrm(ks[19], (L, D_MODEL, N_EXPERTS), D_MODEL ** -0.5),
        'b_router': nrm(ks[20], (L, N_EXPERTS), 0.01),
        'w_e_gate': nrm(ks[21], (L, N_EXPERTS, D_MODEL, D_EXPERT), D_MODEL ** -0.5),
        'w_e_up': nrm(ks[22], (L, N_EXPERTS, D_MODEL, D_EXPERT), D_MODEL ** -0.5),
        'w_e_down': nrm(ks[23], (L, N_EXPERTS, D_EXPERT, D_MODEL), D_EXPERT ** -0.5),
    }

def reference(x, norm1_g, w_in, a_conv_w, a_conv_b, a_gate_bias, a_out_norm_g,
              b_qk_norm_g, b_rel_bias, c_qk_norm_g, c_lambda, c_sub_norm_g, t5_bias,
              w_branch, w_out, norm2_g, w_group, b_group, w_router, b_router,
              w_e_gate, w_e_up, w_e_down):
    for l in range(DEPTH):
        x = x + token_mixers(x, l, norm1_g[l], w_in[l], a_conv_w[l], a_conv_b[l], a_gate_bias[l],
                             a_out_norm_g[l], b_qk_norm_g[l], b_rel_bias[l], c_qk_norm_g[l],
                             c_lambda[l], c_sub_norm_g[l], t5_bias, w_branch[l], w_out[l])
        x = x + hier_moe(rmsnorm(x, norm2_g[l]), w_group[l], b_group[l], w_router[l], b_router[l],
                         w_e_gate[l], w_e_up[l], w_e_down[l])
    return x


_drawn_inputs = setup_inputs


def setup_inputs(seed=0):
    import zlib

    import numpy as np

    out = dict(_drawn_inputs(seed))
    spreads = {}
    factors = {'a_conv_b': 3.537,
     'a_out_norm_g': 23.211,
     'b_qk_norm_g': 4.824,
     'c_qk_norm_g': 4.491,
     'c_sub_norm_g': 16.238,
     'b_group': 18.982,
     'b_rel_bias': 6.573,
     'norm2_g': 4.063,
     'b_router': 6.678}
    for name, (base, spread) in spreads.items():
        noise = np.random.default_rng([zlib.crc32(name.encode()), seed]).standard_normal(out[name].shape)
        drawn = base * np.exp(spread * noise) if base else spread * noise
        out[name] = __import__('jax').numpy.asarray(drawn.astype(out[name].dtype))
    for name, factor in factors.items():
        out[name] = (out[name] * factor).astype(out[name].dtype)
    return out
```

```python
from contextlib import ExitStack

import concourse.bass as bass
from concourse import mybir

F32 = mybir.dt.float32
I32 = mybir.dt.int32
ALU = mybir.AluOpType
ACT = mybir.ActivationFunctionType
AX_X = mybir.AxisListType.X

P = 128
SEQ, D = 256, 1024
TT = SEQ // P
KD = D // P
CHUNK = 64
EPS = 1e-6
NEG = -1e30
LOWEST = -3e38
A_HEADS, A_DH = 4, 128
B_HEADS, B_DH = 8, 64
C_HEADS, C_DQK, C_DV = 4, 64, 128
B_MAX_REL = 256
T5_BUCKETS, T5_MAX_DIST = 32, 1024
GATE_CAP = 15.0
LAM_INIT = 0.2
WIDTH = 512
GROUPS, PER_GROUP, EXPERTS, D_EXPERT = 4, 8, 32, 256
FC = D_EXPERT // P
PAIRS = 2 * SEQ
WIN = 64
LIMIT = WIN
COLS = PAIRS + WIN
SLOTS = 4
EXPERT_FLOATS = 3 * KD * D_EXPERT

COL = dict(aq=0, ak=512, av=1024, ao=1536, aif=2048, bq=2056, bk=2568, bv=3080,
           cq=3592, ck=4104, cv=4616, g=5128)

CONST = {}
_at = 0
for _name, _width in (("ident", 128), ("ones", 128), ("tri", 128), ("strict", 128), ("blocks", 128),
                      ("mask_chunk", 256), ("mask_tri", 256), ("iota", PAIRS), ("pri", EXPERTS),
                      ("prig", GROUPS), ("eps", 1), ("t5hot", 384)):
    CONST[_name] = (_at, _at + _width)
    _at += _width
CONST_WIDTH = _at


def constants():
    import math

    import numpy as np

    c = np.zeros((P, CONST_WIDTH), np.float32)

    def put(name, value):
        a, b = CONST[name]
        c[:, a:b] = value

    i, j = np.arange(P)[:, None], np.arange(P)[None, :]
    put("ident", i == j)
    put("ones", 1.0)
    put("tri", i <= j)
    put("strict", i < j)
    put("blocks", i // 64 == j // 64)
    zero = np.zeros((P, P))
    put("mask_chunk", np.concatenate([zero, np.where(j // CHUNK <= i // CHUNK, 0.0, NEG)], 1))
    put("mask_tri", np.concatenate([zero, np.where(j <= i, 0.0, NEG)], 1))
    put("iota", np.arange(PAIRS)[None, :])
    put("pri", EXPERTS - np.arange(EXPERTS)[None, :])
    put("prig", GROUPS - np.arange(GROUPS)[None, :])
    put("eps", EPS)
    rel = 127 - np.arange(384)
    nb = T5_BUCKETS // 2
    exact = nb // 2
    n = np.abs(rel)
    f = np.float32
    large = exact + (np.log(np.maximum(n, exact).astype(f) / f(exact)) / f(math.log(T5_MAX_DIST / exact))
                     * f(nb - exact)).astype(np.int32)
    bucket = (rel > 0) * nb + np.where(n < exact, n, np.minimum(large, nb - 1))
    put("t5hot", 0.0)
    a, b = CONST["t5hot"]
    c[:T5_BUCKETS, a:b] = bucket[None, :] == np.arange(T5_BUCKETS)[:, None]
    return c


PIECES = []
for _kind, _name in (("norm", "cq"), ("norm", "ck"), ("value", "cv"), ("norm", "bq"), ("norm", "bk"),
                     ("value", "bv"), ("conv", "aq"), ("conv", "ak"), ("value", "av"), ("value", "ao")):
    for _half in range(2):
        PIECES.append((_kind, _name, _half))
    if _name == "bv":
        PIECES.append(("igate", "aif", 0))
for _g in range(12):
    PIECES.append(("gate", "g", _g))
NP = len(PIECES)

UNITS = [("C", h) for h in range(C_HEADS)] + [("B", h) for h in range(B_HEADS)] + [("A", h) for h in range(A_HEADS)]
NU = len(UNITS)
U0 = 9
DRAIN = 3


def build_hybrid_layer(nc, x, norm1_g, w_in, a_conv_w, a_conv_b, a_gate_bias, a_out_norm_g,
                       b_qk_norm_g, b_rel_bias, c_qk_norm_g, c_lambda, c_sub_norm_g, t5_bias,
                       w_branch, w_out, norm2_g, w_group, b_group, w_router, b_router,
                       w_e_gate, w_e_up, w_e_down, consts, scratch, out):
    ctx = ExitStack()
    with ctx:
        def sb(name, shape, dt=F32):
            return ctx.enter_context(nc.sbuf_tensor(name, shape, dt))

        def sem(name):
            return ctx.enter_context(nc.semaphore(name))

        xs = sb("xs", [P, TT, D])
        hT = sb("hT", [P, KD, SEQ])
        cst = sb("cst", [P, CONST_WIDTH])
        early = sb("early", [P, 2 * EXPERT_FLOATS])
        gates = sb("gates", [P, EXPERT_FLOATS])
        expert0 = sb("expert0", [P, EXPERT_FLOATS])
        stream = sb("stream", [P, 2 * KD * COLS])
        branchT = sb("branchT", [P, 3, 4, SEQ])
        yT = sb("yT", [P, KD, SEQ])
        small = sb("small", [64, P])
        par = sb("par", [P, 64])
        bc_norm = sb("bc_norm", [P, WIDTH + C_DV])
        bc_small = sb("bc_small", [P, 8 + 4 + EXPERTS])
        lam_in = sb("lam_in", [P, 4, C_DQK])
        w_if = sb("w_if", [P, KD, 8])
        w_rt = sb("w_rt", [P, KD, GROUPS + EXPERTS])
        g2 = sb("g2", [P, KD])
        t5 = sb("t5", [T5_BUCKETS, C_HEADS])
        t5v = sb("t5v", [P, 3, C_HEADS])
        work = sb("work", [P, 5632])
        st = sb("st", [P, 256])
        offs_i = sb("offs_i", [1, EXPERTS * 4 + 1], I32)
        offs_f = sb("offs_f", [1, EXPERTS * 4 + 1])

        def c(name, rows=P):
            a, b = CONST[name]
            return cst[0:rows, a:b]

        ident, ones = c("ident"), c("ones")
        eps = c("eps")

        qk = early[:, 0:24 * SEQ].rearrange("p (n t) -> p n t", t=SEQ)
        QK = dict(cq=0, ck=4, bq=8, bk=12, aq=16, ak=20)
        vals = early[:, 24 * SEQ:24 * SEQ + 3 * TT * WIDTH].rearrange("p (n t c) -> p n t c", n=3, t=TT)
        VAL = dict(cv=0, bv=1, av=2)
        bias = early[:, 9216:9216 + 12 * SEQ].rearrange("p (h k) -> p h k", k=SEQ)
        slots_w = [stream[:, n * 4096:(n + 1) * 4096] for n in range(2)]
        out_gate = stream[:, 8192:8192 + TT * WIDTH].rearrange("p (t c) -> p t c", t=TT)
        rel_raw = gates[:, 0:2048].rearrange("p (k h) -> p k h", h=B_HEADS)
        t5_raw = gates[:, 2048:3072].rearrange("p (k h) -> p k h", h=C_HEADS)
        gate_s = gates[:, :].rearrange("p (n t) -> p n t", t=SEQ)
        xg = stream[:, 0:KD * COLS].rearrange("p (k n) -> p k n", n=COLS)
        yg = stream[:, KD * COLS:2 * KD * COLS].rearrange("p (k n) -> p k n", n=COLS)

        sq = [work[:, 512 * n:512 * n + 512] for n in range(2)]
        ug = [work[:, 1024 + 512 * n:1536 + 512 * n] for n in range(2)]
        ug_pair = work[:, 1024:2048]
        rs_w = [work[:, 2048 + 512 * n:2560 + 512 * n] for n in range(2)]
        S1 = [work[:, 3072 + 384 * n:3456 + 384 * n] for n in range(2)]
        S2 = [work[:, 3840 + 384 * n:4224 + 384 * n] for n in range(2)]
        PT = [work[:, 4608 + 384 * n:4992 + 384 * n] for n in range(1)]
        hx = [work[:, 4992 + 256 * n:5248 + 256 * n].rearrange("p (t c) -> p t c", t=TT) for n in range(2)]
        xhat = hT[:, :, :].rearrange("p k t -> p (k t)").rearrange("p (t d) -> p t d", t=TT)
        tT = yT[:, :, :]
        sel_g = [work[:, 512 * n:512 * n + 512] for n in range(TT)]
        sel_w = [work[:, 1024 + 512 * n:1536 + 512 * n] for n in range(TT)]
        selT = work[:, 2048:2048 + 4 * SEQ].rearrange("p (s t) -> p s t", t=SEQ)
        hid = [work[:, 3072 + 128 * n:3200 + 128 * n] for n in range(2)]
        eg = [work[:, 3328 + 128 * n:3456 + 128 * n] for n in range(2)]
        rt = work[:, 3584:5632]
        yrows = expert0[:, 0:4 * D].rearrange("p (s d) -> p s d", d=D)
        slot_mem = [expert0[:, :], early[:, 0:EXPERT_FLOATS], early[:, EXPERT_FLOATS:2 * EXPERT_FLOATS],
                    gates[:, :]]
        w_gate = [m[:, 0:2048].rearrange("p (k f) -> p k f", f=D_EXPERT) for m in slot_mem]
        w_up = [m[:, 2048:4096].rearrange("p (k f) -> p k f", f=D_EXPERT) for m in slot_mem]
        w_down = [m[:, 4096:6144].rearrange("p (f d) -> p f d", d=D) for m in slot_mem]

        def stat(at, n):
            return st[:, at:at + n]

        ss1, rstd1 = stat(0, 2), stat(2, 2)
        ss2, rstd2 = stat(4, 2), stat(6, 2)
        lam_s, lam_e, neg_lam = stat(8, 2), stat(10, 2), stat(12, 1)
        ig_z, ig_e, lf = stat(16, 16), stat(32, 16), stat(48, 8)
        ig_v, cum, src = stat(56, 8), stat(64, 8), stat(72, 8)
        mx = [stat(80 + 32 * n, 4) for n in range(3)]
        nm = [stat(84 + 32 * n, 4) for n in range(3)]
        sm = [stat(88 + 32 * n, 4) for n in range(3)]
        rc = [stat(92 + 32 * n, 4) for n in range(3)]
        nl = [stat(96 + 32 * n, 2) for n in range(3)]
        em = [stat(98 + 32 * n, 2) for n in range(3)]
        ssu = [stat(100 + 32 * n, 2) for n in range(3)]
        rsu = [stat(102 + 32 * n, 2) for n in range(3)]
        rr = [stat(104 + 32 * n, 2) for n in range(3)]
        mm = [stat(106 + 32 * n, 2) for n in range(3)]
        gc08 = bc_norm[:, WIDTH:WIDTH + C_DV]
        ga = bc_norm[:, 0:WIDTH]

        CONVW, CONVB, NORM1, QKG = 0, 32, 40, 48

        def bank(name):
            return ctx.enter_context(nc.psum_tensor(name, [P, 512], F32))

        piece_ps = [bank("piece0"), bank("piece1")]
        sum_ps = bank("sum_ps")
        score_ps = [bank("score0"), bank("score1")]
        turn_ps = bank("turn_ps")
        value_ps = bank("value_ps")
        outT_ps = bank("outT_ps")

        logit_ps = [sum_ps, outT_ps]

        x_in = [sem(f"x_in{n}") for n in range(TT)]
        const_in = sem("const_in")
        params_in = sem("params_in")
        rel_in, t5_in = sem("rel_in"), sem("t5_in")
        t5_out = sem("t5_out")
        router_in = sem("router_in")
        block_in = [sem("block_in0"), sem("block_in1")]
        xsq_done, xn_done, xT_done, hT_ready = sem("xsq_done"), sem("xn_done"), sem("xT_done"), sem("hT_ready")
        par_ps, par_ready = sem("par_ps"), sem("par_ready")
        t5_ps, t5v_ready = sem("t5_ps"), sem("t5v_ready")
        bias_ready = sem("bias_ready")
        lam_ready = sem("lam_ready")
        piece_done = sem("piece_done")
        bank_free = [sem("bank_free0"), sem("bank_free1")]
        sq_ready, ss_done, rs_ready, qk_ready = sem("sq_ready"), sem("ss_done"), sem("rs_ready"), sem("qk_ready")
        cexp_ready, cadd_ready, crec_ready, conv_ready = (sem("cexp_ready"), sem("cadd_ready"),
                                                          sem("crec_ready"), sem("conv_ready"))
        sadd_ready, srec_ready, outgate_ready = sem("sadd_ready"), sem("srec_ready"), sem("outgate_ready")
        ig_v_step, ig_a_step, ig_p_step = sem("ig_v_step"), sem("ig_a_step"), sem("ig_p_step")
        sc_done, mx_ready, ex_done, p_ready = sem("sc_done"), sem("mx_ready"), sem("ex_done"), sem("p_ready")
        sc_read, em_ready = sem("sc_read"), sem("em_ready")
        tp_done, pt_ready, pv_done = sem("tp_done"), sem("pt_ready"), sem("pv_done")
        hn_ready, hx_ready = sem("hn_ready"), sem("hx_ready")
        xt_done, branch_ready = sem("xt_done"), sem("branch_ready")
        zg_ready, y_ready = sem("zg_ready"), sem("y_ready")
        x1_ready = sem("x1_ready")
        xh_step = sem("xh_step")
        xh_ready = sem("xh_ready")
        th_done, tT_ready = sem("th_done"), sem("tT_ready")
        lg_done = sem("lg_done")
        rt_exp = sem("rt_exp")
        hot_ready, pos_done, sel_ready = sem("hot_ready"), sem("pos_done"), sem("sel_ready")
        offs_ready = sem("offs_ready")
        ga_done, xg_free, xg_ready_a, xg_ready_v = sem("ga_done"), sem("xg_free"), sem("xg_ready_a"), sem("xg_ready_v")
        selT_done, selT_ready = sem("selT_done"), sem("selT_ready")
        pads_ready = sem("pads_ready")
        v_step, a_step, p_step = sem("v_step"), sem("a_step"), sem("p_step")
        exp_in = [sem(f"exp_in{n}") for n in range(SLOTS)]
        FAST, GENERAL = ({name: sem(f"{path}_{name}") for name in
                          ("up_done", "exp_ready", "step", "hid_ready", "down_done", "down_read")}
                         for path in ("fast", "general"))
        general_in = sem("general_in")
        yg_ready = sem("yg_ready")
        yturn_done, yrow_ready, out_done, out_ready, stored = (sem("yturn_done"), sem("yrow_ready"), sem("out_done"),
                                                               sem("out_ready"), sem("stored"))

        blocks = []
        piece_block = []
        for kind, name, n in PIECES:
            if kind == "igate":
                piece_block.append(None)
            else:
                key = (name, n // 2 if kind == "gate" else 0)
                if key not in blocks:
                    blocks.append(key)
                piece_block.append(blocks.index(key))
        n_in = len(blocks)
        BRANCH_ORDER = (2, 1, 0)
        blocks += [("branch", b) for b in BRANCH_ORDER] + [("out", n) for n in range(2)]

        last_piece = [max(i for i, b in enumerate(piece_block) if b == n) for n in range(n_in)]
        last_piece += [NP + 4 * n + 3 for n in range(3)]

        def block_source(key):
            name, n = key
            if name == "branch":
                return w_branch[0, n].rearrange("(k p) n -> p k n", p=P), 4
            if name == "out":
                return w_out[0].rearrange("(k p) n -> p k n", p=P)[:, :, 512 * n:512 * n + 512], KD
            if name == "g":
                at = COL["g"] + D * BRANCH_ORDER[n // 2] + 512 * (n % 2)
            else:
                at = COL[name]
            return w_in[0].rearrange("(k p) n -> p k n", p=P)[:, :, at:at + 512], KD

        def block_sb(n, k):
            return slots_w[n % 2].rearrange("p (k n) -> p k n", k=k)

        norm_pieces = [i for i, p in enumerate(PIECES) if p[0] == "norm"]
        conv_pieces = [i for i, p in enumerate(PIECES) if p[0] == "conv"]
        sig_pieces = [i for i, p in enumerate(PIECES) if p[0] == "gate" or p[1] == "ao"]
        IG = [p[0] for p in PIECES].index("igate")
        turned = [u for u, (br, h) in enumerate(UNITS) if br != "B" or h % 2]
        normed = [u for u, (br, h) in enumerate(UNITS) if br != "B"]

        def freed(i):
            return i // 2 + 1

        def piece_of(name, half):
            return next(i for i, p in enumerate(PIECES) if p[1] == name and p[2] == half)

        def unit_in_slot(i, lag):
            u = i - U0 - lag
            return u if 0 <= u < NU else None

        def wait_values(eng, name):
            for half in range(2):
                i = piece_of(name, half)
                eng.wait_ge(bank_free[i % 2], freed(i))

        BR = dict(A=0, B=1, C=2)

        def xT_ps(k):
            return [piece_ps[0], piece_ps[1], score_ps[0], score_ps[1]][k // 2][:, SEQ * (k % 2):SEQ * (k % 2) + SEQ]

        def gather_ps(k):
            return [piece_ps[0], piece_ps[1], sum_ps][k % 3]

        def rt_of(t):
            at, found = 1024 * t, {}
            for name, n in (("lg", GROUPS + EXPERTS), ("gm", 1), ("ngm", 1), ("g4", GROUPS), ("gi", 1), ("el", EXPERTS),
                            ("m", 2), ("i", 2), ("o1", EXPERTS), ("o2", EXPERTS), ("hot", EXPERTS), ("bef", EXPERTS),
                            ("d", 1), ("ge", GROUPS), ("gs", 1), ("e2", 1), ("w", 2), ("pos", 2), ("tmp", PAIRS)):
                found[name] = rt[:, at:at + n]
                at += n
            return found

        def load_expert(eng, e, r, done=None):
            done = done or exp_in[r]
            eng.dma_start(w_gate[r], w_e_gate[0, bass.ds(e, 1)].rearrange("o (p k) f -> p (o k) f", k=KD)).then_inc(done, 16)
            eng.dma_start(w_up[r], w_e_up[0, bass.ds(e, 1)].rearrange("o (p k) f -> p (o k) f", k=KD)).then_inc(done, 16)
            eng.dma_start(w_down[r], w_e_down[0, bass.ds(e, 1)].rearrange("o (f p) d -> p (o f) d", p=P)).then_inc(done, 16)

        up_ps, down_ps = score_ps, [turn_ps, value_ps]

        def window(eng, e, j):
            return eng.value_load(offs_i[0:1, bass.ds(EXPERTS * j + e, 1)], min_val=0, max_val=PAIRS)

        def first(n, k):
            return isinstance(n, int) and n < k

        def window_up(pe, S, n, b, e, j, r):
            off = window(pe, e, j)
            if not first(n, 2):
                pe.wait_ge(S["hid_ready"], n - 1)
            for m, w in enumerate((w_gate[r], w_up[r])):
                for f in range(FC):
                    at = WIN * (FC * m + f)
                    for k in range(KD):
                        ins = pe.matmul(up_ps[b][:, at:at + WIN], w[:, k, P * f:P * f + P], xg[:, k, bass.ds(off, WIN)],
                                        start=(k == 0), stop=(k == KD - 1))
            ins.then_inc(S["up_done"], 1)

        def window_down(pe, S, n, b, r):
            pe.wait_ge(S["hid_ready"], n + 1)
            if not first(n, 2):
                pe.wait_ge(S["down_read"], n - 1)
            for ch in range(KD):
                for f in range(FC):
                    ins = pe.matmul(down_ps[b][:, WIN * ch:WIN * ch + WIN], w_down[r][:, f, P * ch:P * ch + P],
                                    hid[b][:, WIN * f:WIN * f + WIN], start=(f == 0), stop=(f == FC - 1))
            ins.then_inc(S["down_done"], 1)

        def window_exp(act, S, n, b):
            act.wait_ge(S["up_done"], n + 1)
            if not first(n, 2):
                act.wait_ge(S["hid_ready"], n - 1)
            act.activation(eg[b], up_ps[b][:, 0:FC * WIN], ACT.Exp, scale=-1.0).then_inc(S["exp_ready"], 1)

        def window_store(act, S, n, b, e, j):
            off = window(act, e, j)
            act.wait_ge(S["down_done"], n + 1)
            if not first(n, 1):
                act.wait_ge(S["down_read"], n)
            act.copy(yg[:, :, bass.ds(off, WIN)], down_ps[b][:, :].rearrange("p (k n) -> p k n", k=KD)).then_inc(S["down_read"], 1)

        WINDOWS = SEQ // WIN

        def general_path(eng):
            largest = eng.value_load(offs_i[0:1, WINDOWS * EXPERTS:WINDOWS * EXPERTS + 1], min_val=0, max_val=PAIRS)
            return eng.If(largest > LIMIT)

        def every_expert(eng, one):
            one(0)
            with eng.Fori(1, EXPERTS) as e:
                one(e)

        final_ps = [score_ps[0], score_ps[1], turn_ps, value_ps]

        def window_hidden(dve, S, n, b):
            dve.wait_ge(S["exp_ready"], n + 1)
            dve.tensor_scalar(eg[b], eg[b], 1.0, None, ALU.add).then_inc(S["step"], 1)
            dve.wait_ge(S["step"], n * 3 + 1)
            dve.reciprocal(eg[b], eg[b]).then_inc(S["step"], 1)
            dve.wait_ge(S["step"], n * 3 + 2)
            dve.tensor_tensor(eg[b], up_ps[b][:, 0:FC * WIN], eg[b], ALU.mult).then_inc(S["step"], 1)
            dve.wait_ge(S["step"], n * 3 + 3)
            if not first(n, 2):
                dve.wait_ge(S["down_done"], n - 1)
            dve.tensor_tensor(hid[b], up_ps[b][:, FC * WIN:2 * FC * WIN], eg[b], ALU.mult).then_inc(S["hid_ready"], 1)

        with nc.Block() as block:
            @block.sync
            def _(sp):
                for t in range(TT):
                    sp.dma_start(xs[:, t, :], x[0, P * t:P * t + P, :]).then_inc(x_in[t], 16)
                for n, key in enumerate(blocks):
                    if n >= 2:
                        sp.wait_ge(piece_done, last_piece[n - 2] + 1)
                    src_ap, k = block_source(key)
                    sp.dma_start(block_sb(n, k), src_ap).then_inc(block_in[n % 2], 16)
                    if n == 2:
                        load_expert(sp, 0, 0)
                    if n == n_in + 1:
                        sp.wait_ge(pv_done, NU)
                        sp.wait_ge(sc_read, NU)
                        load_expert(sp, 1, 1)
                        load_expert(sp, 2, 2)
                sp.wait_ge(zg_ready, 12)
                load_expert(sp, 3, 3)
                with sp.Fori(1, EXPERTS // SLOTS) as i:
                    for r in range(SLOTS):
                        sp.wait_ge(FAST["down_done"], (i - 1) * SLOTS + r + 1)
                        load_expert(sp, i * SLOTS + r, r)
                sp.wait_ge(offs_ready, 1)
                with general_path(sp):
                    sp.wait_ge(FAST["down_done"], EXPERTS)

                    def load(e):
                        if not first(e, 1):
                            sp.wait_ge(GENERAL["down_done"], e * WINDOWS)
                        load_expert(sp, e, 0, general_in)

                    every_expert(sp, load)
                for g in range(4):
                    t, half = g // 2, g % 2
                    sp.wait_ge(out_ready, g + 1)
                    sp.dma_start(out[0, P * t:P * t + P, 512 * half:512 * half + 512],
                                 xs[:, t, 512 * half:512 * half + 512]).then_inc(stored, 16)
                sp.wait_ge(stored, 64)

            @block.gpsimd
            def _(pool):
                pool.wait_ge(const_in, 16)
                pool.wait_ge(rel_in, 16)
                for h in range(B_HEADS):
                    pool.tensor_tensor(bias[:, C_HEADS + h, :], rel_raw[:, ::-1, h], c("mask_chunk"), ALU.add).then_inc(bias_ready, 1)
                pool.wait_ge(t5_in, 16)
                for h in range(C_HEADS):
                    pool.tensor_tensor(bias[:, h, :], t5_raw[:, ::-1, h], c("mask_chunk"), ALU.add).then_inc(bias_ready, 1)
                steps = 0
                for i in range(NP + 1):
                    if i >= 1 and i - 1 in norm_pieces:
                        n = norm_pieces.index(i - 1)
                        name, half = PIECES[i - 1][1:]
                        pool.wait_ge(rs_ready, n + 1)
                        pool.wait_ge(bank_free[(i - 1) % 2], freed(i - 1))
                        at = QK[name] + 2 * half
                        pool.tensor_tensor(qk[:, at:at + 2, :].rearrange("p n t -> p (n t)"), ug[n % 2], rs_w[n % 2],
                                           ALU.mult).then_inc(qk_ready, 1)
                    if i >= 1 and i - 1 in conv_pieces:
                        n = conv_pieces.index(i - 1)
                        name, half = PIECES[i - 1][1:]
                        pool.wait_ge(cexp_ready, n + 1)
                        pool.tensor_scalar(rs_w[n % 2], rs_w[n % 2], 1.0, None, ALU.add).then_inc(cadd_ready, 1)
                        pool.wait_ge(crec_ready, n + 1)
                        at = QK[name] + 2 * half
                        pool.tensor_tensor(qk[:, at:at + 2, :].rearrange("p n t -> p (n t)"), ug[n % 2], rs_w[n % 2],
                                           ALU.mult).then_inc(conv_ready, 1)
                    if i < NP and i in sig_pieces:
                        s = sig_pieces.index(i)
                        g = PIECES[i][2]
                        pool.wait_ge(bank_free[i % 2], freed(i))
                        buf = out_gate[:, g, :] if PIECES[i][1] == "ao" else gate_s[:, 2 * g:2 * g + 2, :].rearrange("p n t -> p (n t)")
                        pool.tensor_scalar(buf, buf, 1.0, None, ALU.add).then_inc(sadd_ready, 1)
                    if i >= 1 and i - 1 < NP and PIECES[i - 1][1] == "ao":
                        g = PIECES[i - 1][2]
                        pool.wait_ge(srec_ready, sig_pieces.index(i - 1) + 1)
                        pool.tensor_tensor(out_gate[:, g, :], out_gate[:, g, :], ga, ALU.mult).then_inc(outgate_ready, 1)
                for j in range(4, 12):
                    pool.wait_ge(zg_ready, j + 1)
                    if j >= 8:
                        pool.wait_ge(y_ready, j - 7)
                    o = yT[:, 2 * (j % 4):2 * (j % 4) + 2, :].rearrange("p n t -> p (n t)")
                    pool.tensor_tensor(o, o, sq[j % 2], ALU.add).then_inc(y_ready, 1)

            @block.scalar
            def _(act):
                act.dma_start(cst[:, :], consts).then_inc(const_in, 16)
                n_par = 0
                for rows, src_ap in (
                    (slice(0, 32), a_conv_w[0].rearrange("w (c p) -> (w c) p", p=P)),
                    (slice(32, 40), a_conv_b.rearrange("l (c p) -> (l c) p", p=P)),
                    (slice(40, 48), norm1_g.rearrange("l (c p) -> (l c) p", p=P)),
                ):
                    act.dma_start(small[rows, :], src_ap).then_inc(params_in, 16)
                    n_par += 1
                for at, g in ((48, b_qk_norm_g), (50, c_qk_norm_g)):
                    for half in range(2):
                        act.dma_start(small[at:at + 2, 64 * half:64 * half + 64], g[0]).then_inc(params_in, 16)
                        n_par += 1
                act.dma_start(w_if[:, :, :], w_in[0].rearrange("(k p) n -> p k n", p=P)[:, :, COL["aif"]:COL["aif"] + 8]).then_inc(params_in, 16)
                act.dma_start(t5[:, :], t5_bias).then_inc(params_in, 16)
                act.dma_start(lam_in[:, :, :].rearrange("p a b -> p (a b)"),
                              c_lambda.rearrange("l a b -> (l a b)").partition_broadcast(P)).then_inc(params_in, 16)
                act.dma_start(ga, a_out_norm_g.rearrange("l a b -> (l a b)").partition_broadcast(P)).then_inc(params_in, 16)
                act.dma_start(gc08, c_sub_norm_g.rearrange("l a -> (l a)").partition_broadcast(P)).then_inc(params_in, 16)
                act.dma_start(bc_small[:, 0:8], a_gate_bias.rearrange("l a -> (l a)").partition_broadcast(P)).then_inc(params_in, 16)
                act.dma_start(rel_raw.rearrange("p k h -> p (k h)"),
                              bass.AP(b_rel_bias.tensor, 129 * B_HEADS, [[B_HEADS, P], [1, SEQ * B_HEADS]])).then_inc(rel_in, 16)
                for dst, src_ap in (
                    (bc_small[:, 8:12], b_group.rearrange("l a -> (l a)").partition_broadcast(P)),
                    (bc_small[:, 12:44], b_router.rearrange("l a -> (l a)").partition_broadcast(P)),
                    (w_rt[:, :, 0:GROUPS], w_group[0].rearrange("(p k) n -> p k n", k=KD)),
                    (w_rt[:, :, GROUPS:], w_router[0].rearrange("(p k) n -> p k n", k=KD)),
                    (g2[:, :], norm2_g.rearrange("l (p k) -> (l p) k", k=KD)),
                ):
                    act.dma_start(dst, src_ap).then_inc(router_in, 16)

                for t in range(TT):
                    act.wait_ge(x_in[t], 16)
                    act.activation(work[:, 1024 * t:1024 * t + 1024], xs[:, t, :], ACT.Square, accum_out=ss1[:, t:t + 1]).then_inc(xsq_done, 1)
                act.wait_ge(xsq_done, TT)
                act.wait_ge(const_in, 16)
                act.activation(rstd1, ss1, ACT.Ln, bias=eps, scale=1.0 / D).then_inc(a_step, 1)
                act.wait_ge(a_step, 1)
                act.activation(rstd1, rstd1, ACT.Exp, scale=-0.5).then_inc(a_step, 1)
                act.wait_ge(par_ps, 1)
                act.copy(par[:, 0:52], sum_ps[:, 0:52]).then_inc(par_ready, 1)
                act.wait_ge(t5_ps, 1)
                act.copy(t5v[:, :, :].rearrange("p c h -> p (c h)"), outT_ps[:, 0:12]).then_inc(t5v_ready, 1)
                act.wait_ge(t5v_ready, 1)
                act.dma_start(scratch.rearrange("(c p h) -> p c h", p=P, h=C_HEADS), t5v[:, :, :]).then_inc(t5_out, 16)
                act.wait_ge(t5_out, 16)
                act.dma_start(t5_raw.rearrange("p k h -> p (k h)"),
                              bass.AP(scratch.tensor, 0, [[C_HEADS, P], [1, SEQ * C_HEADS]])).then_inc(t5_in, 16)
                act.wait_ge(lam_ready, 2)
                act.activation(lam_e, lam_s, ACT.Exp).then_inc(lam_ready, 1)
                steps = 2

                for i in range(NP + DRAIN + 1):
                    u = unit_in_slot(i, 0)
                    if i < NP:
                        kind, name, n = PIECES[i]
                        ps = piece_ps[i % 2]
                        act.wait_ge(piece_done, i + 1)
                        if kind == "norm":
                            j = norm_pieces.index(i)
                            if j >= 2:
                                act.wait_ge(ss_done, j - 1)
                            else:
                                act.wait_ge(xn_done, TT)
                            act.activation(sq[j % 2], ps[:, :], ACT.Square).then_inc(sq_ready, 1)
                        elif kind == "value" and name != "ao":
                            act.copy(vals[:, VAL[name], n, :], ps[:, :]).then_inc(bank_free[i % 2], 1)
                        elif kind == "value":
                            act.activation(out_gate[:, n, :], ps[:, :], ACT.Exp, scale=-1.0).then_inc(bank_free[i % 2], 1)
                        elif kind == "gate":
                            if n == 0:
                                act.wait_ge(bias_ready, 12)
                            act.activation(gate_s[:, 2 * n:2 * n + 2, :].rearrange("p n t -> p (n t)"), ps[:, :], ACT.Exp,
                                           scale=-1.0).then_inc(bank_free[i % 2], 1)
                    if i >= 1 and i - 1 in norm_pieces:
                        j = norm_pieces.index(i - 1)
                        act.wait_ge(ss_done, j + 1)
                        if j >= 2:
                            act.wait_ge(qk_ready, j - 1)
                        act.activation(rs_w[j % 2], sum_ps[:, :], ACT.Ln, bias=eps, scale=1.0 / B_DH).then_inc(a_step, 1)
                        steps += 1
                        act.wait_ge(a_step, steps)
                        act.activation(rs_w[j % 2], rs_w[j % 2], ACT.Exp, scale=-0.5).then_inc(rs_ready, 1)
                    if i < NP and i in conv_pieces:
                        j = conv_pieces.index(i)
                        act.wait_ge(bank_free[i % 2], freed(i))
                        if j >= 2:
                            act.wait_ge(conv_ready, j - 1)
                        else:
                            act.wait_ge(qk_ready, len(norm_pieces))
                        act.activation(rs_w[j % 2], ug[j % 2], ACT.Exp, scale=-1.0).then_inc(cexp_ready, 1)
                    if i == IG + 1:
                        act.wait_ge(ig_v_step, 3)
                        z3 = ig_z.rearrange("p (t n) -> p t n", t=TT)
                        e3 = ig_e.rearrange("p (t n) -> p t n", t=TT)
                        act.activation(e3[:, :, 0:4], z3[:, :, 0:4], ACT.Exp, scale=2.0 / GATE_CAP).then_inc(ig_a_step, 1)
                        act.activation(e3[:, :, 4:8], e3[:, :, 4:8], ACT.Exp, scale=-1.0).then_inc(ig_a_step, 1)
                        act.wait_ge(ig_a_step, 2)
                        act.activation(e3[:, :, 4:8], e3[:, :, 4:8], ACT.Ln, bias=1.0).then_inc(ig_a_step, 1)
                    if u is not None:
                        br, h = UNITS[u]
                        par_u, z = u % 2, u % 3
                        act.wait_ge(mx_ready, u + 1)
                        spans = [(0, 128), (128, 384)]
                        todo = []
                        for m, S in enumerate((S1[par_u], S2[par_u]) if br == "C" else (S1[par_u],)):
                            for t, (a, b) in enumerate(spans):
                                todo.append((S[:, a:b], 2 * m + t))
                        for j, (ap, col) in enumerate(todo):
                            kw = {} if br == "A" else dict(accum_out=sm[z][:, col:col + 1])
                            last = act.activation(ap, ap, ACT.Exp, bias=nm[z][:, col:col + 1], **kw)
                        last.then_inc(ex_done, 1)
                        if br == "A":
                            act.activation(em[z], mm[z], ACT.Exp).then_inc(em_ready, 1)
                    u = unit_in_slot(i, 1)
                    if u is not None:
                        act.wait_ge(tp_done, u + 1)
                        if u >= 1:
                            act.wait_ge(pv_done, u)
                        act.copy(PT[0], turn_ps[:, 0:384]).then_inc(pt_ready, 1)
                    u = unit_in_slot(i, 2)
                    if u is not None and UNITS[u][0] != "B":
                        par_u, z = u % 2, u % 3
                        act.wait_ge(pv_done, u + 1)
                        if u >= 2:
                            act.wait_ge(hx_ready, u - 1)
                        for t in range(TT):
                            kw = dict(scale=rc[z][:, t:t + 1]) if UNITS[u][0] == "A" else {}
                            act.activation(work[:, 5504:5632],
                                           value_ps[:, 128 * t:128 * t + 128], ACT.Square,
                                           accum_out=ssu[z][:, t:t + 1], **kw).then_inc(a_step, 1)
                            steps += 1
                            act.wait_ge(a_step, steps)
                        act.activation(rsu[z], ssu[z], ACT.Ln, bias=eps, scale=1.0 / C_DV).then_inc(a_step, 1)
                        steps += 1
                        act.wait_ge(a_step, steps)
                        act.activation(rsu[z], rsu[z], ACT.Exp, scale=-0.5).then_inc(hn_ready, 1)
                    u = unit_in_slot(i, 3)
                    if u is not None and u in turned:
                        br, h = UNITS[u]
                        ch = h // 2 if br == "B" else h
                        act.wait_ge(xt_done, turned.index(u) + 1)
                        act.copy(branchT[:, BR[br], ch, :], outT_ps[:, 0:SEQ]).then_inc(branch_ready, 1)

                for t in range(TT):
                    act.wait_ge(x1_ready, 2 * t + 2)
                    act.activation(ug_pair, xs[:, t, :], ACT.Square, accum_out=ss2[:, t:t + 1]).then_inc(a_step, 1)
                    steps += 1
                    act.wait_ge(a_step, steps)
                    act.activation(rstd2[:, t:t + 1], ss2[:, t:t + 1], ACT.Ln, bias=eps, scale=1.0 / D).then_inc(a_step, 1)
                    steps += 1
                    act.wait_ge(a_step, steps)
                    act.activation(rstd2[:, t:t + 1], rstd2[:, t:t + 1], ACT.Exp, scale=-0.5).then_inc(xh_step, 1)
                for t in range(TT):
                    for half in range(2):
                        act.wait_ge(th_done, 2 * t + half + 1)
                        act.copy(tT[:, 4 * half:4 * half + 4, P * t:P * t + P],
                                 [score_ps[0], score_ps[1], turn_ps, value_ps][2 * t + half][:, :]
                                 .rearrange("p (k n) -> p k n", k=4)).then_inc(tT_ready, 1)
                for t in range(TT):
                    act.wait_ge(hot_ready, 3 * t + 1)
                    R = rt_of(t)
                    act.activation(R["ge"], R["lg"][:, 0:GROUPS], ACT.Exp, bias=R["ngm"], accum_out=R["gs"]).then_inc(rt_exp, 1)
                    act.wait_ge(hot_ready, 3 * t + 2)
                    act.activation(R["e2"], R["d"], ACT.Exp).then_inc(rt_exp, 1)
                for k in range(0, KD, 2):
                    act.wait_ge(ga_done, k + 1)
                    act.activation(xg[:, k, 0:PAIRS], gather_ps(k)[:, :], ACT.Copy, scale=g2[:, k:k + 1]).then_inc(xg_ready_a, 1)
                for t in range(TT):
                    act.wait_ge(selT_done, t + 1)
                    act.copy(selT[:, :, P * t:P * t + P],
                             outT_ps[:, :].rearrange("p (s n) -> p s n", s=4)).then_inc(selT_ready, 1)
                for e in range(SLOTS):
                    window_exp(act, FAST, e, e % 2)
                    if e:
                        window_store(act, FAST, e - 1, (e - 1) % 2, e - 1, 0)
                with act.Fori(1, EXPERTS // SLOTS) as i:
                    for r in range(SLOTS):
                        e = i * SLOTS + r
                        window_exp(act, FAST, e, r % 2)
                        window_store(act, FAST, e - 1, (r - 1) % 2, e - 1, 0)
                window_store(act, FAST, EXPERTS - 1, 1, EXPERTS - 1, 0)
                with general_path(act):
                    act.wait_ge(FAST["hid_ready"], EXPERTS)
                    act.wait_ge(FAST["down_read"], EXPERTS)

                    def expert(e):
                        for j in range(WINDOWS):
                            window_exp(act, GENERAL, e * WINDOWS + j, j % 2)
                            window_store(act, GENERAL, e * WINDOWS + j, j % 2, e, j)

                    every_expert(act, expert)
                act.copy(st[:, 255:256], eps).then_inc(yg_ready, 1)
                for g in range(8):
                    s, half = g // 2, g % 2
                    act.wait_ge(yturn_done, g + 1)
                    act.copy(yrows[:, s, 512 * half:512 * half + 512], piece_ps[g % 2][:, :]).then_inc(yrow_ready, 1)

            @block.vector
            def _(dve):
                steps = 0
                for t in range(TT):
                    dve.wait_ge(a_step, 2)
                    dve.tensor_scalar(work[:, 2048 + 1024 * t:3072 + 1024 * t], xs[:, t, :], rstd1[:, t:t + 1], None,
                                      ALU.mult).then_inc(xn_done, 1)
                dve.wait_ge(params_in, 16 * 13)
                for j in range(2):
                    dve.tensor_tensor_reduce(work[:, 4096 + 64 * j:4160 + 64 * j], lam_in[:, 2 * j, :], lam_in[:, 2 * j + 1, :],
                                             1.0, 0.0, ALU.mult, ALU.add, lam_s[:, j:j + 1]).then_inc(lam_ready, 1)
                dve.wait_ge(par_ready, 1)
                for k in range(KD):
                    dve.wait_ge(xT_done, 2 * (k // 2) + 2)
                    dve.tensor_scalar(hT[:, k, :], xT_ps(k), par[:, NORM1 + k:NORM1 + k + 1], None, ALU.mult).then_inc(hT_ready, 1)
                dve.wait_ge(lam_ready, 3)
                dve.scalar_tensor_tensor(out=neg_lam, in0=lam_e[:, 1:2], scalar=LAM_INIT, in1=lam_e[:, 0:1],
                                         op0=ALU.subtract, op1=ALU.subtract).then_inc(lam_ready, 1)
                dve.tensor_scalar(gc08, gc08, 1.0 - LAM_INIT, None, ALU.mult).then_inc(lam_ready, 1)
                dve.tensor_scalar(par[:, 54:55], par[:, QKG:QKG + 1], B_DH ** -0.5, None, ALU.mult).then_inc(v_step, 1)
                dve.tensor_scalar(par[:, 55:56], par[:, QKG + 2:QKG + 3], C_DQK ** -0.5, None, ALU.mult).then_inc(v_step, 1)
                steps += 2
                dve.wait_ge(v_step, 2)
                gain = dict(bq=54, cq=55, bk=QKG + 1, ck=QKG + 3)

                for i in range(NP + DRAIN + 1):
                    if i == IG + 3:
                        dve.wait_ge(ig_p_step, 1)
                        dve.tensor_copy(cum, outT_ps[:, 0:8]).then_inc(ig_v_step, 1)
                        dve.wait_ge(ig_v_step, 8)
                        dve.tensor_tensor(src, ig_v, cum, ALU.subtract).then_inc(ig_v_step, 1)
                    if i < NP:
                        kind, name, n = PIECES[i]
                        ps = piece_ps[i % 2]
                        if kind == "norm":
                            j = norm_pieces.index(i)
                            dve.wait_ge(sq_ready, j + 1)
                            if j >= 2:
                                dve.wait_ge(qk_ready, j - 1)
                            dve.tensor_scalar(ug[j % 2], ps[:, :], par[:, gain[name]:gain[name] + 1], None,
                                              ALU.mult).then_inc(bank_free[i % 2], 1)
                        elif kind == "conv":
                            j = conv_pieces.index(i)
                            dve.wait_ge(piece_done, i + 1)
                            if j >= 2:
                                dve.wait_ge(conv_ready, j - 1)
                            else:
                                dve.wait_ge(qk_ready, len(norm_pieces))
                            ch0 = (0 if name == "aq" else 4) + 2 * n
                            for w in range(4):
                                for half in range(2):
                                    ch = ch0 + half
                                    col = par[:, CONVW + 8 * w + ch:CONVW + 8 * w + ch + 1]
                                    y = ug[j % 2][:, SEQ * half:SEQ * half + SEQ]
                                    uu = ps[:, SEQ * half:SEQ * half + SEQ]
                                    if w == 0:
                                        ins = dve.tensor_scalar(y, uu, col, par[:, CONVB + ch:CONVB + ch + 1], ALU.mult, ALU.add)
                                    else:
                                        dve.wait_ge(v_step, steps - 1)
                                        ins = dve.scalar_tensor_tensor(out=y[:, w:], in0=uu[:, :SEQ - w], scalar=col,
                                                                       in1=y[:, w:], op0=ALU.mult, op1=ALU.add)
                                    if w == 3 and half == 1:
                                        ins.then_inc(bank_free[i % 2], 1)
                                    else:
                                        ins.then_inc(v_step, 1)
                                        steps += 1
                                    if w == 3 and half == 0:
                                        dve.wait_ge(v_step, steps)
                        elif kind == "igate":
                            dve.wait_ge(piece_done, i + 1)
                            z3 = ig_z.rearrange("p (t n) -> p t n", t=TT)
                            e3 = ig_e.rearrange("p (t n) -> p t n", t=TT)
                            for t in range(TT):
                                ins = dve.tensor_tensor(z3[:, t, :], ps[:, 8 * t:8 * t + 8], bc_small[:, 0:8], ALU.add)
                                ins.then_inc(bank_free[i % 2] if t else ig_v_step, 1)
                            dve.wait_ge(ig_v_step, 1)
                            dve.wait_ge(bank_free[i % 2], freed(i))
                            dve.scalar_tensor_tensor(out=e3[:, :, 4:8], in0=z3[:, :, 4:8], scalar=-1.0, in1=z3[:, :, 4:8],
                                                     op0=ALU.mult, op1=ALU.max).then_inc(ig_v_step, 1)
                            dve.tensor_scalar(z3[:, :, 4:8], z3[:, :, 4:8], 0.0, None, ALU.min).then_inc(ig_v_step, 1)
                    if i >= 1 and i - 1 in conv_pieces:
                        j = conv_pieces.index(i - 1)
                        dve.wait_ge(cadd_ready, j + 1)
                        dve.reciprocal(rs_w[j % 2], rs_w[j % 2]).then_inc(crec_ready, 1)
                    if i >= 1 and i - 1 in sig_pieces:
                        s = sig_pieces.index(i - 1)
                        g = PIECES[i - 1][2]
                        dve.wait_ge(sadd_ready, s + 1)
                        buf = out_gate[:, g, :] if PIECES[i - 1][1] == "ao" else gate_s[:, 2 * g:2 * g + 2, :].rearrange("p n t -> p (n t)")
                        dve.reciprocal(buf, buf).then_inc(srec_ready, 1)
                    if i == IG + 2:
                        z3 = ig_z.rearrange("p (t n) -> p t n", t=TT)
                        e3 = ig_e.rearrange("p (t n) -> p t n", t=TT)
                        lf3 = lf.rearrange("p (t n) -> p t n", t=TT)
                        iv3 = ig_v.rearrange("p (t n) -> p t n", t=TT)
                        dve.wait_ge(ig_a_step, 3)
                        dve.tensor_tensor(lf3, z3[:, :, 4:8], e3[:, :, 4:8], ALU.subtract).then_inc(ig_v_step, 1)
                        dve.tensor_scalar(e3[:, :, 0:4], e3[:, :, 0:4], 1.0, None, ALU.add).then_inc(ig_v_step, 1)
                        dve.wait_ge(ig_v_step, 5)
                        dve.reciprocal(e3[:, :, 0:4], e3[:, :, 0:4]).then_inc(ig_v_step, 1)
                        dve.wait_ge(ig_v_step, 6)
                        dve.tensor_scalar(iv3, e3[:, :, 0:4], -2.0 * GATE_CAP, GATE_CAP, ALU.mult, ALU.add).then_inc(ig_v_step, 1)
                    u = unit_in_slot(i, 0)
                    if u is not None:
                        br, h = UNITS[u]
                        q, z = u % 2, u % 3
                        dve.wait_ge(sc_done, u + 1)
                        if u >= 2:
                            dve.wait_ge(tp_done, u - 1)
                        if br == "C" and h == 0:
                            dve.wait_ge(bias_ready, 12)
                            dve.wait_ge(lam_ready, 5)
                        if br in "BC":
                            hb = h if br == "C" else C_HEADS + h
                            maps = [(S1[q], score_ps[u % 2])] if br == "B" else [(S1[q], score_ps[0]), (S2[q], score_ps[1])]
                            adds = [(S, ps, bias[:, hb, :]) for S, ps in maps]
                        else:
                            adds = [(S1[q], None, c("mask_tri"))]
                        n_mx = 2 * len(adds)
                        for m, (S, ps, bb) in enumerate(adds):
                            for t in range(TT):
                                sa = slice(0, 128) if t == 0 else slice(128, 384)
                                pa = score_ps[1][:, 0:P * (t + 1)] if br == "A" else ps[:, sa]
                                ins = dve.tensor_tensor_reduce(S[:, sa], pa, bb[:, P * (1 - t):SEQ], 1.0, LOWEST,
                                                               ALU.add, ALU.max, mx[z][:, 2 * m + t:2 * m + t + 1])
                                if br != "A" and m == len(adds) - 1 and t == 1:
                                    ins.then_inc(sc_read, 1)
                                else:
                                    ins.then_inc(v_step, 1)
                                    steps += 1
                        dve.wait_ge(v_step, steps)
                        if br != "A":
                            dve.wait_ge(sc_read, u + 1)
                            dve.tensor_scalar(nm[z][:, 0:n_mx], mx[z][:, 0:n_mx], -1.0, None, ALU.mult).then_inc(mx_ready, 1)
                            dve.wait_ge(ex_done, u + 1)
                            if br == "B":
                                dve.reciprocal(rc[z][:, 0:2], sm[z][:, 0:2]).then_inc(p_ready, 1)
                            else:
                                dve.reciprocal(rc[z][:, 0:4], sm[z][:, 0:4]).then_inc(v_step, 1)
                                steps += 1
                                dve.wait_ge(v_step, steps)
                                dve.tensor_scalar(nl[z], rc[z][:, 2:4], neg_lam, None, ALU.mult).then_inc(v_step, 1)
                                steps += 1
                                dve.wait_ge(v_step, steps)
                                for t in range(TT):
                                    sa = slice(0, 128) if t == 0 else slice(128, 384)
                                    dve.tensor_scalar(S2[q][:, sa], S2[q][:, sa], nl[z][:, t:t + 1], None, ALU.mult).then_inc(v_step, 1)
                                    steps += 1
                                for t in range(TT):
                                    sa = slice(0, 128) if t == 0 else slice(128, 384)
                                    dve.wait_ge(v_step, steps)
                                    dve.scalar_tensor_tensor(out=S2[q][:, sa], in0=S1[q][:, sa], scalar=rc[z][:, t:t + 1],
                                                             in1=S2[q][:, sa], op0=ALU.mult, op1=ALU.add).then_inc(p_ready if t else v_step, 1)
                                    if not t:
                                        steps += 1
                        else:
                            dve.tensor_scalar(nm[z][:, 0:2], mx[z][:, 0:2], 0.0, -1.0, ALU.max, ALU.mult).then_inc(v_step, 1)
                            steps += 1
                            dve.wait_ge(v_step, steps)
                            dve.tensor_tensor(mm[z], nm[z][:, 0:2], cum[:, h:8:4], ALU.subtract).then_inc(mx_ready, 1)
                            dve.wait_ge(ex_done, u + 1)
                            for t in range(TT):
                                sa = slice(0, 128) if t == 0 else slice(128, 384)
                                dve.tensor_tensor_reduce(S2[q][:, sa], score_ps[0][:, sa], S1[q][:, sa], A_DH ** -0.5, 0.0,
                                                         ALU.mult, ALU.add, sm[z][:, t:t + 1]).then_inc(sc_read if t else v_step, 1)
                                if not t:
                                    steps += 1
                            dve.wait_ge(v_step, steps)
                            dve.wait_ge(sc_read, u + 1)
                            dve.wait_ge(em_ready, h + 1)
                            dve.scalar_tensor_tensor(out=rc[z][:, 0:2], in0=sm[z][:, 0:2], scalar=-1.0, in1=sm[z][:, 0:2],
                                                     op0=ALU.mult, op1=ALU.max).then_inc(v_step, 1)
                            steps += 1
                            dve.wait_ge(v_step, steps)
                            dve.tensor_tensor(rc[z][:, 0:2], rc[z][:, 0:2], em[z], ALU.max).then_inc(v_step, 1)
                            steps += 1
                            dve.wait_ge(v_step, steps)
                            dve.reciprocal(rc[z][:, 0:2], rc[z][:, 0:2]).then_inc(p_ready, 1)
                    u = unit_in_slot(i, 2)
                    if u is not None:
                        br, h = UNITS[u]
                        q, z = u % 2, u % 3
                        dve.wait_ge(pv_done, u + 1)
                        nx = turned.index(u) if u in turned else turned.index(u + 1)
                        if nx >= 2:
                            dve.wait_ge(xt_done, nx - 1)
                        H = hx[nx % 2]
                        if br == "B":
                            for t in range(TT):
                                ins = dve.tensor_scalar(H[:, t, 64 * (h % 2):64 * (h % 2) + 64], value_ps[:, 64 * t:64 * t + 64],
                                                        rc[z][:, t:t + 1], None, ALU.mult)
                                if t:
                                    ins.then_inc(hx_ready, 1)
                                else:
                                    ins.then_inc(v_step, 1)
                                    steps += 1
                                    dve.wait_ge(v_step, steps)
                        else:
                            dve.wait_ge(hn_ready, normed.index(u) + 1)
                            if br == "A":
                                dve.wait_ge(outgate_ready, 2)
                                dve.tensor_tensor(rr[z], rsu[z], rc[z][:, 0:2], ALU.mult).then_inc(v_step, 1)
                                steps += 1
                                dve.wait_ge(v_step, steps)
                            for t in range(TT):
                                sc_ap = (rr if br == "A" else rsu)[z][:, t:t + 1]
                                g_ap = out_gate[:, t, P * h:P * h + P] if br == "A" else gc08
                                ins = dve.scalar_tensor_tensor(out=H[:, t, :], in0=value_ps[:, P * t:P * t + P], scalar=sc_ap, in1=g_ap,
                                                               op0=ALU.mult, op1=ALU.mult)
                                if t:
                                    ins.then_inc(hx_ready, 1)
                                else:
                                    ins.then_inc(v_step, 1)
                                    steps += 1
                                    dve.wait_ge(v_step, steps)

                dve.wait_ge(srec_ready, len(sig_pieces))
                for j in range(12):
                    i = NP + j
                    dve.wait_ge(piece_done, i + 1)
                    g = 2 * j
                    dst = yT[:, 2 * j:2 * j + 2, :].rearrange("p n t -> p (n t)") if j < 4 else sq[j % 2]
                    if j >= 6:
                        dve.wait_ge(y_ready, j - 5)
                    dve.tensor_tensor(dst, piece_ps[i % 2][:, :], gate_s[:, g:g + 2, :].rearrange("p n t -> p (n t)"),
                                      ALU.mult).then_inc(zg_ready, 1)
                for j in range(4):
                    i = NP + 12 + j
                    t, half = j // 2, j % 2
                    dve.wait_ge(piece_done, i + 1)
                    o = xs[:, t, 512 * half:512 * half + 512]
                    dve.tensor_tensor(o, piece_ps[i % 2][:, :], o, ALU.add).then_inc(x1_ready, 1)
                dve.wait_ge(router_in, 16 * 5)
                dve.tensor_tensor(w_rt[:, :, :], w_rt[:, :, :], g2[:, :].unsqueeze(2).to_broadcast([P, KD, GROUPS + EXPERTS]),
                                  ALU.mult).then_inc(v_step, 1)
                steps += 1
                for t in range(TT):
                    dve.wait_ge(xh_step, t + 1)
                    dve.tensor_scalar(xhat[:, t, :], xs[:, t, :], rstd2[:, t:t + 1], None, ALU.mult).then_inc(xh_ready, 1)
                dve.memset(xg[:, :, PAIRS:COLS], 0.0).then_inc(pads_ready, 1)

                for t in range(TT):
                    R = rt_of(t)

                    def link(ins):
                        nonlocal steps
                        ins.then_inc(v_step, 1)
                        steps += 1
                        dve.wait_ge(v_step, steps)

                    dve.wait_ge(lg_done, t + 1)
                    link(dve.tensor_tensor(R["lg"], logit_ps[t][:, 0:GROUPS + EXPERTS], bc_small[:, 8:44], ALU.add))
                    link(dve.tensor_reduce(R["gm"], R["lg"][:, 0:GROUPS], AX_X, ALU.max))
                    dve.tensor_scalar(R["ngm"], R["gm"], -1.0, None, ALU.mult).then_inc(hot_ready, 1)
                    link(dve.scalar_tensor_tensor(out=R["g4"], in0=R["lg"][:, 0:GROUPS], scalar=R["gm"], in1=c("prig"),
                                                  op0=ALU.is_equal, op1=ALU.mult))
                    link(dve.tensor_reduce(R["gi"], R["g4"], AX_X, ALU.max))
                    link(dve.tensor_scalar(R["g4"], c("prig"), R["gi"], 1.0, ALU.is_equal, ALU.subtract))
                    link(dve.tensor_scalar(R["g4"], R["g4"], -NEG, None, ALU.mult))
                    link(dve.tensor_tensor(R["el"].rearrange("p (g e) -> p g e", g=GROUPS),
                                           R["lg"][:, GROUPS:].rearrange("p (g e) -> p g e", g=GROUPS),
                                           R["g4"].unsqueeze(2).to_broadcast([P, GROUPS, PER_GROUP]), ALU.add))
                    for j, hot in enumerate((R["o1"], R["o2"])):
                        m, idx = R["m"][:, j:j + 1], R["i"][:, j:j + 1]
                        link(dve.tensor_reduce(m, R["el"], AX_X, ALU.max))
                        link(dve.scalar_tensor_tensor(out=hot, in0=R["el"], scalar=m, in1=c("pri"), op0=ALU.is_equal, op1=ALU.mult))
                        link(dve.tensor_reduce(idx, hot, AX_X, ALU.max))
                        link(dve.tensor_scalar(hot, c("pri"), idx, None, ALU.is_equal))
                        if j == 0:
                            link(dve.scalar_tensor_tensor(out=R["el"], in0=hot, scalar=3 * NEG, in1=R["el"], op0=ALU.mult, op1=ALU.add))
                    dve.tensor_tensor(R["d"], R["m"][:, 1:2], R["m"][:, 0:1], ALU.subtract).then_inc(hot_ready, 1)
                    link(dve.tensor_tensor(R["hot"], R["o1"], R["o2"], ALU.add))
                    link(dve.tensor_scalar(R["bef"], c("pri"), R["i"][:, 0:1], None, ALU.is_lt))
                    dve.scalar_tensor_tensor(out=R["bef"], in0=c("pri"), scalar=R["i"][:, 1:2], in1=R["bef"], op0=ALU.is_lt,
                                             op1=ALU.add).then_inc(hot_ready, 1)
                for t in range(TT):
                    R = rt_of(t)
                    dve.wait_ge(rt_exp, 2 * t + 2)
                    link(dve.tensor_scalar(R["w"][:, 0:1], R["e2"], 1.0, R["gs"], ALU.add, ALU.mult))
                    link(dve.reciprocal(R["w"][:, 0:1], R["w"][:, 0:1]))
                    link(dve.tensor_tensor(R["w"][:, 1:2], R["w"][:, 0:1], R["e2"], ALU.mult))
                for t in range(TT):
                    R = rt_of(t)
                    dve.wait_ge(pos_done, 1)
                    for j, hot in enumerate((R["o1"], R["o2"])):
                        link(dve.tensor_tensor_reduce(R["hot"], hot, outT_ps[:, EXPERTS * t:EXPERTS * t + EXPERTS], 1.0, 0.0,
                                                      ALU.mult, ALU.add, R["pos"][:, j:j + 1]))
                starts, counts = outT_ps[0:1, 64:96], outT_ps[0:1, 96:128]
                for j in range(4):
                    link(dve.tensor_scalar(offs_f[:, EXPERTS * j:EXPERTS * j + EXPERTS], starts, float(WIN * j), float(PAIRS),
                                           ALU.add, ALU.min))
                link(dve.tensor_reduce(offs_f[:, 4 * EXPERTS:4 * EXPERTS + 1], counts, AX_X, ALU.max))
                dve.tensor_copy(offs_i[:, :], offs_f[:, :]).then_inc(offs_ready, 1)
                for t in range(TT):
                    R = rt_of(t)
                    link(dve.tensor_scalar(sel_g[t], c("iota"), R["pos"][:, 0:1], None, ALU.is_equal))
                    dve.scalar_tensor_tensor(out=sel_g[t], in0=c("iota"), scalar=R["pos"][:, 1:2], in1=sel_g[t],
                                             op0=ALU.is_equal, op1=ALU.add).then_inc(sel_ready, 1)
                for t in range(TT):
                    R = rt_of(t)
                    link(dve.tensor_scalar(sel_w[t], c("iota"), R["pos"][:, 0:1], R["w"][:, 0:1], ALU.is_equal, ALU.mult))
                    link(dve.tensor_scalar(R["tmp"], c("iota"), R["pos"][:, 1:2], R["w"][:, 1:2], ALU.is_equal, ALU.mult))
                    dve.tensor_tensor(sel_w[t], sel_w[t], R["tmp"], ALU.add).then_inc(sel_ready, 1)
                for k in range(1, KD, 2):
                    dve.wait_ge(ga_done, k + 1)
                    dve.tensor_scalar(xg[:, k, 0:PAIRS], gather_ps(k)[:, :], g2[:, k:k + 1], None, ALU.mult).then_inc(xg_ready_v, 1)
                for e in range(SLOTS):
                    window_hidden(dve, FAST, e, e % 2)
                with dve.Fori(1, EXPERTS // SLOTS) as i:
                    for r in range(SLOTS):
                        window_hidden(dve, FAST, i * SLOTS + r, r % 2)
                with general_path(dve):
                    dve.wait_ge(FAST["down_done"], EXPERTS)

                    def expert(e):
                        for j in range(WINDOWS):
                            window_hidden(dve, GENERAL, e * WINDOWS + j, j % 2)

                    every_expert(dve, expert)
                for g in range(4):
                    t, half = g // 2, g % 2
                    dve.wait_ge(out_done, g + 1)
                    o = xs[:, t, 512 * half:512 * half + 512]
                    dve.tensor_tensor(o, final_ps[g][:, :], o, ALU.add).then_inc(out_ready, 1)

            @block.tensor
            def _(pe):
                pe.wait_ge(const_in, 16)
                pe.wait_ge(params_in, 16 * 13)
                pe.transpose(sum_ps[:, 0:52], small[0:52, :], c("ident", 52)[:, 0:52]).then_inc(par_ps, 1)
                for j in range(3):
                    a = CONST["t5hot"][0] + P * j
                    ins = pe.matmul(outT_ps[:, 4 * j:4 * j + 4], cst[0:T5_BUCKETS, a:a + P], t5[:, :], start=True, stop=True)
                ins.then_inc(t5_ps, 1)
                pe.wait_ge(xn_done, TT)
                for k in range(KD):
                    for t in range(TT):
                        ins = pe.transpose(xT_ps(k)[:, P * t:P * t + P], work[:, 2048 + 1024 * t + P * k:2048 + 1024 * t + P * k + P], ident)
                    ins.then_inc(xT_done, 1)

                def unit_steps(i):
                    u = unit_in_slot(i, 0)
                    if u is not None:
                        br, h = UNITS[u]
                        if u >= 1:
                            pe.wait_ge(sc_read, u)
                        if br in "BC":
                            pe.wait_ge(qk_ready, 4 if br == "C" else 8)
                            pairs = ([(0, score_ps[0], "cq", "ck", h), (64, score_ps[1], "cq", "ck", h)] if br == "C"
                                     else [(64 * (h % 2), score_ps[u % 2], "bq", "bk", h // 2)])
                            dk = 64
                        else:
                            pe.wait_ge(conv_ready, 4)
                            pe.wait_ge(ig_v_step, 9)
                            pairs = [(0, score_ps[0], "aq", "ak", h)]
                            dk = P
                        for r0, ps, qn, kn, ch in pairs:
                            q, k = qk[r0:r0 + dk, QK[qn] + ch, :], qk[r0:r0 + dk, QK[kn] + ch, :]
                            pe.matmul(ps[:, 0:128], q[:, 0:128], k[:, 0:128], start=True, stop=True)
                            ins = pe.matmul(ps[:, 128:384], q[:, 128:256], k[:, 0:256], start=True, stop=True)
                        if br == "A":
                            for t in range(TT):
                                ins = pe.matmul(score_ps[1][:, P * t:P * t + P], src[:, 4 * t + h:4 * t + h + 1].to_broadcast([P, P]),
                                                ident, start=True, stop=True)
                        ins.then_inc(sc_done, 1)
                    u = unit_in_slot(i, 1)
                    if u is not None:
                        pe.wait_ge(p_ready, u + 1)
                        if u >= 1:
                            pe.wait_ge(pt_ready, u)
                        S = (S1 if UNITS[u][0] == "B" else S2)[u % 2]
                        for j in range(3):
                            ins = pe.transpose(turn_ps[:, P * j:P * j + P], S[:, P * j:P * j + P], ident)
                        ins.then_inc(tp_done, 1)
                    u = unit_in_slot(i, 2)
                    if u is not None:
                        br, h = UNITS[u]
                        pe.wait_ge(pt_ready, u + 1)
                        if u >= 1:
                            pe.wait_ge(hx_ready, u)
                        name, dv = dict(A=("av", 128), B=("bv", 64), C=("cv", 128))[br]
                        if h == 0:
                            wait_values(pe, name)
                        v = vals[:, VAL[name], :, dv * h:dv * h + dv]
                        pe.matmul(value_ps[:, 0:dv], PT[0][:, 0:128], v[:, 0, :], start=True, stop=True)
                        pe.matmul(value_ps[:, dv:2 * dv], PT[0][:, 128:256], v[:, 0, :], start=True, stop=False)
                        pe.matmul(value_ps[:, dv:2 * dv], PT[0][:, 256:384], v[:, 1, :], start=False, stop=True).then_inc(pv_done, 1)
                    u = unit_in_slot(i, 3)
                    if u is not None and u in turned:
                        nx = turned.index(u)
                        pe.wait_ge(hx_ready, u + 1)
                        if nx >= 1:
                            pe.wait_ge(branch_ready, nx)
                        else:
                            pe.wait_ge(t5v_ready, 1)
                        for t in range(TT):
                            ins = pe.transpose(outT_ps[:, P * t:P * t + P], hx[nx % 2][:, t, :], ident)
                        ins.then_inc(xt_done, 1)

                for i in range(NP + DRAIN + 1):
                    if i == IG + 3:
                        pe.wait_ge(ig_v_step, 8)
                    unit_steps(i)
                    if i < NP:
                        kind, name, n = PIECES[i]
                        ps = piece_ps[i % 2]
                        if i >= 2:
                            pe.wait_ge(bank_free[i % 2], freed(i - 2))
                        if i == 0:
                            pe.wait_ge(hT_ready, KD)
                        b = piece_block[i]
                        if b is not None:
                            pe.wait_ge(block_in[b % 2], 16 * (b // 2 + 1))
                            w = block_sb(b, KD)
                        if kind == "igate":
                            for t in range(TT):
                                for k in range(KD):
                                    ins = pe.matmul(ps[:, 8 * t:8 * t + 8], hT[:, k, P * t:P * t + P], w_if[:, k, :],
                                                    start=(k == 0), stop=(k == KD - 1))
                        elif kind == "value":
                            for k in range(KD):
                                ins = pe.matmul(ps[:, :], hT[:, k, P * n:P * n + P], w[:, k, :], start=(k == 0), stop=(k == KD - 1))
                        else:
                            for half in range(2):
                                ch = 2 * (n % 2) + half
                                for k in range(KD):
                                    ins = pe.matmul(ps[:, SEQ * half:SEQ * half + SEQ], w[:, k, P * ch:P * ch + P], hT[:, k, :],
                                                    start=(k == 0), stop=(k == KD - 1))
                        ins.then_inc(piece_done, 1)
                    if i >= 1 and i - 1 in norm_pieces:
                        j = norm_pieces.index(i - 1)
                        pe.wait_ge(sq_ready, j + 1)
                        if j >= 1:
                            pe.wait_ge(rs_ready, j)
                        else:
                            pe.wait_ge(par_ready, 1)
                        pe.matmul(sum_ps[:, :], c("blocks"), sq[j % 2], start=True, stop=True).then_inc(ss_done, 1)

                    if i == IG + 2:
                        pe.wait_ge(ig_v_step, 7)
                        pe.wait_ge(branch_ready, sum(u <= i - U0 - 3 for u in turned))
                        pe.matmul(outT_ps[:, 0:4], c("tri"), lf[:, 0:4], start=True, stop=True)
                        pe.matmul(outT_ps[:, 4:8], ones, lf[:, 0:4], start=True, stop=False)
                        pe.matmul(outT_ps[:, 4:8], c("tri"), lf[:, 4:8], start=False, stop=True).then_inc(ig_p_step, 1)

                for j in range(12):
                    i, b = NP + j, n_in + j // 4
                    pe.wait_ge(bank_free[i % 2], freed(i - 2)) if j < 2 else pe.wait_ge(zg_ready, j - 1)
                    pe.wait_ge(block_in[b % 2], 16 * (b // 2 + 1))
                    if j % 4 == 0:
                        pe.wait_ge(branch_ready, {0: 4, 4: 8, 8: 12}[j])
                    w = block_sb(b, 4)
                    for half in range(2):
                        ch = 2 * (j % 4) + half
                        for k in range(4):
                            ins = pe.matmul(piece_ps[i % 2][:, SEQ * half:SEQ * half + SEQ], w[:, k, P * ch:P * ch + P],
                                            branchT[:, BRANCH_ORDER[j // 4], k, :], start=(k == 0), stop=(k == 3))
                    ins.then_inc(piece_done, 1)
                pe.wait_ge(y_ready, 8)
                for j in range(4):
                    i, t, half = NP + 12 + j, j // 2, j % 2
                    b = n_in + 3 + half
                    pe.wait_ge(zg_ready, 11 + j) if j < 2 else pe.wait_ge(x1_ready, j - 1)
                    pe.wait_ge(block_in[b % 2], 16 * (b // 2 + 1))
                    w = block_sb(b, KD)
                    for k in range(KD):
                        ins = pe.matmul(piece_ps[i % 2][:, :], yT[:, k, P * t:P * t + P], w[:, k, :], start=(k == 0), stop=(k == KD - 1))
                    ins.then_inc(piece_done, 1)
                for t in range(TT):
                    pe.wait_ge(xh_ready, t + 1)
                    for half in range(2):
                        ps = [score_ps[0], score_ps[1], turn_ps, value_ps][2 * t + half]
                        for k in range(4 * half, 4 * half + 4):
                            ins = pe.transpose(ps[:, P * (k % 4):P * (k % 4) + P], xhat[:, t, k:D:KD], ident)
                        ins.then_inc(th_done, 1)
                pe.wait_ge(x1_ready, 4)
                pe.wait_ge(branch_ready, 12)
                for t in range(TT):
                    pe.wait_ge(tT_ready, 2 * t + 2)
                    for k in range(KD):
                        ins = pe.matmul(logit_ps[t][:, 0:GROUPS + EXPERTS], tT[:, k, P * t:P * t + P], w_rt[:, k, :],
                                        start=(k == 0), stop=(k == KD - 1))
                    ins.then_inc(lg_done, 1)
                R0, R1 = rt_of(0), rt_of(1)
                pe.wait_ge(hot_ready, 6)
                pe.wait_ge(branch_ready, 12)
                o = outT_ps[:, 0:EXPERTS]
                pe.matmul(o, ones, R0["bef"], start=True, stop=False)
                pe.matmul(o, ones, R1["bef"], start=False, stop=False)
                pe.matmul(o, c("strict"), R0["hot"], start=False, stop=True)
                o = outT_ps[:, EXPERTS:2 * EXPERTS]
                pe.matmul(o, ones, R0["bef"], start=True, stop=False)
                pe.matmul(o, ones, R1["bef"], start=False, stop=False)
                pe.matmul(o, ones, R0["hot"], start=False, stop=False)
                pe.matmul(o, c("strict"), R1["hot"], start=False, stop=True)
                for j, key in enumerate(("bef", "hot")):
                    o = outT_ps[:, 64 + 32 * j:96 + 32 * j]
                    pe.matmul(o, ones, R0[key], start=True, stop=False)
                    ins = pe.matmul(o, ones, R1[key], start=False, stop=True)
                ins.then_inc(pos_done, 1)
                for k in range(KD):
                    if k == 0:
                        pe.wait_ge(sel_ready, TT)
                    if k >= 3:
                        pe.wait_ge(xg_ready_v if (k - 3) % 2 else xg_ready_a, (k - 3) // 2 + 1)
                    for t in range(TT):
                        ins = pe.matmul(gather_ps(k)[:, :], xhat[:, t, k:D:KD], sel_g[t], start=(t == 0), stop=(t == TT - 1))
                    ins.then_inc(ga_done, 1)
                pe.wait_ge(offs_ready, 1)
                for t in range(TT):
                    pe.wait_ge(sel_ready, TT + t + 1)
                    if t:
                        pe.wait_ge(selT_ready, t)
                    for s in range(4):
                        ins = pe.transpose(outT_ps[:, P * s:P * s + P], sel_w[t][:, P * s:P * s + P], ident)
                    ins.then_inc(selT_done, 1)
                pe.wait_ge(xg_ready_a, KD // 2)
                pe.wait_ge(xg_ready_v, KD // 2)
                pe.wait_ge(pads_ready, 1)
                for e in range(SLOTS):
                    pe.wait_ge(exp_in[e], 48)
                    window_up(pe, FAST, e, e % 2, e, 0, e)
                    if e:
                        window_down(pe, FAST, e - 1, (e - 1) % 2, e - 1)
                with pe.Fori(1, EXPERTS // SLOTS) as i:
                    for r in range(SLOTS):
                        e = i * SLOTS + r
                        pe.wait_ge(exp_in[r], (i + 1) * 48)
                        window_up(pe, FAST, e, r % 2, e, 0, r)
                        window_down(pe, FAST, e - 1, (r - 1) % 2, (r - 1) % SLOTS)
                window_down(pe, FAST, EXPERTS - 1, 1, SLOTS - 1)
                with general_path(pe):
                    pe.wait_ge(FAST["hid_ready"], EXPERTS)
                    pe.wait_ge(FAST["down_read"], EXPERTS)

                    def expert(e):
                        pe.wait_ge(general_in, (e + 1) * 48)
                        for j in range(WINDOWS):
                            window_up(pe, GENERAL, e * WINDOWS + j, j % 2, e, j, 0)
                            window_down(pe, GENERAL, e * WINDOWS + j, j % 2, 0)

                    every_expert(pe, expert)
                pe.wait_ge(yg_ready, 1)
                for g in range(8):
                    s, half = g // 2, g % 2
                    if g >= 2:
                        pe.wait_ge(yrow_ready, g - 1)
                    for k in range(4):
                        ins = pe.transpose(piece_ps[g % 2][:, P * k:P * k + P], yg[:, 4 * half + k, P * s:P * s + P], ident)
                    ins.then_inc(yturn_done, 1)
                pe.wait_ge(yrow_ready, 8)
                for g in range(4):
                    t, half = g // 2, g % 2
                    for s in range(4):
                        ins = pe.matmul(final_ps[g][:, :], selT[:, s, P * t:P * t + P], yrows[:, s, 512 * half:512 * half + 512],
                                        start=(s == 0), stop=(s == 3))
                    ins.then_inc(out_done, 1)



_INS = ['x', 'norm1_g', 'w_in', 'a_conv_w', 'a_conv_b', 'a_gate_bias', 'a_out_norm_g', 'b_qk_norm_g', 'b_rel_bias',
        'c_qk_norm_g', 'c_lambda', 'c_sub_norm_g', 't5_bias', 'w_branch', 'w_out', 'norm2_g', 'w_group', 'b_group',
        'w_router', 'b_router', 'w_e_gate', 'w_e_up', 'w_e_down']


def kernel(**inputs):
    import numpy as _np
    import concourse.bacc as _bacc
    from concourse import mybir as _mybir
    from concourse.bass_utils import run_bass_kernel_spmd as _run

    nc = _bacc.Bacc("TRN2", target_bir_lowering=False, num_devices=1)
    arrays, args = {}, []
    for name in _INS:
        a = _np.ascontiguousarray(inputs[name])
        arrays[f"in_{name}_dram"] = a
        args.append(nc.dram_tensor(f"in_{name}_dram", a.shape, _mybir.dt.from_np(a.dtype), kind="ExternalInput").ap())
    arrays["constants_dram"] = constants()
    consts = nc.dram_tensor("constants_dram", (P, CONST_WIDTH), F32, kind="ExternalInput").ap()
    scratch = nc.dram_tensor("t5_by_position", (3 * P * C_HEADS,), F32, kind="Internal").ap()
    out = nc.dram_tensor("out_0_dram", (1, SEQ, D), F32, kind="ExternalOutput").ap()
    build_hybrid_layer(nc, *args, consts, scratch, out)
    r = _run(nc, [arrays], core_ids=[0])
    return r.results[0]["out_0_dram"]
```

```python
from contextlib import ExitStack

import concourse.bass as bass
from concourse import mybir

F32 = mybir.dt.float32
I32 = mybir.dt.int32
ALU = mybir.AluOpType
ACT = mybir.ActivationFunctionType
AX_X = mybir.AxisListType.X
LN_EXP_SET, SIGMOID_SET = "natural_log_exp_and_others", "sigmoid_and_others"

P = 128
SEQ, D = 256, 1024
TT = SEQ // P
KD = D // P
CHUNK = 64
EPS = 1e-6
NEG = -1e30
LOWEST = -3e38
A_HEADS, A_DH = 4, 128
B_HEADS, B_DH = 8, 64
C_HEADS, C_DQK, C_DV = 4, 64, 128
B_MAX_REL = 256
T5_BUCKETS, T5_MAX_DIST = 32, 1024
GATE_CAP = 15.0
LAM_INIT = 0.2
WIDTH = 512
GROUPS, PER_GROUP, EXPERTS, D_EXPERT = 4, 8, 32, 256
FC = D_EXPERT // P
PAIRS = 2 * SEQ
WIN = 64
LIMIT = WIN
WINDOWS = -(-SEQ // WIN)
COLS = PAIRS + WIN
SLOTS = 4
EXPERT_FLOATS = 3 * KD * D_EXPERT

COL = dict(aq=0, ak=512, av=1024, ao=1536, aif=2048, bq=2056, bk=2568, bv=3080,
           cq=3592, ck=4104, cv=4616, g=5128)

CONST = {}
_at = 0
for _name, _width in (("ident", 128), ("ones", 128), ("tri", 128), ("strict", 128), ("blocks", 128), ("eps", 1),
                      ("mask_chunk", 256), ("mask_tri", 256), ("iota", PAIRS), ("pri", EXPERTS),
                      ("prig", GROUPS), ("t5hot", 384)):
    CONST[_name] = (_at, _at + _width)
    _at += _width
CONST_WIDTH = _at
KEPT = CONST["t5hot"][0]


def constants():
    import math

    import numpy as np

    c = np.zeros((P, CONST_WIDTH), np.float32)

    def put(name, value):
        a, b = CONST[name]
        c[:, a:b] = value

    i, j = np.arange(P)[:, None], np.arange(P)[None, :]
    put("ident", i == j)
    put("ones", 1.0)
    put("tri", i <= j)
    put("strict", i < j)
    put("blocks", i // 64 == j // 64)
    zero = np.zeros((P, P))
    put("mask_chunk", np.concatenate([zero, np.where(j // CHUNK <= i // CHUNK, 0.0, NEG)], 1))
    put("mask_tri", np.concatenate([zero, np.where(j <= i, 0.0, NEG)], 1))
    put("iota", np.arange(PAIRS)[None, :])
    put("pri", EXPERTS - np.arange(EXPERTS)[None, :])
    put("prig", GROUPS - np.arange(GROUPS)[None, :])
    put("eps", EPS)
    rel = 127 - np.arange(384)
    nb = T5_BUCKETS // 2
    exact = nb // 2
    n = np.abs(rel)
    f = np.float32
    large = exact + (np.log(np.maximum(n, exact).astype(f) / f(exact)) / f(math.log(T5_MAX_DIST / exact))
                     * f(nb - exact)).astype(np.int32)
    bucket = (rel > 0) * nb + np.where(n < exact, n, np.minimum(large, nb - 1))
    put("t5hot", 0.0)
    a, b = CONST["t5hot"]
    c[:T5_BUCKETS, a:b] = bucket[None, :] == np.arange(T5_BUCKETS)[:, None]
    return c


PIECES = []
for _kind, _name in (("conv", "aq"), ("conv", "ak"), ("value", "ao"), ("value", "av"), ("norm", "cq"),
                     ("norm", "ck"), ("value", "cv"), ("norm", "bq"), ("norm", "bk"), ("value", "bv")):
    for _half in range(2):
        PIECES.append((_kind, _name, _half))
    if _name == "ao":
        PIECES.append(("igate", "aif", 0))
for _g in range(12):
    PIECES.append(("gate", "g", _g))
NP = len(PIECES)

UNITS = [("A", h) for h in range(A_HEADS)] + [("C", h) for h in range(C_HEADS)] + [("B", h) for h in range(B_HEADS)]
NU = len(UNITS)
U0 = 12
SIG_SLOT = U0 + NU
DRAIN = 3


def build_hybrid_layer(nc, x, norm1_g, w_in, a_conv_w, a_conv_b, a_gate_bias, a_out_norm_g,
                       b_qk_norm_g, b_rel_bias, c_qk_norm_g, c_lambda, c_sub_norm_g, t5_bias,
                       w_branch, w_out, norm2_g, w_group, b_group, w_router, b_router,
                       w_e_gate, w_e_up, w_e_down, consts, scratch, out):
    ctx = ExitStack()
    with ctx:
        def sb(name, shape, dt=F32):
            return ctx.enter_context(nc.sbuf_tensor(name, shape, dt))

        def sem(name):
            return ctx.enter_context(nc.semaphore(name))

        xs = sb("xs", [P, TT, D])
        hT = sb("hT", [P, KD, SEQ])
        cst = sb("cst", [P, KEPT])
        early = sb("early", [P, 2 * EXPERT_FLOATS])
        gates = sb("gates", [P, EXPERT_FLOATS])
        expert0 = sb("expert0", [P, EXPERT_FLOATS])
        stream = sb("stream", [P, 2 * KD * COLS])
        branchT = sb("branchT", [P, 3, 4, SEQ])
        yT = sb("yT", [P, KD, SEQ])
        small = sb("small", [64, P])
        par = sb("par", [P, 64])
        bc_norm = sb("bc_norm", [P, WIDTH + C_DV])
        bc_small = sb("bc_small", [P, 8 + 4 + EXPERTS])
        w_if = sb("w_if", [P, KD, 8])
        w_rt = sb("w_rt", [P, KD, GROUPS + EXPERTS])
        g2 = sb("g2", [P, KD])
        t5 = sb("t5", [T5_BUCKETS, C_HEADS])
        t5v = sb("t5v", [P, 3, C_HEADS])
        work = sb("work", [P, 5632])
        st = sb("st", [P, 256])
        offs_i = sb("offs_i", [1, EXPERTS * WINDOWS + 1], I32)
        offs_f = sb("offs_f", [1, EXPERTS * WINDOWS + 1])

        def c(name, rows=P):
            a, b = CONST[name]
            return cst[0:rows, a:b]

        ident, ones = c("ident"), c("ones")
        eps = c("eps")

        t5hot = early[:, 0:384]
        lam_in = early[:, 384:384 + 4 * C_DQK].rearrange("p (a b) -> p a b", b=C_DQK)
        qk = early[:, 0:24 * SEQ].rearrange("p (n t) -> p n t", t=SEQ)
        QK = dict(cq=0, ck=4, bq=8, bk=12, aq=16, ak=20)
        vals = early[:, 24 * SEQ:24 * SEQ + 3 * TT * WIDTH].rearrange("p (n t c) -> p n t c", n=3, t=TT)
        VAL = dict(cv=0, bv=1, av=2)
        bias = early[:, 9216:9216 + 12 * SEQ].rearrange("p (h k) -> p h k", k=SEQ)
        slots_w = [stream[:, n * 4096:(n + 1) * 4096] for n in range(2)]
        out_gate = stream[:, 8192:8192 + TT * WIDTH].rearrange("p (t c) -> p t c", t=TT)
        rel_raw = gates[:, 0:2048].rearrange("p (k h) -> p k h", h=B_HEADS)
        t5_raw = gates[:, 2048:3072].rearrange("p (k h) -> p k h", h=C_HEADS)
        xg = stream[:, 0:KD * COLS].rearrange("p (k n) -> p k n", n=COLS)
        yg = stream[:, KD * COLS:2 * KD * COLS].rearrange("p (k n) -> p k n", n=COLS)

        sq = [work[:, 512 * n:512 * n + 512] for n in range(2)]
        ug = [work[:, 1024 + 512 * n:1536 + 512 * n] for n in range(2)]
        ug_pair = work[:, 1024:2048]
        rs_w = [work[:, 2048 + 512 * n:2560 + 512 * n] for n in range(2)]
        S1 = [work[:, 3072 + 384 * n:3456 + 384 * n] for n in range(2)]
        S2 = [work[:, 3840 + 384 * n:4224 + 384 * n] for n in range(2)]
        PT = [work[:, 4608 + 384 * n:4992 + 384 * n] for n in range(1)]
        hx = [work[:, 4992 + 256 * n:5248 + 256 * n].rearrange("p (t c) -> p t c", t=TT) for n in range(2)]
        xhat = hT[:, :, :].rearrange("p k t -> p (k t)").rearrange("p (t d) -> p t d", t=TT)
        tT = yT[:, :, :]
        sel_g = [work[:, 512 * n:512 * n + 512] for n in range(TT)]
        sel_w = [work[:, 1024 + 512 * n:1536 + 512 * n] for n in range(TT)]
        selT = work[:, 2048:2048 + 4 * SEQ].rearrange("p (s t) -> p s t", t=SEQ)
        hid, eg, hidT = ([work[:, at + P * n:at + P * n + P] for n in range(2)] for at in (3072, 3328, 3584))
        rt = work[:, 3840:5632]
        xw = [work[:, 512 * n:512 * n + 512].rearrange("p (k n) -> p k n", n=WIN) for n in range(2)]
        ysb = [work[:, 1024 + 512 * n:1536 + 512 * n] for n in range(2)]
        yrows = expert0[:, 0:4 * D].rearrange("p (s d) -> p s d", d=D)
        slot_mem = [expert0[:, :], early[:, 0:EXPERT_FLOATS], early[:, EXPERT_FLOATS:2 * EXPERT_FLOATS],
                    gates[:, :]]
        w_gate_up = [m[:, 0:4096].rearrange("p (m k f) -> p m k f", m=2, k=KD) for m in slot_mem]
        w_down = [m[:, 4096:6144].rearrange("p (f d) -> p f d", d=D) for m in slot_mem]

        def stat(at, n):
            return st[:, at:at + n]

        ss1, rstd1 = stat(0, 2), stat(2, 2)
        ss2, rstd2 = stat(4, 2), stat(6, 2)
        lam_s, lam_e, neg_lam = stat(8, 2), stat(10, 2), stat(12, 1)
        ig_z, ig_e, lf = stat(16, 16), stat(32, 16), stat(48, 8)
        ig_v, cum, src = stat(56, 8), stat(64, 8), stat(72, 8)
        mx = [stat(80 + 32 * n, 4) for n in range(3)]
        nm = [stat(84 + 32 * n, 4) for n in range(3)]
        sm = [stat(88 + 32 * n, 4) for n in range(3)]
        rc = [stat(92 + 32 * n, 4) for n in range(3)]
        nl = [stat(96 + 32 * n, 2) for n in range(3)]
        em = [stat(98 + 32 * n, 2) for n in range(3)]
        ssu = [stat(100 + 32 * n, 2) for n in range(3)]
        rsu = [stat(102 + 32 * n, 2) for n in range(3)]
        rr = [stat(104 + 32 * n, 2) for n in range(3)]
        mm = [stat(106 + 32 * n, 2) for n in range(3)]
        gc08 = bc_norm[:, WIDTH:WIDTH + C_DV]
        ga = bc_norm[:, 0:WIDTH]

        CONVW, CONVB, NORM1, QKG = 0, 32, 40, 48

        def bank(name):
            return ctx.enter_context(nc.psum_tensor(name, [P, 512], F32))

        piece_ps = [bank("piece0"), bank("piece1")]
        sum_ps = bank("sum_ps")
        score_ps = [bank("score0"), bank("score1")]
        turn_ps = bank("turn_ps")
        value_ps = bank("value_ps")
        outT_ps = bank("outT_ps")

        logit_ps = [sum_ps, outT_ps]

        x_in = [sem(f"x_in{n}") for n in range(TT)]
        const_in = sem("const_in")
        params_in = sem("params_in")
        lead_in, half_in = sem("lead_in"), sem("half_in")
        rel_in, t5_in = sem("rel_in"), sem("t5_in")
        t5_out = sem("t5_out")
        router_in = sem("router_in")
        block_in = [sem("block_in0"), sem("block_in1")]
        xsq_done, xn_done, xT_done, hT_ready = sem("xsq_done"), sem("xn_done"), sem("xT_done"), sem("hT_ready")
        par_ps, par_ready = sem("par_ps"), sem("par_ready")
        t5_ps, t5v_ready = sem("t5_ps"), sem("t5v_ready")
        bias_ready = sem("bias_ready")
        lam_ready = sem("lam_ready")
        piece_done = sem("piece_done")
        bank_free = [sem("bank_free0"), sem("bank_free1")]
        sq_ready, ss_done, rs_ready, qk_ready = sem("sq_ready"), sem("ss_done"), sem("rs_ready"), sem("qk_ready")
        csig_ready, conv_ready = sem("csig_ready"), sem("conv_ready")
        gate_ready, outgate_ready = sem("gate_ready"), sem("outgate_ready")
        ig_v_step, ig_a_step, ig_p_step = sem("ig_v_step"), sem("ig_a_step"), sem("ig_p_step")
        sc_done, mx_ready, ex_done, p_ready = sem("sc_done"), sem("mx_ready"), sem("ex_done"), sem("p_ready")
        sc_read, em_ready = sem("sc_read"), sem("em_ready")
        tp_done, pt_ready, pv_done = sem("tp_done"), sem("pt_ready"), sem("pv_done")
        hn_ready, hx_ready = sem("hn_ready"), sem("hx_ready")
        xt_done, branch_ready = sem("xt_done"), sem("branch_ready")
        zg_ready, y_ready = sem("zg_ready"), sem("y_ready")
        x1_ready = sem("x1_ready")
        xh_step = sem("xh_step")
        xh_ready = sem("xh_ready")
        th_done, tT_ready = sem("th_done"), sem("tT_ready")
        lg_done = sem("lg_done")
        rt_exp = sem("rt_exp")
        hot_ready, pos_done, sel_ready = sem("hot_ready"), sem("pos_done"), sem("sel_ready")
        offs_ready = sem("offs_ready")
        ga_done, xg_free, xg_ready_a, xg_ready_v = sem("ga_done"), sem("xg_free"), sem("xg_ready_a"), sem("xg_ready_v")
        selT_done, selT_ready = sem("selT_done"), sem("selT_ready")
        pads_ready = sem("pads_ready")
        v_step, a_step, p_step = sem("v_step"), sem("a_step"), sem("p_step")
        exp_in = [sem(f"exp_in{n}") for n in range(SLOTS)]
        FAST, GENERAL = ({name: sem(f"{path}_{name}") for name in
                          ("xw_ready", "up_done", "sig_ready", "step", "hid_ready", "hturn_done", "hidT_ready",
                           "down_done", "ysb_ready", "yturn_done", "yg_done")}
                         for path in ("fast", "general"))
        general_in = sem("general_in")
        yg_ready = sem("yg_ready")
        yturn_done, yrow_ready, out_done, out_ready, stored = (sem("yturn_done"), sem("yrow_ready"), sem("out_done"),
                                                               sem("out_ready"), sem("stored"))

        blocks = []
        piece_block = []
        for kind, name, n in PIECES:
            if kind == "igate":
                piece_block.append(None)
            else:
                key = (name, n // 2 if kind == "gate" else 0)
                if key not in blocks:
                    blocks.append(key)
                piece_block.append(blocks.index(key))
        n_in = len(blocks)
        BRANCH_ORDER = (0, 2, 1)
        blocks += [("branch", b) for b in BRANCH_ORDER] + [("out", n) for n in range(2)]

        last_piece = [max(i for i, b in enumerate(piece_block) if b == n) for n in range(n_in)]
        last_piece += [NP + 4 * n + 3 for n in range(3)]

        def block_source(key):
            name, n = key
            if name == "branch":
                return w_branch[0, n].rearrange("(k p) n -> p k n", p=P), 4
            if name == "out":
                return w_out[0].rearrange("(k p) n -> p k n", p=P)[:, :, 512 * n:512 * n + 512], KD
            if name == "g":
                at = COL["g"] + D * BRANCH_ORDER[n // 2] + 512 * (n % 2)
            else:
                at = COL[name]
            return w_in[0].rearrange("(k p) n -> p k n", p=P)[:, :, at:at + 512], KD

        def block_sb(n, k):
            return slots_w[n % 2].rearrange("p (k n) -> p k n", k=k)

        norm_pieces = [i for i, p in enumerate(PIECES) if p[0] == "norm"]
        conv_pieces = [i for i, p in enumerate(PIECES) if p[0] == "conv"]
        gate_pieces = [i for i, p in enumerate(PIECES) if p[0] == "gate"]
        late_gates = [i for i in gate_pieces if i < SIG_SLOT]
        IG = [p[0] for p in PIECES].index("igate")
        turned = [u for u, (br, h) in enumerate(UNITS) if br != "B" or h % 2]
        normed = [u for u, (br, h) in enumerate(UNITS) if br != "B"]

        def freed(i):
            return i // 2 + 1

        def gate_of(g):
            return gates[:, 2 * SEQ * g:2 * SEQ * (g + 1)]

        def piece_of(name, half):
            return next(i for i, p in enumerate(PIECES) if p[1] == name and p[2] == half)

        def unit_in_slot(i, lag):
            u = i - U0 - lag
            return u if 0 <= u < NU else None

        def wait_values(eng, name):
            for half in range(2):
                i = piece_of(name, half)
                eng.wait_ge(bank_free[i % 2], freed(i))

        BR = dict(A=0, B=1, C=2)

        def xT_ps(k):
            return [piece_ps[0], piece_ps[1], score_ps[0], score_ps[1]][k // 2][:, SEQ * (k % 2):SEQ * (k % 2) + SEQ]

        def gather_ps(k):
            return [piece_ps[0], piece_ps[1], sum_ps][k % 3]

        def rt_of(t):
            at, found = 896 * t, {}
            for name, n in (("lg", GROUPS + EXPERTS), ("gm", 1), ("ngm", 1), ("g4", GROUPS), ("gi", 1), ("el", EXPERTS),
                            ("m", 2), ("i", 2), ("o1", EXPERTS), ("o2", EXPERTS), ("hot", EXPERTS), ("bef", EXPERTS),
                            ("d", 1), ("ge", GROUPS), ("gs", 1), ("e2", 1), ("w", 2), ("pos", 2), ("tmp", PAIRS)):
                found[name] = rt[:, at:at + n]
                at += n
            return found

        def load_expert(eng, e, r, done=None):
            done = done or exp_in[r]
            eng.dma_start(w_gate_up[r][:, 0], w_e_gate[0, bass.ds(e, 1)].rearrange("o (p k) f -> p (o k) f", k=KD)).then_inc(done, 16)
            eng.dma_start(w_gate_up[r][:, 1], w_e_up[0, bass.ds(e, 1)].rearrange("o (p k) f -> p (o k) f", k=KD)).then_inc(done, 16)
            eng.dma_start(w_down[r], w_e_down[0, bass.ds(e, 1)].rearrange("o (f p) d -> p (o f) d", p=P)).then_inc(done, 16)

        up_ps, hturn_ps, down_ps, yturn_ps = score_ps, sum_ps, piece_ps, [turn_ps, value_ps]

        def window(eng, e, j):
            return eng.value_load(offs_i[0:1, bass.ds(EXPERTS * j + e, 1)], min_val=0, max_val=PAIRS)

        def first(n, k):
            return isinstance(n, int) and n < k

        def window_tokens(dve, S, n, b, e, j):
            off = window(dve, e, j)
            if not first(n, 2):
                dve.wait_ge(S["up_done"], n - 1)
            dve.tensor_copy(xw[b], xg[:, :, bass.ds(off, WIN)]).then_inc(S["xw_ready"], 1)

        def window_up(pe, S, n, b, r):
            pe.wait_ge(S["xw_ready"], n + 1)
            if not first(n, 2):
                pe.wait_ge(S["hid_ready"], n - 1)
            for k in range(KD):
                for f in range(FC):
                    ins = pe.matmul(up_ps[b][WIN * f:WIN * f + WIN, 0:2 * P].rearrange("p (m f) -> p m f", m=2),
                                    xw[b][:, k, :], w_gate_up[r][:, :, k, P * f:P * f + P], start=(k == 0), stop=(k == KD - 1))
            ins.then_inc(S["up_done"], 1)

        def window_sigmoid(act, S, n, b):
            act.wait_ge(S["up_done"], n + 1)
            if not first(n, 2):
                act.wait_ge(S["hid_ready"], n - 1)
            act.activation(eg[b], up_ps[b][:, 0:P], ACT.Sigmoid).then_inc(S["sig_ready"], 1)

        def window_hidden(dve, S, n, b):
            dve.wait_ge(S["sig_ready"], n + 1)
            dve.tensor_tensor(eg[b], up_ps[b][:, 0:P], eg[b], ALU.mult).then_inc(S["step"], 1)
            dve.wait_ge(S["step"], n + 1)
            if not first(n, 2):
                dve.wait_ge(S["hturn_done"], n - 1)
            dve.tensor_tensor(hid[b], up_ps[b][:, P:2 * P], eg[b], ALU.mult).then_inc(S["hid_ready"], 1)

        def window_turn_hidden(pe, S, n, b):
            pe.wait_ge(S["hid_ready"], n + 1)
            if not first(n, 1):
                pe.wait_ge(S["hidT_ready"], n)
            pe.transpose(hturn_ps[:, 0:P], hid[b], ident).then_inc(S["hturn_done"], 1)

        def window_hiddenT(dve, S, n, b):
            dve.wait_ge(S["hturn_done"], n + 1)
            if not first(n, 2):
                dve.wait_ge(S["down_done"], n - 1)
            dve.tensor_copy(hidT[b], hturn_ps[:, 0:P]).then_inc(S["hidT_ready"], 1)

        def window_down(pe, S, n, b, r):
            pe.wait_ge(S["hidT_ready"], n + 1)
            if not first(n, 2):
                pe.wait_ge(S["ysb_ready"], n - 1)
            for f in range(FC):
                for half in range(2):
                    ins = pe.matmul(down_ps[b][WIN * half:WIN * half + WIN, :], hidT[b][:, WIN * f:WIN * f + WIN],
                                    w_down[r][:, f, 512 * half:512 * half + 512], start=(f == 0), stop=(f == FC - 1))
            ins.then_inc(S["down_done"], 1)

        def window_result(act, S, n, b):
            act.wait_ge(S["down_done"], n + 1)
            if not first(n, 2):
                act.wait_ge(S["yturn_done"], n - 1)
            act.copy(ysb[b], down_ps[b][:, :]).then_inc(S["ysb_ready"], 1)

        def window_turn_result(pe, S, n, b):
            pe.wait_ge(S["ysb_ready"], n + 1)
            if not first(n, 2):
                pe.wait_ge(S["yg_done"], n - 1)
            for ch in range(4):
                ins = pe.transpose(yturn_ps[b][:, P * ch:P * ch + P], ysb[b][:, P * ch:P * ch + P], ident)
            ins.then_inc(S["yturn_done"], 1)

        def window_store(act, S, n, b, e, j):
            off = window(act, e, j)
            act.wait_ge(S["yturn_done"], n + 1)
            if not first(n, 1):
                act.wait_ge(S["yg_done"], n)
            act.copy(yg[:, :, bass.ds(off, WIN)].rearrange("p (h c) n -> p h c n", h=2),
                     yturn_ps[b][:, :].rearrange("p (c h n) -> p h c n", c=4, h=2)).then_inc(S["yg_done"], 1)

        def general_path(eng):
            largest = eng.value_load(offs_i[0:1, WINDOWS * EXPERTS:WINDOWS * EXPERTS + 1], min_val=0, max_val=PAIRS)
            return eng.If(largest > LIMIT)

        def every_expert(eng, one):
            one(0)
            with eng.Fori(1, EXPERTS) as e:
                one(e)

        final_ps = [score_ps[0], score_ps[1], turn_ps, value_ps]

        def load_rest(sp):
            rest_from = CONST["mask_chunk"][0]
            sp.dma_start(t5hot, consts[:, KEPT:]).then_inc(lead_in, 16)
            sp.dma_start(t5[:, :], t5_bias).then_inc(lead_in, 16)
            sp.dma_start(w_if[:, :, :], w_in[0].rearrange("(k p) n -> p k n", p=P)[:, :, COL["aif"]:COL["aif"] + 8]).then_inc(lead_in, 16)
            sp.dma_start(lam_in.rearrange("p a b -> p (a b)"),
                         c_lambda.rearrange("l a b -> (l a b)").partition_broadcast(P)).then_inc(lead_in, 16)
            sp.dma_start(ga, a_out_norm_g.rearrange("l a b -> (l a b)").partition_broadcast(P)).then_inc(lead_in, 16)
            sp.dma_start(gc08, c_sub_norm_g.rearrange("l a -> (l a)").partition_broadcast(P)).then_inc(lead_in, 16)
            sp.dma_start(bc_small[:, 0:8], a_gate_bias.rearrange("l a -> (l a)").partition_broadcast(P)).then_inc(lead_in, 16)
            sp.dma_start(cst[:, rest_from:], consts[:, rest_from:KEPT]).then_inc(lead_in, 16)

        LEAD = 16 * 8

        def load_tables(sp):
            sp.dma_start(rel_raw.rearrange("p k h -> p (k h)"),
                         bass.AP(b_rel_bias.tensor, 129 * B_HEADS, [[B_HEADS, P], [1, SEQ * B_HEADS]])).then_inc(rel_in, 16)
            for dst, src_ap in (
                (bc_small[:, 8:12], b_group.rearrange("l a -> (l a)").partition_broadcast(P)),
                (bc_small[:, 12:44], b_router.rearrange("l a -> (l a)").partition_broadcast(P)),
                (w_rt[:, :, 0:GROUPS], w_group[0].rearrange("(p k) n -> p k n", k=KD)),
                (w_rt[:, :, GROUPS:], w_router[0].rearrange("(p k) n -> p k n", k=KD)),
                (g2[:, :], norm2_g.rearrange("l (p k) -> (l p) k", k=KD)),
            ):
                sp.dma_start(dst, src_ap).then_inc(router_in, 16)

        with nc.Block() as block:
            @block.sync
            def _(sp):
                for t in range(TT):
                    sp.dma_start(xs[:, t, :], x[0, P * t:P * t + P, :]).then_inc(x_in[t], 16)
                for n, key in enumerate(blocks):
                    if n >= 2:
                        sp.wait_ge(piece_done, last_piece[n - 2] + 1)
                    src_ap, k = block_source(key)
                    if n == 0:
                        sp.dma_start(block_sb(n, k)[:, :, 0:SEQ], src_ap[:, :, 0:SEQ]).then_inc(half_in, 16)
                        sp.dma_start(block_sb(n, k)[:, :, SEQ:], src_ap[:, :, SEQ:]).then_inc(block_in[n % 2], 16)
                        load_rest(sp)
                        continue
                    sp.dma_start(block_sb(n, k), src_ap).then_inc(block_in[n % 2], 16)
                    if n == 1:
                        load_tables(sp)
                    if n == 3:
                        load_expert(sp, 0, 0)
                    if n == n_in + 1:
                        sp.wait_ge(pv_done, NU)
                        sp.wait_ge(sc_read, NU)
                        load_expert(sp, 1, 1)
                        load_expert(sp, 2, 2)
                sp.wait_ge(zg_ready, 12)
                load_expert(sp, 3, 3)
                with sp.Fori(1, EXPERTS // SLOTS) as i:
                    for r in range(SLOTS):
                        sp.wait_ge(FAST["down_done"], (i - 1) * SLOTS + r + 1)
                        load_expert(sp, i * SLOTS + r, r)
                sp.wait_ge(offs_ready, 1)
                with general_path(sp):
                    sp.wait_ge(FAST["down_done"], EXPERTS)

                    def load(e):
                        if not first(e, 1):
                            sp.wait_ge(GENERAL["down_done"], e * WINDOWS)
                        load_expert(sp, e, 0, general_in)

                    every_expert(sp, load)
                for g in range(4):
                    t, half = g // 2, g % 2
                    sp.wait_ge(out_ready, g + 1)
                    sp.dma_start(out[0, P * t:P * t + P, 512 * half:512 * half + 512],
                                 xs[:, t, 512 * half:512 * half + 512]).then_inc(stored, 16)
                sp.wait_ge(stored, 64)

            @block.gpsimd
            def _(pool):
                for i in range(NP + 1):
                    if i >= 1 and i - 1 in norm_pieces:
                        n = norm_pieces.index(i - 1)
                        name, half = PIECES[i - 1][1:]
                        pool.wait_ge(rs_ready, n + 1)
                        pool.wait_ge(bank_free[(i - 1) % 2], freed(i - 1))
                        at = QK[name] + 2 * half
                        pool.tensor_tensor(qk[:, at:at + 2, :].rearrange("p n t -> p (n t)"), ug[n % 2], rs_w[n % 2],
                                           ALU.mult).then_inc(qk_ready, 1)
                    if i >= 1 and i - 1 in conv_pieces:
                        n = conv_pieces.index(i - 1)
                        name, half = PIECES[i - 1][1:]
                        pool.wait_ge(csig_ready, n + 1)
                        at = QK[name] + 2 * half
                        pool.tensor_tensor(qk[:, at:at + 2, :].rearrange("p n t -> p (n t)"), ug[n % 2], rs_w[n % 2],
                                           ALU.mult).then_inc(conv_ready, 1)
                    if i >= 1 and i - 1 < NP and PIECES[i - 1][1] == "ao":
                        g = PIECES[i - 1][2]
                        pool.wait_ge(lead_in, LEAD)
                        pool.wait_ge(bank_free[(i - 1) % 2], freed(i - 1))
                        pool.tensor_tensor(out_gate[:, g, :], out_gate[:, g, :], ga, ALU.mult).then_inc(outgate_ready, 1)
                    if i == IG + 1:
                        pool.wait_ge(lead_in, LEAD)
                        pool.wait_ge(rel_in, 16)
                        for h in range(B_HEADS):
                            pool.tensor_tensor(bias[:, C_HEADS + h, :], rel_raw[:, ::-1, h], c("mask_chunk"), ALU.add).then_inc(bias_ready, 1)
                        pool.wait_ge(t5_in, 16)
                        for h in range(C_HEADS):
                            pool.tensor_tensor(bias[:, h, :], t5_raw[:, ::-1, h], c("mask_chunk"), ALU.add).then_inc(bias_ready, 1)
                for j in range(4, 12):
                    pool.wait_ge(zg_ready, j + 1)
                    if j >= 8:
                        pool.wait_ge(y_ready, j - 7)
                    o = yT[:, 2 * (j % 4):2 * (j % 4) + 2, :].rearrange("p n t -> p (n t)")
                    pool.tensor_tensor(o, o, sq[j % 2], ALU.add).then_inc(y_ready, 1)

            @block.scalar
            def _(act):
                act.preload_act_table_set(LN_EXP_SET)
                first_part = CONST["mask_chunk"][0]
                act.dma_start(cst[:, 0:first_part], consts[:, 0:first_part]).then_inc(const_in, 16)
                for rows, src_ap in (
                    (slice(0, 32), a_conv_w[0].rearrange("w (c p) -> (w c) p", p=P)),
                    (slice(32, 40), a_conv_b.rearrange("l (c p) -> (l c) p", p=P)),
                    (slice(40, 48), norm1_g.rearrange("l (c p) -> (l c) p", p=P)),
                ):
                    act.dma_start(small[rows, :], src_ap).then_inc(params_in, 16)
                for at, g in ((48, b_qk_norm_g), (50, c_qk_norm_g)):
                    for half in range(2):
                        act.dma_start(small[at:at + 2, 64 * half:64 * half + 64], g[0]).then_inc(params_in, 16)

                for t in range(TT):
                    act.wait_ge(x_in[t], 16)
                    act.activation(work[:, 1024 * t:1024 * t + 1024], xs[:, t, :], ACT.Square, accum_out=ss1[:, t:t + 1]).then_inc(xsq_done, 1)
                act.wait_ge(xsq_done, TT)
                act.wait_ge(const_in, 16)
                act.activation(rstd1, ss1, ACT.Ln, bias=eps, scale=1.0 / D).then_inc(a_step, 1)
                act.wait_ge(a_step, 1)
                act.activation(rstd1, rstd1, ACT.Exp, scale=-0.5).then_inc(a_step, 1)
                act.wait_ge(par_ps, 1)
                act.copy(par[:, 0:52], sum_ps[:, 0:52]).then_inc(par_ready, 1)
                steps = 2
                act.preload_act_table_set(SIGMOID_SET)

                for i in range(NP + DRAIN + 1):
                    if i == 3:
                        act.wait_ge(t5_ps, 1)
                        act.copy(t5v[:, :, :].rearrange("p c h -> p (c h)"), outT_ps[:, 0:12]).then_inc(t5v_ready, 1)
                        act.wait_ge(t5v_ready, 1)
                        act.dma_start(scratch.rearrange("(c p h) -> p c h", p=P, h=C_HEADS), t5v[:, :, :]).then_inc(t5_out, 16)
                    if i == 5:
                        act.wait_ge(t5_out, 16)
                        act.dma_start(t5_raw.rearrange("p k h -> p (k h)"),
                                      bass.AP(scratch.tensor, 0, [[C_HEADS, P], [1, SEQ * C_HEADS]])).then_inc(t5_in, 16)
                    if i == IG + 1:
                        act.preload_act_table_set(LN_EXP_SET)
                        act.wait_ge(lam_ready, 2)
                        act.activation(lam_e, lam_s, ACT.Exp).then_inc(lam_ready, 1)
                    if i == SIG_SLOT:
                        act.preload_act_table_set(SIGMOID_SET)
                        for p in late_gates:
                            n = PIECES[p][2]
                            act.wait_ge(bank_free[p % 2], freed(p))
                            act.activation(gate_of(n), gate_of(n), ACT.Sigmoid).then_inc(gate_ready, 1)
                    u = unit_in_slot(i, 1)
                    if u is not None:
                        act.wait_ge(tp_done, u + 1)
                        if u >= 1:
                            act.wait_ge(pv_done, u)
                        act.copy(PT[0], turn_ps[:, 0:384]).then_inc(pt_ready, 1)
                    u = unit_in_slot(i, 2)
                    if u is not None and UNITS[u][0] != "B":
                        par_u, z = u % 2, u % 3
                        act.wait_ge(pv_done, u + 1)
                        if u >= 2:
                            act.wait_ge(hx_ready, u - 1)
                        for t in range(TT):
                            kw = dict(scale=rc[z][:, t:t + 1]) if UNITS[u][0] == "A" else {}
                            act.activation(work[:, 5504:5632],
                                           value_ps[:, 128 * t:128 * t + 128], ACT.Square,
                                           accum_out=ssu[z][:, t:t + 1], **kw).then_inc(a_step, 1)
                            steps += 1
                            act.wait_ge(a_step, steps)
                        act.activation(rsu[z], ssu[z], ACT.Ln, bias=eps, scale=1.0 / C_DV).then_inc(a_step, 1)
                        steps += 1
                        act.wait_ge(a_step, steps)
                        act.activation(rsu[z], rsu[z], ACT.Exp, scale=-0.5).then_inc(hn_ready, 1)
                    u = unit_in_slot(i, 3)
                    if u is not None and u in turned:
                        br, h = UNITS[u]
                        ch = h // 2 if br == "B" else h
                        act.wait_ge(xt_done, turned.index(u) + 1)
                        act.copy(branchT[:, BR[br], ch, :], outT_ps[:, 0:SEQ]).then_inc(branch_ready, 1)
                    u = unit_in_slot(i, 0)
                    if u is not None:
                        br, h = UNITS[u]
                        par_u, z = u % 2, u % 3
                        act.wait_ge(mx_ready, u + 1)
                        spans = [(0, 128), (128, 384)]
                        todo = []
                        for m, S in enumerate((S1[par_u], S2[par_u]) if br == "C" else (S1[par_u],)):
                            for t, (a, b) in enumerate(spans):
                                todo.append((S[:, a:b], 2 * m + t))
                        for j, (ap, col) in enumerate(todo):
                            kw = {} if br == "A" else dict(accum_out=sm[z][:, col:col + 1])
                            last = act.activation(ap, ap, ACT.Exp, bias=nm[z][:, col:col + 1], **kw)
                        last.then_inc(ex_done, 1)
                        if br == "A":
                            act.activation(em[z], mm[z], ACT.Exp).then_inc(em_ready, 1)
                    if i >= 1 and i - 1 in norm_pieces:
                        j = norm_pieces.index(i - 1)
                        act.wait_ge(ss_done, j + 1)
                        if j >= 2:
                            act.wait_ge(qk_ready, j - 1)
                        else:
                            act.wait_ge(conv_ready, len(conv_pieces))
                        act.activation(rs_w[j % 2], sum_ps[:, :], ACT.Ln, bias=eps, scale=1.0 / B_DH).then_inc(a_step, 1)
                        steps += 1
                        act.wait_ge(a_step, steps)
                        act.activation(rs_w[j % 2], rs_w[j % 2], ACT.Exp, scale=-0.5).then_inc(rs_ready, 1)
                    if i == IG + 1:
                        act.wait_ge(ig_v_step, 3)
                        z3 = ig_z.rearrange("p (t n) -> p t n", t=TT)
                        e3 = ig_e.rearrange("p (t n) -> p t n", t=TT)
                        act.activation(e3[:, :, 0:4], z3[:, :, 0:4], ACT.Exp, scale=2.0 / GATE_CAP).then_inc(ig_a_step, 1)
                        act.activation(e3[:, :, 4:8], e3[:, :, 4:8], ACT.Exp, scale=-1.0).then_inc(ig_a_step, 1)
                        act.wait_ge(ig_a_step, 2)
                        act.activation(e3[:, :, 4:8], e3[:, :, 4:8], ACT.Ln, bias=1.0).then_inc(ig_a_step, 1)
                    if i < NP:
                        kind, name, n = PIECES[i]
                        ps = piece_ps[i % 2]
                        act.wait_ge(piece_done, i + 1)
                        if kind == "norm":
                            j = norm_pieces.index(i)
                            if j >= 2:
                                act.wait_ge(ss_done, j - 1)
                            act.activation(sq[j % 2], ps[:, :], ACT.Square).then_inc(sq_ready, 1)
                        elif kind == "value" and name != "ao":
                            act.copy(vals[:, VAL[name], n, :], ps[:, :]).then_inc(bank_free[i % 2], 1)
                        elif kind == "value":
                            act.activation(out_gate[:, n, :], ps[:, :], ACT.Sigmoid).then_inc(bank_free[i % 2], 1)
                        elif kind == "gate":
                            if n == 0:
                                act.wait_ge(bias_ready, 12)
                            func = ACT.Copy if i in late_gates else ACT.Sigmoid
                            act.activation(gate_of(n), ps[:, :], func).then_inc(bank_free[i % 2], 1)
                    if i < NP and i in conv_pieces:
                        j = conv_pieces.index(i)
                        act.wait_ge(bank_free[i % 2], freed(i))
                        if j >= 2:
                            act.wait_ge(conv_ready, j - 1)
                        act.activation(rs_w[j % 2], ug[j % 2], ACT.Sigmoid).then_inc(csig_ready, 1)

                act.preload_act_table_set(LN_EXP_SET)
                for t in range(TT):
                    act.wait_ge(x1_ready, 2 * t + 2)
                    act.activation(ug_pair, xs[:, t, :], ACT.Square, accum_out=ss2[:, t:t + 1]).then_inc(a_step, 1)
                    steps += 1
                    act.wait_ge(a_step, steps)
                    act.activation(rstd2[:, t:t + 1], ss2[:, t:t + 1], ACT.Ln, bias=eps, scale=1.0 / D).then_inc(a_step, 1)
                    steps += 1
                    act.wait_ge(a_step, steps)
                    act.activation(rstd2[:, t:t + 1], rstd2[:, t:t + 1], ACT.Exp, scale=-0.5).then_inc(xh_step, 1)
                for t in range(TT):
                    for half in range(2):
                        act.wait_ge(th_done, 2 * t + half + 1)
                        act.copy(tT[:, 4 * half:4 * half + 4, P * t:P * t + P],
                                 [score_ps[0], score_ps[1], turn_ps, value_ps][2 * t + half][:, :]
                                 .rearrange("p (k n) -> p k n", k=4)).then_inc(tT_ready, 1)
                for t in range(TT):
                    act.wait_ge(hot_ready, 3 * t + 1)
                    R = rt_of(t)
                    act.activation(R["ge"], R["lg"][:, 0:GROUPS], ACT.Exp, bias=R["ngm"], accum_out=R["gs"]).then_inc(rt_exp, 1)
                    act.wait_ge(hot_ready, 3 * t + 2)
                    act.activation(R["e2"], R["d"], ACT.Exp).then_inc(rt_exp, 1)
                for k in range(0, KD, 2):
                    act.wait_ge(ga_done, k + 1)
                    act.activation(xg[:, k, 0:PAIRS], gather_ps(k)[:, :], ACT.Copy, scale=g2[:, k:k + 1]).then_inc(xg_ready_a, 1)
                for t in range(TT):
                    act.wait_ge(selT_done, t + 1)
                    act.copy(selT[:, :, P * t:P * t + P],
                             outT_ps[:, :].rearrange("p (s n) -> p s n", s=4)).then_inc(selT_ready, 1)
                act.preload_act_table_set(SIGMOID_SET)
                for e in range(SLOTS):
                    window_sigmoid(act, FAST, e, e % 2)
                    if e >= 2:
                        window_store(act, FAST, e - 2, e % 2, e - 2, 0)
                    if e >= 1:
                        window_result(act, FAST, e - 1, (e - 1) % 2)
                with act.Fori(1, EXPERTS // SLOTS) as i:
                    for r in range(SLOTS):
                        e = i * SLOTS + r
                        window_sigmoid(act, FAST, e, r % 2)
                        window_store(act, FAST, e - 2, r % 2, e - 2, 0)
                        window_result(act, FAST, e - 1, (r - 1) % 2)
                last = EXPERTS - 1
                window_store(act, FAST, last - 1, 0, last - 1, 0)
                window_result(act, FAST, last, 1)
                window_store(act, FAST, last, 1, last, 0)
                with general_path(act):
                    act.wait_ge(FAST["hid_ready"], EXPERTS)

                    def expert(e):
                        for j in range(WINDOWS):
                            n = e * WINDOWS + j
                            window_sigmoid(act, GENERAL, n, j % 2)
                            window_result(act, GENERAL, n, j % 2)
                            window_store(act, GENERAL, n, j % 2, e, j)

                    every_expert(act, expert)
                act.copy(st[:, 255:256], eps).then_inc(yg_ready, 1)
                for g in range(8):
                    s, half = g // 2, g % 2
                    act.wait_ge(yturn_done, g + 1)
                    act.copy(yrows[:, s, 512 * half:512 * half + 512], piece_ps[g % 2][:, :]).then_inc(yrow_ready, 1)

            @block.vector
            def _(dve):
                steps = 0
                for t in range(TT):
                    dve.wait_ge(a_step, 2)
                    dve.tensor_scalar(work[:, 2048 + 1024 * t:3072 + 1024 * t], xs[:, t, :], rstd1[:, t:t + 1], None,
                                      ALU.mult).then_inc(xn_done, 1)
                dve.wait_ge(par_ready, 1)
                for k in range(KD):
                    dve.wait_ge(xT_done, 2 * (k // 2) + 2)
                    dve.tensor_scalar(hT[:, k, :], xT_ps(k), par[:, NORM1 + k:NORM1 + k + 1], None, ALU.mult).then_inc(hT_ready, 1)
                dve.tensor_scalar(par[:, 54:55], par[:, QKG:QKG + 1], B_DH ** -0.5, None, ALU.mult).then_inc(v_step, 1)
                dve.tensor_scalar(par[:, 55:56], par[:, QKG + 2:QKG + 3], C_DQK ** -0.5, None, ALU.mult).then_inc(v_step, 1)
                steps += 2
                dve.wait_ge(v_step, 2)
                gain = dict(bq=54, cq=55, bk=QKG + 1, ck=QKG + 3)

                for i in range(NP + DRAIN + 1):
                    if i == IG - 1:
                        dve.wait_ge(lead_in, LEAD)
                        for j in range(2):
                            dve.tensor_tensor_reduce(S1[j][:, 0:C_DQK], lam_in[:, 2 * j, :], lam_in[:, 2 * j + 1, :],
                                                     1.0, 0.0, ALU.mult, ALU.add, lam_s[:, j:j + 1]).then_inc(lam_ready, 1)
                    if i == IG + 2:
                        dve.wait_ge(lam_ready, 3)
                        dve.scalar_tensor_tensor(out=neg_lam, in0=lam_e[:, 1:2], scalar=LAM_INIT, in1=lam_e[:, 0:1],
                                                 op0=ALU.subtract, op1=ALU.subtract).then_inc(lam_ready, 1)
                        dve.tensor_scalar(gc08, gc08, 1.0 - LAM_INIT, None, ALU.mult).then_inc(lam_ready, 1)
                    if i == IG + 3:
                        dve.wait_ge(ig_p_step, 1)
                        dve.tensor_copy(cum, outT_ps[:, 0:8]).then_inc(ig_v_step, 1)
                        dve.wait_ge(ig_v_step, 8)
                        dve.tensor_tensor(src, ig_v, cum, ALU.subtract).then_inc(ig_v_step, 1)
                    u = unit_in_slot(i, 0)
                    if u is not None:
                        br, h = UNITS[u]
                        q, z = u % 2, u % 3
                        dve.wait_ge(sc_done, u + 1)
                        if u >= 2:
                            dve.wait_ge(tp_done, u - 1)
                        if br == "C" and h == 0:
                            dve.wait_ge(bias_ready, 12)
                            dve.wait_ge(lam_ready, 5)
                        if br in "BC":
                            hb = h if br == "C" else C_HEADS + h
                            maps = [(S1[q], score_ps[u % 2])] if br == "B" else [(S1[q], score_ps[0]), (S2[q], score_ps[1])]
                            adds = [(S, ps, bias[:, hb, :]) for S, ps in maps]
                        else:
                            adds = [(S1[q], None, c("mask_tri"))]
                        n_mx = 2 * len(adds)
                        for m, (S, ps, bb) in enumerate(adds):
                            for t in range(TT):
                                sa = slice(0, 128) if t == 0 else slice(128, 384)
                                pa = score_ps[1][:, 0:P * (t + 1)] if br == "A" else ps[:, sa]
                                ins = dve.tensor_tensor_reduce(S[:, sa], pa, bb[:, P * (1 - t):SEQ], 1.0, LOWEST,
                                                               ALU.add, ALU.max, mx[z][:, 2 * m + t:2 * m + t + 1])
                                if br != "A" and m == len(adds) - 1 and t == 1:
                                    ins.then_inc(sc_read, 1)
                                else:
                                    ins.then_inc(v_step, 1)
                                    steps += 1
                        dve.wait_ge(v_step, steps)
                        if br != "A":
                            dve.wait_ge(sc_read, u + 1)
                            dve.tensor_scalar(nm[z][:, 0:n_mx], mx[z][:, 0:n_mx], -1.0, None, ALU.mult).then_inc(mx_ready, 1)
                        else:
                            dve.tensor_scalar(nm[z][:, 0:2], mx[z][:, 0:2], 0.0, -1.0, ALU.max, ALU.mult).then_inc(v_step, 1)
                            steps += 1
                            dve.wait_ge(v_step, steps)
                            dve.tensor_tensor(mm[z], nm[z][:, 0:2], cum[:, h:8:4], ALU.subtract).then_inc(mx_ready, 1)
                    u = unit_in_slot(i, 2)
                    if u is not None:
                        br, h = UNITS[u]
                        q, z = u % 2, u % 3
                        dve.wait_ge(pv_done, u + 1)
                        nx = turned.index(u) if u in turned else turned.index(u + 1)
                        if nx >= 2:
                            dve.wait_ge(xt_done, nx - 1)
                        H = hx[nx % 2]
                        if br == "B":
                            for t in range(TT):
                                ins = dve.tensor_scalar(H[:, t, 64 * (h % 2):64 * (h % 2) + 64], value_ps[:, 64 * t:64 * t + 64],
                                                        rc[z][:, t:t + 1], None, ALU.mult)
                                if t:
                                    ins.then_inc(hx_ready, 1)
                                else:
                                    ins.then_inc(v_step, 1)
                                    steps += 1
                                    dve.wait_ge(v_step, steps)
                        else:
                            dve.wait_ge(hn_ready, normed.index(u) + 1)
                            if br == "A":
                                dve.wait_ge(outgate_ready, 2)
                                dve.tensor_tensor(rr[z], rsu[z], rc[z][:, 0:2], ALU.mult).then_inc(v_step, 1)
                                steps += 1
                                dve.wait_ge(v_step, steps)
                            for t in range(TT):
                                sc_ap = (rr if br == "A" else rsu)[z][:, t:t + 1]
                                g_ap = out_gate[:, t, P * h:P * h + P] if br == "A" else gc08
                                ins = dve.scalar_tensor_tensor(out=H[:, t, :], in0=value_ps[:, P * t:P * t + P], scalar=sc_ap, in1=g_ap,
                                                               op0=ALU.mult, op1=ALU.mult)
                                if t:
                                    ins.then_inc(hx_ready, 1)
                                else:
                                    ins.then_inc(v_step, 1)
                                    steps += 1
                                    dve.wait_ge(v_step, steps)
                    u = unit_in_slot(i, 0)
                    if u is not None:
                        br, h = UNITS[u]
                        q, z = u % 2, u % 3
                        dve.wait_ge(ex_done, u + 1)
                        if br != "A":
                            if br == "B":
                                dve.reciprocal(rc[z][:, 0:2], sm[z][:, 0:2]).then_inc(p_ready, 1)
                            else:
                                dve.reciprocal(rc[z][:, 0:4], sm[z][:, 0:4]).then_inc(v_step, 1)
                                steps += 1
                                dve.wait_ge(v_step, steps)
                                dve.tensor_scalar(nl[z], rc[z][:, 2:4], neg_lam, None, ALU.mult).then_inc(v_step, 1)
                                steps += 1
                                dve.wait_ge(v_step, steps)
                                for t in range(TT):
                                    sa = slice(0, 128) if t == 0 else slice(128, 384)
                                    dve.tensor_scalar(S2[q][:, sa], S2[q][:, sa], nl[z][:, t:t + 1], None, ALU.mult).then_inc(v_step, 1)
                                    steps += 1
                                for t in range(TT):
                                    sa = slice(0, 128) if t == 0 else slice(128, 384)
                                    dve.wait_ge(v_step, steps)
                                    dve.scalar_tensor_tensor(out=S2[q][:, sa], in0=S1[q][:, sa], scalar=rc[z][:, t:t + 1],
                                                             in1=S2[q][:, sa], op0=ALU.mult, op1=ALU.add).then_inc(p_ready if t else v_step, 1)
                                    if not t:
                                        steps += 1
                        else:
                            for t in range(TT):
                                sa = slice(0, 128) if t == 0 else slice(128, 384)
                                dve.tensor_tensor_reduce(S2[q][:, sa], score_ps[0][:, sa], S1[q][:, sa], A_DH ** -0.5, 0.0,
                                                         ALU.mult, ALU.add, sm[z][:, t:t + 1]).then_inc(sc_read if t else v_step, 1)
                                if not t:
                                    steps += 1
                            dve.wait_ge(v_step, steps)
                            dve.wait_ge(sc_read, u + 1)
                            dve.wait_ge(em_ready, h + 1)
                            dve.scalar_tensor_tensor(out=rc[z][:, 0:2], in0=sm[z][:, 0:2], scalar=-1.0, in1=sm[z][:, 0:2],
                                                     op0=ALU.mult, op1=ALU.max).then_inc(v_step, 1)
                            steps += 1
                            dve.wait_ge(v_step, steps)
                            dve.tensor_tensor(rc[z][:, 0:2], rc[z][:, 0:2], em[z], ALU.max).then_inc(v_step, 1)
                            steps += 1
                            dve.wait_ge(v_step, steps)
                            dve.reciprocal(rc[z][:, 0:2], rc[z][:, 0:2]).then_inc(p_ready, 1)
                    if i == IG + 2:
                        z3 = ig_z.rearrange("p (t n) -> p t n", t=TT)
                        e3 = ig_e.rearrange("p (t n) -> p t n", t=TT)
                        lf3 = lf.rearrange("p (t n) -> p t n", t=TT)
                        iv3 = ig_v.rearrange("p (t n) -> p t n", t=TT)
                        dve.wait_ge(ig_a_step, 3)
                        dve.tensor_tensor(lf3, z3[:, :, 4:8], e3[:, :, 4:8], ALU.subtract).then_inc(ig_v_step, 1)
                        dve.tensor_scalar(e3[:, :, 0:4], e3[:, :, 0:4], 1.0, None, ALU.add).then_inc(ig_v_step, 1)
                        dve.wait_ge(ig_v_step, 5)
                        dve.reciprocal(e3[:, :, 0:4], e3[:, :, 0:4]).then_inc(ig_v_step, 1)
                        dve.wait_ge(ig_v_step, 6)
                        dve.tensor_scalar(iv3, e3[:, :, 0:4], -2.0 * GATE_CAP, GATE_CAP, ALU.mult, ALU.add).then_inc(ig_v_step, 1)
                    if i < NP:
                        kind, name, n = PIECES[i]
                        ps = piece_ps[i % 2]
                        if kind == "norm":
                            j = norm_pieces.index(i)
                            dve.wait_ge(sq_ready, j + 1)
                            if j >= 2:
                                dve.wait_ge(qk_ready, j - 1)
                            else:
                                dve.wait_ge(conv_ready, len(conv_pieces))
                            dve.tensor_scalar(ug[j % 2], ps[:, :], par[:, gain[name]:gain[name] + 1], None,
                                              ALU.mult).then_inc(bank_free[i % 2], 1)
                        elif kind == "conv":
                            j = conv_pieces.index(i)
                            dve.wait_ge(piece_done, i + 1)
                            if j >= 2:
                                dve.wait_ge(conv_ready, j - 1)
                            ch0 = (0 if name == "aq" else 4) + 2 * n
                            for w in range(4):
                                for half in range(2):
                                    ch = ch0 + half
                                    col = par[:, CONVW + 8 * w + ch:CONVW + 8 * w + ch + 1]
                                    y = ug[j % 2][:, SEQ * half:SEQ * half + SEQ]
                                    uu = ps[:, SEQ * half:SEQ * half + SEQ]
                                    if w == 0:
                                        ins = dve.tensor_scalar(y, uu, col, par[:, CONVB + ch:CONVB + ch + 1], ALU.mult, ALU.add)
                                    else:
                                        dve.wait_ge(v_step, steps - 1)
                                        ins = dve.scalar_tensor_tensor(out=y[:, w:], in0=uu[:, :SEQ - w], scalar=col,
                                                                       in1=y[:, w:], op0=ALU.mult, op1=ALU.add)
                                    if w == 3 and half == 1:
                                        ins.then_inc(bank_free[i % 2], 1)
                                    else:
                                        ins.then_inc(v_step, 1)
                                        steps += 1
                                    if w == 3 and half == 0:
                                        dve.wait_ge(v_step, steps)
                        elif kind == "igate":
                            dve.wait_ge(piece_done, i + 1)
                            z3 = ig_z.rearrange("p (t n) -> p t n", t=TT)
                            e3 = ig_e.rearrange("p (t n) -> p t n", t=TT)
                            for t in range(TT):
                                ins = dve.tensor_tensor(z3[:, t, :], ps[:, 8 * t:8 * t + 8], bc_small[:, 0:8], ALU.add)
                                ins.then_inc(bank_free[i % 2] if t else ig_v_step, 1)
                            dve.wait_ge(ig_v_step, 1)
                            dve.wait_ge(bank_free[i % 2], freed(i))
                            dve.scalar_tensor_tensor(out=e3[:, :, 4:8], in0=z3[:, :, 4:8], scalar=-1.0, in1=z3[:, :, 4:8],
                                                     op0=ALU.mult, op1=ALU.max).then_inc(ig_v_step, 1)
                            dve.tensor_scalar(z3[:, :, 4:8], z3[:, :, 4:8], 0.0, None, ALU.min).then_inc(ig_v_step, 1)

                for j in range(12):
                    i = NP + j
                    dve.wait_ge(piece_done, i + 1)
                    p = gate_pieces[j]
                    if p in late_gates:
                        dve.wait_ge(gate_ready, late_gates.index(p) + 1)
                    else:
                        dve.wait_ge(bank_free[p % 2], freed(p))
                    dst = yT[:, 2 * j:2 * j + 2, :].rearrange("p n t -> p (n t)") if j < 4 else sq[j % 2]
                    if j >= 6:
                        dve.wait_ge(y_ready, j - 5)
                    dve.tensor_tensor(dst, piece_ps[i % 2][:, :], gate_of(j),
                                      ALU.mult).then_inc(zg_ready, 1)
                for j in range(4):
                    i = NP + 12 + j
                    t, half = j // 2, j % 2
                    dve.wait_ge(piece_done, i + 1)
                    o = xs[:, t, 512 * half:512 * half + 512]
                    dve.tensor_tensor(o, piece_ps[i % 2][:, :], o, ALU.add).then_inc(x1_ready, 1)
                dve.wait_ge(router_in, 16 * 5)
                dve.tensor_tensor(w_rt[:, :, :], w_rt[:, :, :], g2[:, :].unsqueeze(2).to_broadcast([P, KD, GROUPS + EXPERTS]),
                                  ALU.mult).then_inc(v_step, 1)
                steps += 1
                for t in range(TT):
                    dve.wait_ge(xh_step, t + 1)
                    dve.tensor_scalar(xhat[:, t, :], xs[:, t, :], rstd2[:, t:t + 1], None, ALU.mult).then_inc(xh_ready, 1)
                dve.memset(xg[:, :, PAIRS:COLS], 0.0).then_inc(pads_ready, 1)

                for t in range(TT):
                    R = rt_of(t)

                    def link(ins):
                        nonlocal steps
                        ins.then_inc(v_step, 1)
                        steps += 1
                        dve.wait_ge(v_step, steps)

                    dve.wait_ge(lg_done, t + 1)
                    link(dve.tensor_tensor(R["lg"], logit_ps[t][:, 0:GROUPS + EXPERTS], bc_small[:, 8:44], ALU.add))
                    link(dve.tensor_reduce(R["gm"], R["lg"][:, 0:GROUPS], AX_X, ALU.max))
                    dve.tensor_scalar(R["ngm"], R["gm"], -1.0, None, ALU.mult).then_inc(hot_ready, 1)
                    link(dve.scalar_tensor_tensor(out=R["g4"], in0=R["lg"][:, 0:GROUPS], scalar=R["gm"], in1=c("prig"),
                                                  op0=ALU.is_equal, op1=ALU.mult))
                    link(dve.tensor_reduce(R["gi"], R["g4"], AX_X, ALU.max))
                    link(dve.tensor_scalar(R["g4"], c("prig"), R["gi"], 1.0, ALU.is_equal, ALU.subtract))
                    link(dve.tensor_scalar(R["g4"], R["g4"], -NEG, None, ALU.mult))
                    link(dve.tensor_tensor(R["el"].rearrange("p (g e) -> p g e", g=GROUPS),
                                           R["lg"][:, GROUPS:].rearrange("p (g e) -> p g e", g=GROUPS),
                                           R["g4"].unsqueeze(2).to_broadcast([P, GROUPS, PER_GROUP]), ALU.add))
                    for j, hot in enumerate((R["o1"], R["o2"])):
                        m, idx = R["m"][:, j:j + 1], R["i"][:, j:j + 1]
                        link(dve.tensor_reduce(m, R["el"], AX_X, ALU.max))
                        link(dve.scalar_tensor_tensor(out=hot, in0=R["el"], scalar=m, in1=c("pri"), op0=ALU.is_equal, op1=ALU.mult))
                        link(dve.tensor_reduce(idx, hot, AX_X, ALU.max))
                        link(dve.tensor_scalar(hot, c("pri"), idx, None, ALU.is_equal))
                        if j == 0:
                            link(dve.scalar_tensor_tensor(out=R["el"], in0=hot, scalar=3 * NEG, in1=R["el"], op0=ALU.mult, op1=ALU.add))
                    dve.tensor_tensor(R["d"], R["m"][:, 1:2], R["m"][:, 0:1], ALU.subtract).then_inc(hot_ready, 1)
                    link(dve.tensor_tensor(R["hot"], R["o1"], R["o2"], ALU.add))
                    link(dve.tensor_scalar(R["bef"], c("pri"), R["i"][:, 0:1], None, ALU.is_lt))
                    dve.scalar_tensor_tensor(out=R["bef"], in0=c("pri"), scalar=R["i"][:, 1:2], in1=R["bef"], op0=ALU.is_lt,
                                             op1=ALU.add).then_inc(hot_ready, 1)
                for t in range(TT):
                    R = rt_of(t)
                    dve.wait_ge(rt_exp, 2 * t + 2)
                    link(dve.tensor_scalar(R["w"][:, 0:1], R["e2"], 1.0, R["gs"], ALU.add, ALU.mult))
                    link(dve.reciprocal(R["w"][:, 0:1], R["w"][:, 0:1]))
                    link(dve.tensor_tensor(R["w"][:, 1:2], R["w"][:, 0:1], R["e2"], ALU.mult))
                for t in range(TT):
                    R = rt_of(t)
                    dve.wait_ge(pos_done, 1)
                    for j, hot in enumerate((R["o1"], R["o2"])):
                        link(dve.tensor_tensor_reduce(R["hot"], hot, outT_ps[:, EXPERTS * t:EXPERTS * t + EXPERTS], 1.0, 0.0,
                                                      ALU.mult, ALU.add, R["pos"][:, j:j + 1]))
                starts, counts = outT_ps[0:1, 64:96], outT_ps[0:1, 96:128]
                for j in range(WINDOWS):
                    link(dve.tensor_scalar(offs_f[:, EXPERTS * j:EXPERTS * j + EXPERTS], starts, float(WIN * j), float(PAIRS),
                                           ALU.add, ALU.min))
                link(dve.tensor_reduce(offs_f[:, WINDOWS * EXPERTS:WINDOWS * EXPERTS + 1], counts, AX_X, ALU.max))
                dve.tensor_copy(offs_i[:, :], offs_f[:, :]).then_inc(offs_ready, 1)
                for t in range(TT):
                    R = rt_of(t)
                    link(dve.tensor_scalar(sel_g[t], c("iota"), R["pos"][:, 0:1], None, ALU.is_equal))
                    dve.scalar_tensor_tensor(out=sel_g[t], in0=c("iota"), scalar=R["pos"][:, 1:2], in1=sel_g[t],
                                             op0=ALU.is_equal, op1=ALU.add).then_inc(sel_ready, 1)
                for t in range(TT):
                    R = rt_of(t)
                    link(dve.tensor_scalar(sel_w[t], c("iota"), R["pos"][:, 0:1], R["w"][:, 0:1], ALU.is_equal, ALU.mult))
                    link(dve.tensor_scalar(R["tmp"], c("iota"), R["pos"][:, 1:2], R["w"][:, 1:2], ALU.is_equal, ALU.mult))
                    dve.tensor_tensor(sel_w[t], sel_w[t], R["tmp"], ALU.add).then_inc(sel_ready, 1)
                for k in range(1, KD, 2):
                    dve.wait_ge(ga_done, k + 1)
                    dve.tensor_scalar(xg[:, k, 0:PAIRS], gather_ps(k)[:, :], g2[:, k:k + 1], None, ALU.mult).then_inc(xg_ready_v, 1)
                dve.wait_ge(xg_ready_a, KD // 2)
                dve.wait_ge(xg_ready_v, KD // 2)
                dve.wait_ge(pads_ready, 1)
                for e in range(SLOTS):
                    window_tokens(dve, FAST, e, e % 2, e, 0)
                    if e >= 1:
                        window_hidden(dve, FAST, e - 1, (e - 1) % 2)
                        window_hiddenT(dve, FAST, e - 1, (e - 1) % 2)
                with dve.Fori(1, EXPERTS // SLOTS) as i:
                    for r in range(SLOTS):
                        e = i * SLOTS + r
                        window_tokens(dve, FAST, e, r % 2, e, 0)
                        window_hidden(dve, FAST, e - 1, (r - 1) % 2)
                        window_hiddenT(dve, FAST, e - 1, (r - 1) % 2)
                window_hidden(dve, FAST, EXPERTS - 1, 1)
                window_hiddenT(dve, FAST, EXPERTS - 1, 1)
                with general_path(dve):
                    dve.wait_ge(FAST["down_done"], EXPERTS)

                    def expert(e):
                        for j in range(WINDOWS):
                            n = e * WINDOWS + j
                            window_tokens(dve, GENERAL, n, j % 2, e, j)
                            window_hidden(dve, GENERAL, n, j % 2)
                            window_hiddenT(dve, GENERAL, n, j % 2)

                    every_expert(dve, expert)
                for g in range(4):
                    t, half = g // 2, g % 2
                    dve.wait_ge(out_done, g + 1)
                    o = xs[:, t, 512 * half:512 * half + 512]
                    dve.tensor_tensor(o, final_ps[g][:, :], o, ALU.add).then_inc(out_ready, 1)

            @block.tensor
            def _(pe):
                pe.wait_ge(const_in, 16)
                pe.wait_ge(params_in, 16 * 7)
                pe.transpose(sum_ps[:, 0:52], small[0:52, :], c("ident", 52)[:, 0:52]).then_inc(par_ps, 1)
                pe.wait_ge(xn_done, TT)
                for k in range(KD):
                    for t in range(TT):
                        ins = pe.transpose(xT_ps(k)[:, P * t:P * t + P], work[:, 2048 + 1024 * t + P * k:2048 + 1024 * t + P * k + P], ident)
                    ins.then_inc(xT_done, 1)

                def unit_steps(i):
                    u = unit_in_slot(i, 0)
                    if u is not None:
                        br, h = UNITS[u]
                        if u >= 1:
                            pe.wait_ge(sc_read, u)
                        if br in "BC":
                            pe.wait_ge(qk_ready, 4 if br == "C" else 8)
                            pairs = ([(0, score_ps[0], "cq", "ck", h), (64, score_ps[1], "cq", "ck", h)] if br == "C"
                                     else [(64 * (h % 2), score_ps[u % 2], "bq", "bk", h // 2)])
                            dk = 64
                        else:
                            pe.wait_ge(conv_ready, 4)
                            pe.wait_ge(ig_v_step, 9)
                            pairs = [(0, score_ps[0], "aq", "ak", h)]
                            dk = P
                        for r0, ps, qn, kn, ch in pairs:
                            q, k = qk[r0:r0 + dk, QK[qn] + ch, :], qk[r0:r0 + dk, QK[kn] + ch, :]
                            pe.matmul(ps[:, 0:128], q[:, 0:128], k[:, 0:128], start=True, stop=True)
                            ins = pe.matmul(ps[:, 128:384], q[:, 128:256], k[:, 0:256], start=True, stop=True)
                        if br == "A":
                            for t in range(TT):
                                ins = pe.matmul(score_ps[1][:, P * t:P * t + P], src[:, 4 * t + h:4 * t + h + 1].to_broadcast([P, P]),
                                                ident, start=True, stop=True)
                        ins.then_inc(sc_done, 1)
                    u = unit_in_slot(i, 1)
                    if u is not None:
                        pe.wait_ge(p_ready, u + 1)
                        if u >= 1:
                            pe.wait_ge(pt_ready, u)
                        S = (S1 if UNITS[u][0] == "B" else S2)[u % 2]
                        for j in range(3):
                            ins = pe.transpose(turn_ps[:, P * j:P * j + P], S[:, P * j:P * j + P], ident)
                        ins.then_inc(tp_done, 1)
                    u = unit_in_slot(i, 2)
                    if u is not None:
                        br, h = UNITS[u]
                        pe.wait_ge(pt_ready, u + 1)
                        if u >= 1:
                            pe.wait_ge(hx_ready, u)
                        name, dv = dict(A=("av", 128), B=("bv", 64), C=("cv", 128))[br]
                        if h == 0:
                            wait_values(pe, name)
                        v = vals[:, VAL[name], :, dv * h:dv * h + dv]
                        pe.matmul(value_ps[:, 0:dv], PT[0][:, 0:128], v[:, 0, :], start=True, stop=True)
                        pe.matmul(value_ps[:, dv:2 * dv], PT[0][:, 128:256], v[:, 0, :], start=True, stop=False)
                        pe.matmul(value_ps[:, dv:2 * dv], PT[0][:, 256:384], v[:, 1, :], start=False, stop=True).then_inc(pv_done, 1)
                    u = unit_in_slot(i, 3)
                    if u is not None and u in turned:
                        nx = turned.index(u)
                        pe.wait_ge(hx_ready, u + 1)
                        if nx >= 1:
                            pe.wait_ge(branch_ready, nx)
                        for t in range(TT):
                            ins = pe.transpose(outT_ps[:, P * t:P * t + P], hx[nx % 2][:, t, :], ident)
                        ins.then_inc(xt_done, 1)

                def head_sums(i):
                    if i >= 1 and i - 1 in norm_pieces:
                        j = norm_pieces.index(i - 1)
                        pe.wait_ge(sq_ready, j + 1)
                        if j >= 1:
                            pe.wait_ge(rs_ready, j)
                        else:
                            pe.wait_ge(par_ready, 1)
                        pe.matmul(sum_ps[:, :], c("blocks"), sq[j % 2], start=True, stop=True).then_inc(ss_done, 1)

                for i in range(NP + DRAIN + 1):
                    if i == 3:
                        pe.wait_ge(lead_in, LEAD)
                        for j in range(3):
                            ins = pe.matmul(outT_ps[:, 4 * j:4 * j + 4], t5hot[0:T5_BUCKETS, P * j:P * j + P], t5[:, :], start=True, stop=True)
                        ins.then_inc(t5_ps, 1)
                    if i == IG + 3:
                        pe.wait_ge(ig_v_step, 8)
                    unit_steps(i)
                    if i < NP:
                        kind, name, n = PIECES[i]
                        ps = piece_ps[i % 2]
                        if i >= 2:
                            pe.wait_ge(bank_free[i % 2], freed(i - 2))
                        if i == 0:
                            pe.wait_ge(hT_ready, KD)
                        b = piece_block[i]
                        if b is not None:
                            if i == 0:
                                pe.wait_ge(half_in, 16)
                            else:
                                pe.wait_ge(block_in[b % 2], 16 * (b // 2 + 1))
                            w = block_sb(b, KD)
                        if kind == "igate":
                            for t in range(TT):
                                for k in range(KD):
                                    ins = pe.matmul(ps[:, 8 * t:8 * t + 8], hT[:, k, P * t:P * t + P], w_if[:, k, :],
                                                    start=(k == 0), stop=(k == KD - 1))
                        elif kind == "value":
                            for k in range(KD):
                                if k == KD // 2:
                                    head_sums(i)
                                ins = pe.matmul(ps[:, :], hT[:, k, P * n:P * n + P], w[:, k, :], start=(k == 0), stop=(k == KD - 1))
                        else:
                            for half in range(2):
                                if half:
                                    head_sums(i)
                                ch = 2 * (n % 2) + half
                                for k in range(KD):
                                    ins = pe.matmul(ps[:, SEQ * half:SEQ * half + SEQ], w[:, k, P * ch:P * ch + P], hT[:, k, :],
                                                    start=(k == 0), stop=(k == KD - 1))
                        ins.then_inc(piece_done, 1)

                    if i == IG + 2:
                        pe.wait_ge(ig_v_step, 7)
                        pe.wait_ge(t5v_ready, 1)
                        pe.matmul(outT_ps[:, 0:4], c("tri"), lf[:, 0:4], start=True, stop=True)
                        pe.matmul(outT_ps[:, 4:8], ones, lf[:, 0:4], start=True, stop=False)
                        pe.matmul(outT_ps[:, 4:8], c("tri"), lf[:, 4:8], start=False, stop=True).then_inc(ig_p_step, 1)

                for j in range(12):
                    i, b = NP + j, n_in + j // 4
                    pe.wait_ge(bank_free[i % 2], freed(i - 2)) if j < 2 else pe.wait_ge(zg_ready, j - 1)
                    pe.wait_ge(block_in[b % 2], 16 * (b // 2 + 1))
                    if j % 4 == 0:
                        pe.wait_ge(branch_ready, {0: 4, 4: 8, 8: 12}[j])
                    w = block_sb(b, 4)
                    for half in range(2):
                        ch = 2 * (j % 4) + half
                        for k in range(4):
                            ins = pe.matmul(piece_ps[i % 2][:, SEQ * half:SEQ * half + SEQ], w[:, k, P * ch:P * ch + P],
                                            branchT[:, BRANCH_ORDER[j // 4], k, :], start=(k == 0), stop=(k == 3))
                    ins.then_inc(piece_done, 1)
                pe.wait_ge(y_ready, 8)
                for j in range(4):
                    i, t, half = NP + 12 + j, j // 2, j % 2
                    b = n_in + 3 + half
                    pe.wait_ge(zg_ready, 11 + j) if j < 2 else pe.wait_ge(x1_ready, j - 1)
                    pe.wait_ge(block_in[b % 2], 16 * (b // 2 + 1))
                    w = block_sb(b, KD)
                    for k in range(KD):
                        ins = pe.matmul(piece_ps[i % 2][:, :], yT[:, k, P * t:P * t + P], w[:, k, :], start=(k == 0), stop=(k == KD - 1))
                    ins.then_inc(piece_done, 1)
                for t in range(TT):
                    pe.wait_ge(xh_ready, t + 1)
                    for half in range(2):
                        ps = [score_ps[0], score_ps[1], turn_ps, value_ps][2 * t + half]
                        for k in range(4 * half, 4 * half + 4):
                            ins = pe.transpose(ps[:, P * (k % 4):P * (k % 4) + P], xhat[:, t, k:D:KD], ident)
                        ins.then_inc(th_done, 1)
                pe.wait_ge(x1_ready, 4)
                pe.wait_ge(branch_ready, 12)
                for t in range(TT):
                    pe.wait_ge(tT_ready, 2 * t + 2)
                    for k in range(KD):
                        ins = pe.matmul(logit_ps[t][:, 0:GROUPS + EXPERTS], tT[:, k, P * t:P * t + P], w_rt[:, k, :],
                                        start=(k == 0), stop=(k == KD - 1))
                    ins.then_inc(lg_done, 1)
                R0, R1 = rt_of(0), rt_of(1)
                pe.wait_ge(hot_ready, 6)
                pe.wait_ge(branch_ready, 12)
                o = outT_ps[:, 0:EXPERTS]
                pe.matmul(o, ones, R0["bef"], start=True, stop=False)
                pe.matmul(o, ones, R1["bef"], start=False, stop=False)
                pe.matmul(o, c("strict"), R0["hot"], start=False, stop=True)
                o = outT_ps[:, EXPERTS:2 * EXPERTS]
                pe.matmul(o, ones, R0["bef"], start=True, stop=False)
                pe.matmul(o, ones, R1["bef"], start=False, stop=False)
                pe.matmul(o, ones, R0["hot"], start=False, stop=False)
                pe.matmul(o, c("strict"), R1["hot"], start=False, stop=True)
                for j, key in enumerate(("bef", "hot")):
                    o = outT_ps[:, 64 + 32 * j:96 + 32 * j]
                    pe.matmul(o, ones, R0[key], start=True, stop=False)
                    ins = pe.matmul(o, ones, R1[key], start=False, stop=True)
                ins.then_inc(pos_done, 1)
                for k in range(KD):
                    if k == 0:
                        pe.wait_ge(sel_ready, TT)
                    if k >= 3:
                        pe.wait_ge(xg_ready_v if (k - 3) % 2 else xg_ready_a, (k - 3) // 2 + 1)
                    for t in range(TT):
                        ins = pe.matmul(gather_ps(k)[:, :], xhat[:, t, k:D:KD], sel_g[t], start=(t == 0), stop=(t == TT - 1))
                    ins.then_inc(ga_done, 1)
                pe.wait_ge(offs_ready, 1)
                for t in range(TT):
                    pe.wait_ge(sel_ready, TT + t + 1)
                    if t:
                        pe.wait_ge(selT_ready, t)
                    for s in range(4):
                        ins = pe.transpose(outT_ps[:, P * s:P * s + P], sel_w[t][:, P * s:P * s + P], ident)
                    ins.then_inc(selT_done, 1)
                pe.wait_ge(xg_ready_a, KD // 2)
                pe.wait_ge(xg_ready_v, KD // 2)
                for e in range(SLOTS):
                    pe.wait_ge(exp_in[e], 48)
                    window_up(pe, FAST, e, e % 2, e)
                    if e >= 1:
                        window_turn_hidden(pe, FAST, e - 1, (e - 1) % 2)
                    if e >= 2:
                        window_turn_result(pe, FAST, e - 2, e % 2)
                    if e >= 1:
                        window_down(pe, FAST, e - 1, (e - 1) % 2, e - 1)
                with pe.Fori(1, EXPERTS // SLOTS) as i:
                    for r in range(SLOTS):
                        e = i * SLOTS + r
                        pe.wait_ge(exp_in[r], (i + 1) * 48)
                        window_up(pe, FAST, e, r % 2, r)
                        window_turn_hidden(pe, FAST, e - 1, (r - 1) % 2)
                        window_turn_result(pe, FAST, e - 2, r % 2)
                        window_down(pe, FAST, e - 1, (r - 1) % 2, (r - 1) % SLOTS)
                last = EXPERTS - 1
                window_turn_hidden(pe, FAST, last, 1)
                window_turn_result(pe, FAST, last - 1, 0)
                window_down(pe, FAST, last, 1, SLOTS - 1)
                window_turn_result(pe, FAST, last, 1)
                with general_path(pe):
                    pe.wait_ge(FAST["yg_done"], EXPERTS)

                    def expert(e):
                        pe.wait_ge(general_in, (e + 1) * 48)
                        for j in range(WINDOWS):
                            n = e * WINDOWS + j
                            window_up(pe, GENERAL, n, j % 2, 0)
                            window_turn_hidden(pe, GENERAL, n, j % 2)
                            window_down(pe, GENERAL, n, j % 2, 0)
                            window_turn_result(pe, GENERAL, n, j % 2)

                    every_expert(pe, expert)
                pe.wait_ge(yg_ready, 1)
                for g in range(8):
                    s, half = g // 2, g % 2
                    if g >= 2:
                        pe.wait_ge(yrow_ready, g - 1)
                    for k in range(4):
                        ins = pe.transpose(piece_ps[g % 2][:, P * k:P * k + P], yg[:, 4 * half + k, P * s:P * s + P], ident)
                    ins.then_inc(yturn_done, 1)
                pe.wait_ge(yrow_ready, 8)
                for g in range(4):
                    t, half = g // 2, g % 2
                    for s in range(4):
                        ins = pe.matmul(final_ps[g][:, :], selT[:, s, P * t:P * t + P], yrows[:, s, 512 * half:512 * half + 512],
                                        start=(s == 0), stop=(s == 3))
                    ins.then_inc(out_done, 1)



_INS = ['x', 'norm1_g', 'w_in', 'a_conv_w', 'a_conv_b', 'a_gate_bias', 'a_out_norm_g', 'b_qk_norm_g', 'b_rel_bias',
        'c_qk_norm_g', 'c_lambda', 'c_sub_norm_g', 't5_bias', 'w_branch', 'w_out', 'norm2_g', 'w_group', 'b_group',
        'w_router', 'b_router', 'w_e_gate', 'w_e_up', 'w_e_down']


def kernel(**inputs):
    import numpy as _np
    import concourse.bacc as _bacc
    from concourse import mybir as _mybir
    from concourse.bass_utils import run_bass_kernel_spmd as _run

    nc = _bacc.Bacc("TRN2", target_bir_lowering=False, num_devices=1)
    arrays, args = {}, []
    for name in _INS:
        a = _np.ascontiguousarray(inputs[name])
        arrays[f"in_{name}_dram"] = a
        args.append(nc.dram_tensor(f"in_{name}_dram", a.shape, _mybir.dt.from_np(a.dtype), kind="ExternalInput").ap())
    arrays["constants_dram"] = constants()
    consts = nc.dram_tensor("constants_dram", (P, CONST_WIDTH), F32, kind="ExternalInput").ap()
    scratch = nc.dram_tensor("t5_by_position", (3 * P * C_HEADS,), F32, kind="Internal").ap()
    out = nc.dram_tensor("out_0_dram", (1, SEQ, D), F32, kind="ExternalOutput").ap()
    build_hybrid_layer(nc, *args, consts, scratch, out)
    r = _run(nc, [arrays], core_ids=[0])
    return r.results[0]["out_0_dram"]
```

```python
from contextlib import ExitStack

import concourse.bass as bass
from concourse import mybir

F32 = mybir.dt.float32
I32 = mybir.dt.int32
ALU = mybir.AluOpType
ACT = mybir.ActivationFunctionType
AX_X = mybir.AxisListType.X
LN_EXP_SET, SIGMOID_SET = "natural_log_exp_and_others", "sigmoid_and_others"

P = 128
SEQ, D = 256, 1024
TT = SEQ // P
KD = D // P
CHUNK = 64
EPS = 1e-6
NEG = -1e30
LOWEST = -3e38
A_HEADS, A_DH = 4, 128
B_HEADS, B_DH = 8, 64
C_HEADS, C_DQK, C_DV = 4, 64, 128
B_MAX_REL = 256
T5_BUCKETS, T5_MAX_DIST = 32, 1024
GATE_CAP = 15.0
LAM_INIT = 0.2
WIDTH = 512
GROUPS, PER_GROUP, EXPERTS, D_EXPERT = 4, 8, 32, 256
FC = D_EXPERT // P
PAIRS = 2 * SEQ
TWIN = 32
WIN = TT * TWIN
LIMIT = TWIN
WINDOWS = -(-P // TWIN)
COLS = PAIRS + TWIN
SLOTS = 6
TURNS = SLOTS // 2
PASSES = EXPERTS // 2
EXPERT_FLOATS = 3 * KD * D_EXPERT

COL = dict(aq=0, ak=512, av=1024, ao=1536, aif=2048, bq=2056, bk=2568, bv=3080,
           cq=3592, ck=4104, cv=4616, g=5128)

CONST = {}
_at = 0
for _name, _width in (("ident", 128), ("ones", 128), ("tri", 128), ("strict", 128), ("blocks", 128), ("eps", 1),
                      ("mask_chunk", 256), ("mask_tri", 256), ("iota", PAIRS), ("pri", EXPERTS),
                      ("prig", GROUPS), ("t5hot", 384)):
    CONST[_name] = (_at, _at + _width)
    _at += _width
CONST_WIDTH = _at
KEPT = CONST["t5hot"][0]


def constants():
    import math

    import numpy as np

    c = np.zeros((P, CONST_WIDTH), np.float32)

    def put(name, value):
        a, b = CONST[name]
        c[:, a:b] = value

    i, j = np.arange(P)[:, None], np.arange(P)[None, :]
    put("ident", i == j)
    put("ones", 1.0)
    put("tri", i <= j)
    put("strict", i < j)
    put("blocks", i // 64 == j // 64)
    zero = np.zeros((P, P))
    put("mask_chunk", np.concatenate([zero, np.where(j // CHUNK <= i // CHUNK, 0.0, NEG)], 1))
    put("mask_tri", np.concatenate([zero, np.where(j <= i, 0.0, NEG)], 1))
    put("iota", np.arange(PAIRS)[None, :])
    put("pri", EXPERTS - np.arange(EXPERTS)[None, :])
    put("prig", GROUPS - np.arange(GROUPS)[None, :])
    put("eps", EPS)
    rel = 127 - np.arange(384)
    nb = T5_BUCKETS // 2
    exact = nb // 2
    n = np.abs(rel)
    f = np.float32
    large = exact + (np.log(np.maximum(n, exact).astype(f) / f(exact)) / f(math.log(T5_MAX_DIST / exact))
                     * f(nb - exact)).astype(np.int32)
    bucket = (rel > 0) * nb + np.where(n < exact, n, np.minimum(large, nb - 1))
    put("t5hot", 0.0)
    a, b = CONST["t5hot"]
    c[:T5_BUCKETS, a:b] = bucket[None, :] == np.arange(T5_BUCKETS)[:, None]
    return c


PIECES = []
for _kind, _name in (("conv", "aq"), ("conv", "ak"), ("value", "ao"), ("value", "av"), ("norm", "cq"),
                     ("norm", "ck"), ("value", "cv"), ("norm", "bq"), ("norm", "bk"), ("value", "bv")):
    for _half in range(2):
        PIECES.append((_kind, _name, _half))
    if _name == "ao":
        PIECES.append(("igate", "aif", 0))
for _g in range(12):
    PIECES.append(("gate", "g", _g))
NP = len(PIECES)

UNITS = [("A", h) for h in range(A_HEADS)] + [("C", h) for h in range(C_HEADS)] + [("B", h) for h in range(B_HEADS)]
NU = len(UNITS)
U0 = 12
SIG_SLOT = U0 + NU
DRAIN = 3


def build_hybrid_layer(nc, x, norm1_g, w_in, a_conv_w, a_conv_b, a_gate_bias, a_out_norm_g,
                       b_qk_norm_g, b_rel_bias, c_qk_norm_g, c_lambda, c_sub_norm_g, t5_bias,
                       w_branch, w_out, norm2_g, w_group, b_group, w_router, b_router,
                       w_e_gate, w_e_up, w_e_down, consts, scratch, out):
    ctx = ExitStack()
    with ctx:
        def sb(name, shape, dt=F32):
            return ctx.enter_context(nc.sbuf_tensor(name, shape, dt))

        def sem(name):
            return ctx.enter_context(nc.semaphore(name))

        xs = sb("xs", [P, TT, D])
        mid = sb("mid", [P, 2 * KD * SEQ + 3 * 4 * SEQ + 1024])
        cst = sb("cst", [P, KEPT])
        early = sb("early", [P, 2 * EXPERT_FLOATS])
        gates = sb("gates", [P, EXPERT_FLOATS])
        expert0 = sb("expert0", [P, EXPERT_FLOATS])
        stream = sb("stream", [P, 2 * 4096 + TT * WIDTH])
        small = sb("small", [64, P])
        par = sb("par", [P, 64])
        bc_norm = sb("bc_norm", [P, WIDTH + C_DV])
        bc_small = sb("bc_small", [P, 8 + 4 + EXPERTS])
        w_if = sb("w_if", [P, KD, 8])
        w_rt = sb("w_rt", [P, KD, GROUPS + EXPERTS])
        g2 = sb("g2", [P, KD])
        t5 = sb("t5", [T5_BUCKETS, C_HEADS])
        t5v = sb("t5v", [P, 3, C_HEADS])
        work = sb("work", [P, 4608])
        pair_key, rel = sb("pair_key", [P, 2 * TT]), sb("rel", [P, 2 * TT])
        st = sb("st", [P, 256])
        offs_i = sb("offs_i", [1, TT * EXPERTS * WINDOWS + TT], I32)
        offs_f = sb("offs_f", [1, TT * EXPERTS * WINDOWS + TT])

        def c(name, rows=P):
            a, b = CONST[name]
            return cst[0:rows, a:b]

        ident, ones = c("ident"), c("ones")
        eps = c("eps")

        t5hot = early[:, 0:384]
        lam_in = early[:, 384:384 + 4 * C_DQK].rearrange("p (a b) -> p a b", b=C_DQK)
        qk = early[:, 0:24 * SEQ].rearrange("p (n t) -> p n t", t=SEQ)
        QK = dict(cq=0, ck=4, bq=8, bk=12, aq=16, ak=20)
        vals = early[:, 24 * SEQ:24 * SEQ + 3 * TT * WIDTH].rearrange("p (n t c) -> p n t c", n=3, t=TT)
        VAL = dict(cv=0, bv=1, av=2)
        bias = early[:, 9216:9216 + 12 * SEQ].rearrange("p (h k) -> p h k", k=SEQ)
        slots_w = [stream[:, n * 4096:(n + 1) * 4096] for n in range(2)]
        out_gate = stream[:, 8192:8192 + TT * WIDTH].rearrange("p (t c) -> p t c", t=TT)
        rel_raw = gates[:, 0:2048].rearrange("p (k h) -> p k h", h=B_HEADS)
        t5_raw = gates[:, 2048:3072].rearrange("p (k h) -> p k h", h=C_HEADS)
        xg = stream[:, 4096:4096 + KD * COLS].rearrange("p (k n) -> p k n", n=COLS)

        sq = [work[:, 512 * n:512 * n + 512] for n in range(2)]
        ug = [work[:, 1024 + 512 * n:1536 + 512 * n] for n in range(2)]
        ug_pair = work[:, 1024:2048]
        hT = mid[:, 0:2048].rearrange("p (k t) -> p k t", t=SEQ)
        branchT = mid[:, 2048:5120].rearrange("p (b c t) -> p b c t", b=3, c=4)
        rs_w = [mid[:, 5120 + 512 * n:5632 + 512 * n] for n in range(2)]
        yT = mid[:, 6144:8192].rearrange("p (k t) -> p k t", t=SEQ)
        S1 = [work[:, 2048 + 384 * n:2432 + 384 * n] for n in range(2)]
        S2 = [work[:, 2816 + 384 * n:3200 + 384 * n] for n in range(2)]
        PT = [work[:, 3584:3968]]
        hx = [work[:, 3968 + 256 * n:4224 + 256 * n].rearrange("p (t c) -> p t c", t=TT) for n in range(2)]
        squares = work[:, 4480:4608]
        xhat = mid[:, 0:2048].rearrange("p (t d) -> p t d", t=TT)
        tT = yT
        sel_g = [work[:, 512 * n:512 * n + 2 * P] for n in range(TT)]
        rt = work[:, 2048:2816]
        xw = [work[:, 512 * n:512 * n + 512].rearrange("p (k n) -> p k n", n=WIN) for n in range(2)]
        ysb = work[:, 1024:2048]
        hid, eg, hidT, selT = (work[:, at:at + 2 * P] for at in (2816, 3072, 3328, 3584))
        sel_a, sel_b = (work[:, at:at + 2 * P].rearrange("p (t j) -> p t j", t=TT) for at in (3840, 4096))
        result = gates[:, 0:TT * D].rearrange("p (t d) -> p t d", t=TT)
        slot_mem = [expert0[:, :], early[:, 0:EXPERT_FLOATS], early[:, EXPERT_FLOATS:2 * EXPERT_FLOATS],
                    gates[:, :], None, mid[:, 0:EXPERT_FLOATS]]
        gate_up_mem = [m[:, 0:4096] if m is not None else stream[:, 0:4096] for m in slot_mem]
        down_mem = [m[:, 4096:6144] if m is not None else mid[:, 6144:8192] for m in slot_mem]
        w_gate_up = [m.rearrange("p (m k f) -> p m k f", m=2, k=KD) for m in gate_up_mem]
        w_down = [m.rearrange("p (f d) -> p f d", d=D) for m in down_mem]

        def stat(at, n):
            return st[:, at:at + n]

        ss1, rstd1 = stat(0, 2), stat(2, 2)
        ss2, rstd2 = stat(4, 2), stat(6, 2)
        lam_s, lam_e, neg_lam = stat(8, 2), stat(10, 2), stat(12, 1)
        ig_z, ig_e, lf = stat(16, 16), stat(32, 16), stat(48, 8)
        ig_v, cum, src = stat(56, 8), stat(64, 8), stat(72, 8)
        mx = [stat(80 + 32 * n, 4) for n in range(3)]
        nm = [stat(84 + 32 * n, 4) for n in range(3)]
        sm = [stat(88 + 32 * n, 4) for n in range(3)]
        rc = [stat(92 + 32 * n, 4) for n in range(3)]
        nl = [stat(96 + 32 * n, 2) for n in range(3)]
        em = [stat(98 + 32 * n, 2) for n in range(3)]
        ssu = [stat(100 + 32 * n, 2) for n in range(3)]
        rsu = [stat(102 + 32 * n, 2) for n in range(3)]
        rr = [stat(104 + 32 * n, 2) for n in range(3)]
        mm = [stat(106 + 32 * n, 2) for n in range(3)]
        gc08 = bc_norm[:, WIDTH:WIDTH + C_DV]
        ga = bc_norm[:, 0:WIDTH]

        NORM1, CONVW, CONVB, QKG = 0, 8, 40, 48

        def bank(name):
            return ctx.enter_context(nc.psum_tensor(name, [P, 512], F32))

        piece_ps = [bank("piece0"), bank("piece1")]
        sum_ps = bank("sum_ps")
        score_ps = [bank("score0"), bank("score1")]
        turn_ps = bank("turn_ps")
        value_ps = bank("value_ps")
        outT_ps = bank("outT_ps")

        logit_ps = [sum_ps, outT_ps]
        turned_x_ps = [score_ps, [turn_ps, value_ps]]
        pos_ps = score_ps

        x_in = [sem(f"x_in{n}") for n in range(TT)]
        const_in = sem("const_in")
        params_in = sem("params_in")
        last_block_in = sem("last_block_in")
        norm1_in, lead_in, half_in = sem("norm1_in"), sem("lead_in"), sem("half_in")
        rel_in, t5_in = sem("rel_in"), sem("t5_in")
        t5_out = sem("t5_out")
        router_in = sem("router_in")
        block_in = [sem("block_in0"), sem("block_in1")]
        xsq_done, xn_done, xT_done = sem("xsq_done"), sem("xn_done"), sem("xT_done")
        hT_ready = [sem("hT_ready_v"), sem("hT_ready_a")]
        par_ps, par_ready = sem("par_ps"), sem("par_ready")
        t5_ps, t5v_ready = sem("t5_ps"), sem("t5v_ready")
        bias_ready = sem("bias_ready")
        lam_ready = sem("lam_ready")
        piece_done = sem("piece_done")
        bank_free = [sem("bank_free0"), sem("bank_free1")]
        sq_ready, ss_done, rs_ready, qk_ready = sem("sq_ready"), sem("ss_done"), sem("rs_ready"), sem("qk_ready")
        csig_ready, conv_ready = sem("csig_ready"), sem("conv_ready")
        gate_ready, outgate_ready = sem("gate_ready"), sem("outgate_ready")
        ig_v_step, ig_a_step, ig_p_step = sem("ig_v_step"), sem("ig_a_step"), sem("ig_p_step")
        sc_done, mx_ready, ex_done, p_ready = sem("sc_done"), sem("mx_ready"), sem("ex_done"), sem("p_ready")
        sc_read, em_ready = sem("sc_read"), sem("em_ready")
        tp_done, pt_ready, pv_done = sem("tp_done"), sem("pt_ready"), sem("pv_done")
        hn_ready, hx_ready = sem("hn_ready"), sem("hx_ready")
        xt_done, branch_ready = sem("xt_done"), sem("branch_ready")
        zg_ready, y_ready = sem("zg_ready"), sem("y_ready")
        x1_ready = sem("x1_ready")
        xh_step = sem("xh_step")
        xh_ready = sem("xh_ready")
        th_done, tT_ready = sem("th_done"), sem("tT_ready")
        lg_done = sem("lg_done")
        rt_exp = sem("rt_exp")
        wrt_ready = sem("wrt_ready")
        hot_ready, pos_done, sel_ready = sem("hot_ready"), sem("pos_done"), sem("sel_ready")
        offs_ready = sem("offs_ready")
        ga_done, xg_ready_a, xg_ready_v = sem("ga_done"), sem("xg_ready_a"), sem("xg_ready_v")
        pads_ready = sem("pads_ready")
        v_step, a_step = sem("v_step"), sem("a_step")
        gate_in = [sem(f"gate_in{n}") for n in range(TURNS)]
        up_in = [sem(f"up_in{n}") for n in range(TURNS)]
        down_in = [sem(f"down_in{n}") for n in range(TURNS)]
        gate0_done = sem("gate0_done")
        FAST, GENERAL = ({name: sem(f"{path}_{name}") for name in
                          ("out_done", "out_ready", "xw_ready", "up_done", "sig_ready", "step", "hid_ready",
                           "rel_done", "sel_part", "sel_done", "hturn_done", "hturn_read", "sturn_done", "sturn_read",
                           "down_done", "ysb_ready", "comb_done")}
                         for path in ("fast", "general"))
        general_in = sem("general_in")
        rel_ready = sem("rel_ready")
        stored = sem("stored")

        blocks = []
        piece_block = []
        for kind, name, n in PIECES:
            if kind == "igate":
                piece_block.append(None)
            else:
                key = (name, n // 2 if kind == "gate" else 0)
                if key not in blocks:
                    blocks.append(key)
                piece_block.append(blocks.index(key))
        n_in = len(blocks)
        BRANCH_ORDER = (0, 2, 1)
        blocks += [("branch", b) for b in BRANCH_ORDER] + [("out", n) for n in range(2)]

        last_piece = [max(i for i, b in enumerate(piece_block) if b == n) for n in range(n_in)]
        last_piece += [NP + 4 * n + 3 for n in range(3)]

        def block_source(key):
            name, n = key
            if name == "branch":
                return w_branch[0, n].rearrange("(k p) n -> p k n", p=P), 4
            if name == "out":
                return w_out[0].rearrange("(k p) n -> p k n", p=P)[:, :, 512 * n:512 * n + 512], KD
            if name == "g":
                at = COL["g"] + D * BRANCH_ORDER[n // 2] + 512 * (n % 2)
            else:
                at = COL[name]
            return w_in[0].rearrange("(k p) n -> p k n", p=P)[:, :, at:at + 512], KD

        def block_sb(n, k):
            mem = slots_w[n % 2] if n < n_in + 4 else early[:, EXPERT_FLOATS:EXPERT_FLOATS + 4096]
            return mem.rearrange("p (k n) -> p k n", k=k)

        norm_pieces = [i for i, p in enumerate(PIECES) if p[0] == "norm"]
        conv_pieces = [i for i, p in enumerate(PIECES) if p[0] == "conv"]
        gate_pieces = [i for i, p in enumerate(PIECES) if p[0] == "gate"]
        late_gates = [i for i in gate_pieces if i < SIG_SLOT]
        IG = [p[0] for p in PIECES].index("igate")
        turned = [u for u, (br, h) in enumerate(UNITS) if br != "B" or h % 2]
        normed = [u for u, (br, h) in enumerate(UNITS) if br != "B"]

        def freed(i):
            return i // 2 + 1

        def gate_of(g):
            return gates[:, 2 * SEQ * g:2 * SEQ * (g + 1)]

        def piece_of(name, half):
            return next(i for i, p in enumerate(PIECES) if p[1] == name and p[2] == half)

        def unit_in_slot(i, lag):
            u = i - U0 - lag
            return u if 0 <= u < NU else None

        def wait_values(eng, name):
            for half in range(2):
                i = piece_of(name, half)
                eng.wait_ge(bank_free[i % 2], freed(i))

        BR = dict(A=0, B=1, C=2)

        def xT_ps(k):
            return [piece_ps[0], piece_ps[1], score_ps[0], score_ps[1]][k // 2][:, SEQ * (k % 2):SEQ * (k % 2) + SEQ]

        def gather_ps(k):
            return [piece_ps[0], piece_ps[1], turn_ps, value_ps][k // 2][:, SEQ * (k % 2):SEQ * (k % 2) + SEQ]

        def gathered(t, k):
            return xg[:, k, 2 * P * t:2 * P * (t + 1)]

        def rt_of(t):
            at, found = 384 * t, {}
            for name, n in (("lg", GROUPS + EXPERTS), ("gm", 1), ("ngm", 1), ("g4", GROUPS), ("gi", 1), ("el", EXPERTS),
                            ("m", 2), ("i", 2), ("o1", EXPERTS), ("o2", EXPERTS), ("both", 2 * EXPERTS),
                            ("d", 1), ("ge", GROUPS), ("gs", 1), ("e2", 1), ("w", 2), ("pos", 2), ("rank", 2),
                            ("junk", 2 * EXPERTS), ("junk2", 2 * EXPERTS)):
                found[name] = rt[:, at:at + n]
                at += n
            found["bef"], found["hot"] = found["both"][:, 0:EXPERTS], found["both"][:, EXPERTS:]
            return found

        def load_one(eng, e, r, m, done=None):
            eng.dma_start(w_gate_up[r][:, m], (w_e_gate, w_e_up)[m][0, bass.ds(e, 1)]
                          .rearrange("o (p k) f -> p (o k) f", k=KD)).then_inc(done or (gate_in, up_in)[m][r // 2], 16)

        def load_gate_up(eng, e, r, done=None):
            for m in range(2):
                load_one(eng, e, r, m, done)

        def load_down(eng, e, r, done=None):
            done = done or down_in[r // 2]
            eng.dma_start(w_down[r], w_e_down[0, bass.ds(e, 1)].rearrange("o (f p) d -> p (o f) d", p=P)).then_inc(done, 16)

        def load_expert(eng, e, r):
            load_gate_up(eng, e, r)
            load_down(eng, e, r)

        up_ps, side_ps, down_ps = score_ps[0], sum_ps, [score_ps[1], outT_ps]
        acc_ps = [[piece_ps[0], piece_ps[1]], [turn_ps, value_ps]]

        def window(eng, e, j):
            return [eng.value_load(offs_i[0:1, bass.ds(EXPERTS * (WINDOWS * t + j) + e, 1)], min_val=0, max_val=PAIRS)
                    for t in range(TT)]

        def first(m):
            return isinstance(m, int) and m == 0

        def pass_tokens(dve, S, m, windows, offs=None):
            offs = offs or [window(dve, e, j) for e, j in windows]
            if not first(m):
                dve.wait_ge(S["up_done"], m)
            for i in range(2):
                for t in range(TT):
                    dve.tensor_copy(xw[i][:, :, TWIN * t:TWIN * t + TWIN], xg[:, :, bass.ds(offs[i][t], TWIN)]).then_inc(S["xw_ready"], 1)

        def pass_up(pe, S, m, slots, weights=None):
            pe.wait_ge(S["xw_ready"], 2 * TT * m + 2 * TT)
            if not first(m):
                pe.wait_ge(S["hid_ready"], m)
            if weights:
                pe.wait_ge(*weights[0])
                pe.wait_ge(*weights[1])
            for k in range(KD):
                for i in range(2):
                    ins = pe.matmul(up_ps[WIN * i:WIN * i + WIN, :].rearrange("p (m f) -> p m f", m=2),
                                    xw[i][:, k, :], w_gate_up[slots[i]][:, :, k, :], start=(k == 0), stop=(k == KD - 1))
            ins.then_inc(S["up_done"], 1)

        def pass_gate_then_up(pe, S, m, slots, weights):
            pe.wait_ge(S["xw_ready"], 2 * TT * m + 2 * TT)
            if not first(m):
                pe.wait_ge(S["hid_ready"], m)
            for part in range(2):
                pe.wait_ge(*weights[part])
                for k in range(KD):
                    for i in range(2):
                        ins = pe.matmul(up_ps[WIN * i:WIN * i + WIN, D_EXPERT * part:D_EXPERT * (part + 1)],
                                        xw[i][:, k, :], w_gate_up[slots[i]][:, part, k, :], start=(k == 0), stop=(k == KD - 1))
                if part:
                    ins.then_inc(S["up_done"], 1)
                elif first(m):
                    ins.then_inc(gate0_done, 1)

        def pass_sigmoid(act, S, m):
            act.wait_ge(S["up_done"], m + 1)
            if not first(m):
                act.wait_ge(S["hid_ready"], m)
            act.activation(eg, up_ps[:, 0:D_EXPERT], ACT.Sigmoid).then_inc(S["sig_ready"], 1)

        def pass_hidden(dve, S, m):
            dve.wait_ge(S["sig_ready"], m + 1)
            dve.tensor_tensor(eg, up_ps[:, 0:D_EXPERT], eg, ALU.mult).then_inc(S["step"], 1)
            dve.wait_ge(S["step"], m + 1)
            if not first(m):
                dve.wait_ge(S["hturn_done"], m)
            dve.tensor_tensor(hid, up_ps[:, D_EXPERT:2 * D_EXPERT], eg, ALU.mult).then_inc(S["hid_ready"], 1)

        def pass_select(dve, S, m, apart, step):
            if not first(m):
                dve.wait_ge(S["sel_part"], 4 * m)
                dve.tensor_scalar(rel[:, :], rel[:, :], -float(step), None, ALU.add).then_inc(S["rel_done"], 1)
                dve.wait_ge(S["rel_done"], m)
                dve.wait_ge(S["sturn_done"], m)
                dve.wait_ge(S["sel_done"], 2 * m)
            slots = c("iota")[:, 0:2 * apart].rearrange("p (i n) -> p i n", i=2)[:, :, 0:TWIN]

            def own(sel, t):
                return sel[:, t, :].rearrange("p (i n) -> p i n", i=2)[:, :, TWIN * t:TWIN * t + TWIN]

            for t in range(TT):
                for j, sel in enumerate((sel_a, sel_b)):
                    dve.tensor_scalar(own(sel, t), slots, rel[:, 2 * t + j:2 * t + j + 1],
                                      rt_of(t)["w"][:, j:j + 1], ALU.is_equal, ALU.mult).then_inc(S["sel_part"], 1)
            for t in range(TT):
                dve.wait_ge(S["sel_part"], 4 * m + 2 * t + 2)
                dve.tensor_tensor(own(sel_a, t), own(sel_a, t), own(sel_b, t), ALU.add).then_inc(S["sel_done"], 1)

        def pass_turn_hidden(pe, S, m):
            pe.wait_ge(S["hid_ready"], m + 1)
            if not first(m):
                pe.wait_ge(S["sturn_read"], m)
            for f in range(FC):
                ins = pe.transpose(side_ps[:, P * f:P * f + P], hid[:, P * f:P * f + P], ident)
            ins.then_inc(S["hturn_done"], 1)

        def pass_hiddenT(dve, S, m):
            dve.wait_ge(S["hturn_done"], m + 1)
            if not first(m):
                dve.wait_ge(S["down_done"], 2 * m)
            dve.tensor_copy(hidT, side_ps[:, 0:2 * P]).then_inc(S["hturn_read"], 1)

        def pass_turn_select(pe, S, m):
            pe.wait_ge(S["sel_done"], 2 * m + 2)
            pe.wait_ge(S["hturn_read"], m + 1)
            for t in range(TT):
                ins = pe.transpose(side_ps[:, P * t:P * t + P], sel_a[:, t, :], ident)
            ins.then_inc(S["sturn_done"], 1)

        def pass_selectT(dve, S, m):
            dve.wait_ge(S["sturn_done"], m + 1)
            if not first(m):
                dve.wait_ge(S["comb_done"], m)
            dve.tensor_copy(selT, side_ps[:, 0:2 * P]).then_inc(S["sturn_read"], 1)

        def pass_down(pe, S, m, slots):
            pe.wait_ge(S["hturn_read"], m + 1)
            if not first(m):
                pe.wait_ge(S["ysb_ready"], 2 * m)
            for half in range(2):
                for f in range(FC):
                    for i in range(2):
                        ins = pe.matmul(down_ps[half][WIN * i:WIN * i + WIN, :], hidT[:, P * f + WIN * i:P * f + WIN * i + WIN],
                                        w_down[slots[i]][:, f, 512 * half:512 * half + 512], start=(f == 0), stop=(f == FC - 1))
                ins.then_inc(S["down_done"], 1)

        def pass_result(act, S, m):
            if not first(m):
                act.wait_ge(S["comb_done"], m)
            for half in range(2):
                act.wait_ge(S["down_done"], 2 * m + half + 1)
                act.copy(ysb[:, 512 * half:512 * half + 512], down_ps[half][:, :]).then_inc(S["ysb_ready"], 1)

        def pass_combine(pe, S, m, t):
            pe.wait_ge(S["ysb_ready"], 2 * m + 2)
            pe.wait_ge(S["sturn_read"], m + 1)
            for half in range(2):
                ins = pe.matmul(acc_ps[t][half][:, :], selT[:, P * t:P * t + P], ysb[:, 512 * half:512 * half + 512],
                                start=first(m), stop=False)
            if t == TT - 1:
                ins.then_inc(S["comb_done"], 1)

        def last_combine(pe, S, m):
            pe.wait_ge(S["sturn_read"], m + 1)
            for half in range(2):
                pe.wait_ge(S["ysb_ready"], 2 * m + half + 1)
                for t in range(TT):
                    pe.matmul(acc_ps[t][half][:, :], selT[:, P * t:P * t + P], ysb[:, 512 * half:512 * half + 512],
                              start=False, stop=True).then_inc(S["out_done"], 1)

        def results(dve, S):
            for g in range(4):
                half, t = g // 2, g % 2
                dve.wait_ge(S["out_done"], g + 1)
                dve.tensor_tensor(result[:, t, 512 * half:512 * half + 512], acc_ps[t][half][:, :],
                                  xs[:, t, 512 * half:512 * half + 512], ALU.add).then_inc(S["out_ready"], 1)

        def pe_pass(pe, S, m, slots, before=True, weights=None, up=pass_up):
            up(pe, S, m, slots, weights)
            if before:
                pass_combine(pe, S, m - 1, 0)
            pass_turn_hidden(pe, S, m)
            if before:
                pass_combine(pe, S, m - 1, 1)
            pass_turn_select(pe, S, m)
            if weights:
                pe.wait_ge(*weights[2])
            pass_down(pe, S, m, slots)

        def weights_in(q, n):
            return (gate_in[q], 32 * n), (up_in[q], 32 * n), (down_in[q], 32 * n)

        def dve_pass(dve, S, m, apart, step, next_windows):
            pass_select(dve, S, m, apart, step)
            pass_hidden(dve, S, m)
            pass_hiddenT(dve, S, m)
            if next_windows:
                pass_tokens(dve, S, m + 1, next_windows)
            pass_selectT(dve, S, m)

        def act_pass(act, S, m):
            pass_sigmoid(act, S, m)
            pass_result(act, S, m)

        def experts_of(m):
            return [(2 * m, 0), (2 * m + 1, 0)]

        def general_path(eng):
            at = TT * WINDOWS * EXPERTS
            largest = eng.value_load(offs_i[0:1, at:at + 1], min_val=0, max_val=PAIRS)
            return eng.If(largest > LIMIT)

        LOOPS = PASSES // TURNS
        assert WINDOWS % 2 == 0

        def every_expert(eng, one):
            one(0)
            with eng.Fori(1, EXPERTS - 1) as e:
                one(e)
            one(EXPERTS - 1)

        def load_rest(sp):
            rest_from = CONST["mask_chunk"][0]
            sp.dma_start(t5hot, consts[:, KEPT:]).then_inc(lead_in, 16)
            sp.dma_start(t5[:, :], t5_bias).then_inc(lead_in, 16)
            sp.dma_start(w_if[:, :, :], w_in[0].rearrange("(k p) n -> p k n", p=P)[:, :, COL["aif"]:COL["aif"] + 8]).then_inc(lead_in, 16)
            sp.dma_start(lam_in.rearrange("p a b -> p (a b)"),
                         c_lambda.rearrange("l a b -> (l a b)").partition_broadcast(P)).then_inc(lead_in, 16)
            sp.dma_start(ga, a_out_norm_g.rearrange("l a b -> (l a b)").partition_broadcast(P)).then_inc(lead_in, 16)
            sp.dma_start(gc08, c_sub_norm_g.rearrange("l a -> (l a)").partition_broadcast(P)).then_inc(lead_in, 16)
            sp.dma_start(bc_small[:, 0:8], a_gate_bias.rearrange("l a -> (l a)").partition_broadcast(P)).then_inc(lead_in, 16)
            sp.dma_start(cst[:, rest_from:], consts[:, rest_from:KEPT]).then_inc(lead_in, 16)

        LEAD = 16 * 8

        def load_tables(sp):
            sp.dma_start(rel_raw.rearrange("p k h -> p (k h)"),
                         bass.AP(b_rel_bias.tensor, 129 * B_HEADS, [[B_HEADS, P], [1, SEQ * B_HEADS]])).then_inc(rel_in, 16)
            for dst, src_ap in (
                (bc_small[:, 8:12], b_group.rearrange("l a -> (l a)").partition_broadcast(P)),
                (bc_small[:, 12:44], b_router.rearrange("l a -> (l a)").partition_broadcast(P)),
                (w_rt[:, :, 0:GROUPS], w_group[0].rearrange("(p k) n -> p k n", k=KD)),
                (w_rt[:, :, GROUPS:], w_router[0].rearrange("(p k) n -> p k n", k=KD)),
                (g2[:, :], norm2_g.rearrange("l (p k) -> (l p) k", k=KD)),
            ):
                sp.dma_start(dst, src_ap).then_inc(router_in, 16)

        with nc.Block() as block:
            @block.sync
            def _(sp):
                for t in range(TT):
                    sp.dma_start(xs[:, t, :], x[0, P * t:P * t + P, :]).then_inc(x_in[t], 16)
                for n, key in enumerate(blocks[:-1]):
                    if n >= 2:
                        sp.wait_ge(piece_done, last_piece[n - 2] + 1)
                    src_ap, k = block_source(key)
                    if n == 0:
                        sp.dma_start(block_sb(n, k)[:, :, 0:SEQ], src_ap[:, :, 0:SEQ]).then_inc(half_in, 16)
                        sp.dma_start(block_sb(n, k)[:, :, SEQ:], src_ap[:, :, SEQ:]).then_inc(block_in[n % 2], 16)
                        load_rest(sp)
                        continue
                    sp.dma_start(block_sb(n, k), src_ap).then_inc(block_in[n % 2], 16)
                    if n == 1:
                        load_tables(sp)
                    if n == 3:
                        load_expert(sp, 0, 0)
                    if n == n_in + 2:
                        sp.wait_ge(pv_done, NU)
                        sp.wait_ge(sc_read, NU)
                        src_ap, k = block_source(blocks[-1])
                        sp.dma_start(block_sb(n_in + 4, k), src_ap).then_inc(last_block_in, 16)
                        load_expert(sp, 1, 1)
                load_down(sp, 2, 2)
                sp.wait_ge(zg_ready, 12)
                load_expert(sp, 3, 3)
                load_gate_up(sp, 4, 4)
                load_down(sp, 5, 5)
                load_one(sp, 5, 5, 1)
                sp.wait_ge(x1_ready, 4)
                load_gate_up(sp, 2, 2)
                sp.wait_ge(lg_done, 2)
                load_down(sp, 4, 4)
                sp.wait_ge(ga_done, TT * KD // 2)
                load_one(sp, 5, 5, 0)

                def load_pair(m, before, q):
                    for part in range(2):
                        if first(before) and part == 0:
                            sp.wait_ge(gate0_done, 1)
                        else:
                            sp.wait_ge(FAST["up_done"], before + 1)
                        for half in range(2):
                            load_one(sp, 2 * m + half, 2 * q + half, part)
                    sp.wait_ge(FAST["down_done"], 2 * before + 2)
                    for half in range(2):
                        load_down(sp, 2 * m + half, 2 * q + half)

                for q in range(TURNS):
                    load_pair(TURNS + q, q, q)
                with sp.Fori(2, LOOPS) as i:
                    for q in range(TURNS):
                        load_pair(i * TURNS + q, (i - 1) * TURNS + q, q)
                for m in range(LOOPS * TURNS, PASSES):
                    load_pair(m, m - TURNS, m % TURNS)
                sp.wait_ge(offs_ready, 1)
                with general_path(sp):
                    sp.wait_ge(FAST["down_done"], 2 * PASSES)

                    def load(e):
                        if not first(e):
                            sp.wait_ge(GENERAL["down_done"], 4 * e)
                        load_gate_up(sp, e, 0, general_in)
                        load_down(sp, e, 0, general_in)

                    every_expert(sp, load)
                    sp.wait_ge(GENERAL["out_ready"], 4)
                for g in range(4):
                    half, t = g // 2, g % 2
                    sp.wait_ge(FAST["out_ready"], g + 1)
                    sp.dma_start(out[0, P * t:P * t + P, 512 * half:512 * half + 512],
                                 result[:, t, 512 * half:512 * half + 512]).then_inc(stored, 16)
                sp.wait_ge(stored, 64)

            @block.gpsimd
            def _(pool):
                for i in range(NP + 1):
                    if i >= 1 and i - 1 in norm_pieces:
                        n = norm_pieces.index(i - 1)
                        name, half = PIECES[i - 1][1:]
                        pool.wait_ge(rs_ready, n + 1)
                        pool.wait_ge(bank_free[(i - 1) % 2], freed(i - 1))
                        at = QK[name] + 2 * half
                        pool.tensor_tensor(qk[:, at:at + 2, :].rearrange("p n t -> p (n t)"), ug[n % 2], rs_w[n % 2],
                                           ALU.mult).then_inc(qk_ready, 1)
                    if i >= 1 and i - 1 in conv_pieces:
                        n = conv_pieces.index(i - 1)
                        name, half = PIECES[i - 1][1:]
                        pool.wait_ge(csig_ready, n + 1)
                        at = QK[name] + 2 * half
                        pool.tensor_tensor(qk[:, at:at + 2, :].rearrange("p n t -> p (n t)"), ug[n % 2], rs_w[n % 2],
                                           ALU.mult).then_inc(conv_ready, 1)
                    if i >= 1 and i - 1 < NP and PIECES[i - 1][1] == "ao":
                        g = PIECES[i - 1][2]
                        pool.wait_ge(lead_in, LEAD)
                        pool.wait_ge(bank_free[(i - 1) % 2], freed(i - 1))
                        pool.tensor_tensor(out_gate[:, g, :], out_gate[:, g, :], ga, ALU.mult).then_inc(outgate_ready, 1)
                    if i == IG + 1:
                        pool.wait_ge(lead_in, LEAD)
                        pool.wait_ge(rel_in, 16)
                        for h in range(B_HEADS):
                            pool.tensor_tensor(bias[:, C_HEADS + h, :], rel_raw[:, ::-1, h], c("mask_chunk"), ALU.add).then_inc(bias_ready, 1)
                        pool.wait_ge(t5_in, 16)
                        for h in range(C_HEADS):
                            pool.tensor_tensor(bias[:, h, :], t5_raw[:, ::-1, h], c("mask_chunk"), ALU.add).then_inc(bias_ready, 1)
                for j in range(4, 12):
                    pool.wait_ge(zg_ready, j + 1)
                    if j >= 8:
                        pool.wait_ge(y_ready, j - 7)
                    o = yT[:, 2 * (j % 4):2 * (j % 4) + 2, :].rearrange("p n t -> p (n t)")
                    pool.tensor_tensor(o, o, sq[j % 2], ALU.add).then_inc(y_ready, 1)
                pool.wait_ge(x1_ready, 4)
                pool.memset(xg[:, :, PAIRS:COLS], 0.0).then_inc(pads_ready, 1)
                pool.memset(sel_a, 0.0).then_inc(pads_ready, 1)

            @block.scalar
            def _(act):
                act.preload_act_table_set(LN_EXP_SET)
                act.dma_start(small[NORM1:NORM1 + 8, :], norm1_g.rearrange("l (c p) -> (l c) p", p=P)).then_inc(norm1_in, 16)
                first_part = CONST["mask_chunk"][0]
                act.dma_start(cst[:, 0:first_part], consts[:, 0:first_part]).then_inc(const_in, 16)
                act.dma_start(small[CONVW:CONVW + 32, :], a_conv_w[0].rearrange("w (c p) -> (w c) p", p=P)).then_inc(params_in, 16)
                act.dma_start(small[CONVB:CONVB + 8, :], a_conv_b.rearrange("l (c p) -> (l c) p", p=P)).then_inc(params_in, 16)
                for at, g in ((QKG, b_qk_norm_g), (QKG + 2, c_qk_norm_g)):
                    act.dma_start(small[at:at + 2, :].rearrange("r (h c) -> r h c", h=2),
                                  bass.AP(g.tensor, 0, [[B_DH, 2], [0, 2], [1, B_DH]])).then_inc(params_in, 16)

                for t in range(TT):
                    act.wait_ge(x_in[t], 16)
                    act.activation(work[:, 1024 * t:1024 * t + 1024], xs[:, t, :], ACT.Square, accum_out=ss1[:, t:t + 1]).then_inc(xsq_done, 1)
                    act.wait_ge(xsq_done, t + 1)
                    if t == 0:
                        act.wait_ge(const_in, 16)
                    act.activation(rstd1[:, t:t + 1], ss1[:, t:t + 1], ACT.Ln, bias=eps, scale=1.0 / D).then_inc(a_step, 1)
                    act.wait_ge(a_step, 2 * t + 1)
                    act.activation(rstd1[:, t:t + 1], rstd1[:, t:t + 1], ACT.Exp, scale=-0.5).then_inc(a_step, 1)
                act.wait_ge(par_ps, 1)
                act.copy(par[:, 0:8], sum_ps[:, 0:8]).then_inc(par_ready, 1)
                act.wait_ge(par_ready, 1)
                for k in range(KD // 2, KD):
                    act.wait_ge(xT_done, 2 * (k // 2) + 2)
                    act.activation(hT[:, k, :], xT_ps(k), ACT.Copy, scale=par[:, NORM1 + k:NORM1 + k + 1]).then_inc(hT_ready[1], 1)
                act.wait_ge(par_ps, 2)
                act.copy(par[:, 8:52], sum_ps[:, 8:52]).then_inc(par_ready, 1)
                steps = 2 * TT
                act.preload_act_table_set(SIGMOID_SET)

                for i in range(NP + DRAIN + 1):
                    if i == 3:
                        act.wait_ge(t5_ps, 1)
                        act.copy(t5v[:, :, :].rearrange("p c h -> p (c h)"), outT_ps[:, 0:12]).then_inc(t5v_ready, 1)
                        act.wait_ge(t5v_ready, 1)
                        act.dma_start(scratch.rearrange("(c p h) -> p c h", p=P, h=C_HEADS), t5v[:, :, :]).then_inc(t5_out, 16)
                    if i == 5:
                        act.wait_ge(t5_out, 16)
                        act.dma_start(t5_raw.rearrange("p k h -> p (k h)"),
                                      bass.AP(scratch.tensor, 0, [[C_HEADS, P], [1, SEQ * C_HEADS]])).then_inc(t5_in, 16)
                    if i == IG + 1:
                        act.preload_act_table_set(LN_EXP_SET)
                        act.wait_ge(lam_ready, 2)
                        act.activation(lam_e, lam_s, ACT.Exp).then_inc(lam_ready, 1)
                    if i == SIG_SLOT:
                        act.preload_act_table_set(SIGMOID_SET)
                        for p in late_gates:
                            n = PIECES[p][2]
                            act.wait_ge(bank_free[p % 2], freed(p))
                            act.activation(gate_of(n), gate_of(n), ACT.Sigmoid).then_inc(gate_ready, 1)
                    u = unit_in_slot(i, 1)
                    if u is not None:
                        act.wait_ge(tp_done, u + 1)
                        if u >= 1:
                            act.wait_ge(pv_done, u)
                        act.copy(PT[0], turn_ps[:, 0:384]).then_inc(pt_ready, 1)
                    u = unit_in_slot(i, 2)
                    if u is not None and UNITS[u][0] != "B":
                        par_u, z = u % 2, u % 3
                        act.wait_ge(pv_done, u + 1)
                        if u >= 2:
                            act.wait_ge(hx_ready, u - 1)
                        for t in range(TT):
                            kw = dict(scale=rc[z][:, t:t + 1]) if UNITS[u][0] == "A" else {}
                            act.activation(squares,
                                           value_ps[:, 128 * t:128 * t + 128], ACT.Square,
                                           accum_out=ssu[z][:, t:t + 1], **kw).then_inc(a_step, 1)
                            steps += 1
                            act.wait_ge(a_step, steps)
                        act.activation(rsu[z], ssu[z], ACT.Ln, bias=eps, scale=1.0 / C_DV).then_inc(a_step, 1)
                        steps += 1
                        act.wait_ge(a_step, steps)
                        act.activation(rsu[z], rsu[z], ACT.Exp, scale=-0.5).then_inc(hn_ready, 1)
                    u = unit_in_slot(i, 3)
                    if u is not None and u in turned:
                        br, h = UNITS[u]
                        ch = h // 2 if br == "B" else h
                        act.wait_ge(xt_done, turned.index(u) + 1)
                        act.copy(branchT[:, BR[br], ch, :], outT_ps[:, 0:SEQ]).then_inc(branch_ready, 1)
                    u = unit_in_slot(i, 0)
                    if u is not None:
                        br, h = UNITS[u]
                        par_u, z = u % 2, u % 3
                        act.wait_ge(mx_ready, u + 1)
                        spans = [(0, 128), (128, 384)]
                        todo = []
                        for m, S in enumerate((S1[par_u], S2[par_u]) if br == "C" else (S1[par_u],)):
                            for t, (a, b) in enumerate(spans):
                                todo.append((S[:, a:b], 2 * m + t))
                        for j, (ap, col) in enumerate(todo):
                            kw = {} if br == "A" else dict(accum_out=sm[z][:, col:col + 1])
                            last = act.activation(ap, ap, ACT.Exp, bias=nm[z][:, col:col + 1], **kw)
                        last.then_inc(ex_done, 1)
                        if br == "A":
                            act.activation(em[z], mm[z], ACT.Exp).then_inc(em_ready, 1)
                    if i >= 1 and i - 1 in norm_pieces:
                        j = norm_pieces.index(i - 1)
                        act.wait_ge(ss_done, j + 1)
                        if j >= 2:
                            act.wait_ge(qk_ready, j - 1)
                        else:
                            act.wait_ge(conv_ready, len(conv_pieces))
                        act.activation(rs_w[j % 2], sum_ps[:, :], ACT.Ln, bias=eps, scale=1.0 / B_DH).then_inc(a_step, 1)
                        steps += 1
                        act.wait_ge(a_step, steps)
                        act.activation(rs_w[j % 2], rs_w[j % 2], ACT.Exp, scale=-0.5).then_inc(rs_ready, 1)
                    if i == IG + 1:
                        act.wait_ge(ig_v_step, 3)
                        z3 = ig_z.rearrange("p (t n) -> p t n", t=TT)
                        e3 = ig_e.rearrange("p (t n) -> p t n", t=TT)
                        act.activation(e3[:, :, 0:4], z3[:, :, 0:4], ACT.Exp, scale=2.0 / GATE_CAP).then_inc(ig_a_step, 1)
                        act.activation(e3[:, :, 4:8], e3[:, :, 4:8], ACT.Exp, scale=-1.0).then_inc(ig_a_step, 1)
                        act.wait_ge(ig_a_step, 2)
                        act.activation(e3[:, :, 4:8], e3[:, :, 4:8], ACT.Ln, bias=1.0).then_inc(ig_a_step, 1)
                    if i < NP:
                        kind, name, n = PIECES[i]
                        ps = piece_ps[i % 2]
                        act.wait_ge(piece_done, i + 1)
                        if kind == "norm":
                            j = norm_pieces.index(i)
                            if j >= 2:
                                act.wait_ge(ss_done, j - 1)
                            act.activation(sq[j % 2], ps[:, :], ACT.Square).then_inc(sq_ready, 1)
                        elif kind == "value" and name != "ao":
                            act.copy(vals[:, VAL[name], n, :], ps[:, :]).then_inc(bank_free[i % 2], 1)
                        elif kind == "value":
                            act.activation(out_gate[:, n, :], ps[:, :], ACT.Sigmoid).then_inc(bank_free[i % 2], 1)
                        elif kind == "gate":
                            if n == 0:
                                act.wait_ge(bias_ready, 12)
                            func = ACT.Copy if i in late_gates else ACT.Sigmoid
                            act.activation(gate_of(n), ps[:, :], func).then_inc(bank_free[i % 2], 1)
                    if i < NP and i in conv_pieces:
                        j = conv_pieces.index(i)
                        act.wait_ge(bank_free[i % 2], freed(i))
                        if j >= 2:
                            act.wait_ge(conv_ready, j - 1)
                        act.activation(rs_w[j % 2], ug[j % 2], ACT.Sigmoid).then_inc(csig_ready, 1)

                act.preload_act_table_set(LN_EXP_SET)
                for t in range(TT):
                    act.wait_ge(x1_ready, 2 * t + 2)
                    act.activation(ug_pair, xs[:, t, :], ACT.Square, accum_out=ss2[:, t:t + 1]).then_inc(a_step, 1)
                    steps += 1
                    act.wait_ge(a_step, steps)
                    act.activation(rstd2[:, t:t + 1], ss2[:, t:t + 1], ACT.Ln, bias=eps, scale=1.0 / D).then_inc(a_step, 1)
                    steps += 1
                    act.wait_ge(a_step, steps)
                    act.activation(rstd2[:, t:t + 1], rstd2[:, t:t + 1], ACT.Exp, scale=-0.5).then_inc(xh_step, 1)
                    for half in range(2 - 2 * t):
                        act.wait_ge(th_done, half + 1)
                        act.copy(tT[:, 4 * half:4 * half + 4, 0:P],
                                 turned_x_ps[0][half][:, :].rearrange("p (k n) -> p k n", k=4)).then_inc(tT_ready, 1)
                    if t == 1:
                        act.wait_ge(xh_step, 2)
                        act.activation(xhat[:, 1, :], xs[:, 1, :], ACT.Copy, scale=rstd2[:, 1:2]).then_inc(xh_ready, 1)
                        for k in range(KD):
                            act.wait_ge(ga_done, k // 2 + 1)
                            act.activation(gathered(0, k), gather_ps(k), ACT.Copy, scale=g2[:, k:k + 1]).then_inc(xg_ready_a, 1)
                    R = rt_of(t)
                    act.wait_ge(hot_ready, 3 * t + 1)
                    act.activation(R["ge"], R["lg"][:, 0:GROUPS], ACT.Exp, bias=R["ngm"], accum_out=R["gs"]).then_inc(rt_exp, 1)
                    act.wait_ge(hot_ready, 3 * t + 2)
                    act.activation(R["e2"], R["d"], ACT.Exp).then_inc(rt_exp, 1)
                act.preload_act_table_set(SIGMOID_SET)
                for k in (0, 1, 4, 5, 6, 7):
                    act.wait_ge(ga_done, (KD + k) // 2 + 1)
                    act.activation(gathered(1, k), gather_ps(k), ACT.Copy, scale=g2[:, k:k + 1]).then_inc(xg_ready_a, 1)
                for m in range(TURNS):
                    act_pass(act, FAST, m)
                with act.Fori(1, LOOPS) as i:
                    for q in range(TURNS):
                        act_pass(act, FAST, i * TURNS + q)
                for m in range(LOOPS * TURNS, PASSES):
                    act_pass(act, FAST, m)
                act.wait_ge(offs_ready, 1)
                with general_path(act):
                    act.wait_ge(FAST["out_done"], 4)

                    def expert(e):
                        for j in range(2):
                            act_pass(act, GENERAL, 2 * e + j)

                    every_expert(act, expert)

            @block.vector
            def _(dve):
                steps = 0
                for t in range(TT):
                    dve.wait_ge(a_step, 2 * t + 2)
                    dve.tensor_scalar(work[:, 2048 + 1024 * t:3072 + 1024 * t], xs[:, t, :], rstd1[:, t:t + 1], None,
                                      ALU.mult).then_inc(xn_done, 1)
                dve.wait_ge(par_ready, 1)
                for k in range(KD // 2):
                    dve.wait_ge(xT_done, 2 * (k // 2) + 2)
                    dve.tensor_scalar(hT[:, k, :], xT_ps(k), par[:, NORM1 + k:NORM1 + k + 1], None, ALU.mult).then_inc(hT_ready[0], 1)
                dve.wait_ge(par_ready, 2)
                dve.tensor_scalar(par[:, 54:55], par[:, QKG:QKG + 1], B_DH ** -0.5, None, ALU.mult).then_inc(v_step, 1)
                dve.tensor_scalar(par[:, 55:56], par[:, QKG + 2:QKG + 3], C_DQK ** -0.5, None, ALU.mult).then_inc(v_step, 1)
                steps += 2
                dve.wait_ge(v_step, 2)
                gain = dict(bq=54, cq=55, bk=QKG + 1, ck=QKG + 3)

                for i in range(NP + DRAIN + 1):
                    if i == IG - 1:
                        dve.wait_ge(lead_in, LEAD)
                        for j in range(2):
                            dve.tensor_tensor_reduce(S1[j][:, 0:C_DQK], lam_in[:, 2 * j, :], lam_in[:, 2 * j + 1, :],
                                                     1.0, 0.0, ALU.mult, ALU.add, lam_s[:, j:j + 1]).then_inc(lam_ready, 1)
                    if i == IG + 2:
                        dve.wait_ge(lam_ready, 3)
                        dve.scalar_tensor_tensor(out=neg_lam, in0=lam_e[:, 1:2], scalar=LAM_INIT, in1=lam_e[:, 0:1],
                                                 op0=ALU.subtract, op1=ALU.subtract).then_inc(lam_ready, 1)
                        dve.tensor_scalar(gc08, gc08, 1.0 - LAM_INIT, None, ALU.mult).then_inc(lam_ready, 1)
                    if i == IG + 3:
                        dve.wait_ge(ig_p_step, 1)
                        dve.tensor_copy(cum, outT_ps[:, 0:8]).then_inc(ig_v_step, 1)
                        dve.wait_ge(ig_v_step, 8)
                        dve.tensor_tensor(src, ig_v, cum, ALU.subtract).then_inc(ig_v_step, 1)
                    u = unit_in_slot(i, 0)
                    if u is not None:
                        br, h = UNITS[u]
                        q, z = u % 2, u % 3
                        dve.wait_ge(sc_done, u + 1)
                        if u >= 2:
                            dve.wait_ge(tp_done, u - 1)
                        if br == "C" and h == 0:
                            dve.wait_ge(bias_ready, 12)
                            dve.wait_ge(lam_ready, 5)
                        if br in "BC":
                            hb = h if br == "C" else C_HEADS + h
                            maps = [(S1[q], score_ps[u % 2])] if br == "B" else [(S1[q], score_ps[0]), (S2[q], score_ps[1])]
                            adds = [(S, ps, bias[:, hb, :]) for S, ps in maps]
                        else:
                            adds = [(S1[q], None, c("mask_tri"))]
                        n_mx = 2 * len(adds)
                        for m, (S, ps, bb) in enumerate(adds):
                            for t in range(TT):
                                sa = slice(0, 128) if t == 0 else slice(128, 384)
                                pa = score_ps[1][:, 0:P * (t + 1)] if br == "A" else ps[:, sa]
                                ins = dve.tensor_tensor_reduce(S[:, sa], pa, bb[:, P * (1 - t):SEQ], 1.0, LOWEST,
                                                               ALU.add, ALU.max, mx[z][:, 2 * m + t:2 * m + t + 1])
                                if br != "A" and m == len(adds) - 1 and t == 1:
                                    ins.then_inc(sc_read, 1)
                                else:
                                    ins.then_inc(v_step, 1)
                                    steps += 1
                        dve.wait_ge(v_step, steps)
                        if br != "A":
                            dve.wait_ge(sc_read, u + 1)
                            dve.tensor_scalar(nm[z][:, 0:n_mx], mx[z][:, 0:n_mx], -1.0, None, ALU.mult).then_inc(mx_ready, 1)
                        else:
                            dve.tensor_scalar(nm[z][:, 0:2], mx[z][:, 0:2], 0.0, -1.0, ALU.max, ALU.mult).then_inc(v_step, 1)
                            steps += 1
                            dve.wait_ge(v_step, steps)
                            dve.tensor_tensor(mm[z], nm[z][:, 0:2], cum[:, h:8:4], ALU.subtract).then_inc(mx_ready, 1)
                    u = unit_in_slot(i, 2)
                    if u is not None:
                        br, h = UNITS[u]
                        q, z = u % 2, u % 3
                        dve.wait_ge(pv_done, u + 1)
                        nx = turned.index(u) if u in turned else turned.index(u + 1)
                        if nx >= 2:
                            dve.wait_ge(xt_done, nx - 1)
                        H = hx[nx % 2]
                        if br == "B":
                            for t in range(TT):
                                ins = dve.tensor_scalar(H[:, t, 64 * (h % 2):64 * (h % 2) + 64], value_ps[:, 64 * t:64 * t + 64],
                                                        rc[z][:, t:t + 1], None, ALU.mult)
                                if t:
                                    ins.then_inc(hx_ready, 1)
                                else:
                                    ins.then_inc(v_step, 1)
                                    steps += 1
                                    dve.wait_ge(v_step, steps)
                        else:
                            dve.wait_ge(hn_ready, normed.index(u) + 1)
                            if br == "A":
                                dve.wait_ge(outgate_ready, 2)
                                dve.tensor_tensor(rr[z], rsu[z], rc[z][:, 0:2], ALU.mult).then_inc(v_step, 1)
                                steps += 1
                                dve.wait_ge(v_step, steps)
                            for t in range(TT):
                                sc_ap = (rr if br == "A" else rsu)[z][:, t:t + 1]
                                g_ap = out_gate[:, t, P * h:P * h + P] if br == "A" else gc08
                                ins = dve.scalar_tensor_tensor(out=H[:, t, :], in0=value_ps[:, P * t:P * t + P], scalar=sc_ap, in1=g_ap,
                                                               op0=ALU.mult, op1=ALU.mult)
                                if t:
                                    ins.then_inc(hx_ready, 1)
                                else:
                                    ins.then_inc(v_step, 1)
                                    steps += 1
                                    dve.wait_ge(v_step, steps)
                    u = unit_in_slot(i, 0)
                    if u is not None:
                        br, h = UNITS[u]
                        q, z = u % 2, u % 3
                        dve.wait_ge(ex_done, u + 1)
                        if br != "A":
                            if br == "B":
                                dve.reciprocal(rc[z][:, 0:2], sm[z][:, 0:2]).then_inc(p_ready, 1)
                            else:
                                dve.reciprocal(rc[z][:, 0:4], sm[z][:, 0:4]).then_inc(v_step, 1)
                                steps += 1
                                dve.wait_ge(v_step, steps)
                                dve.tensor_scalar(nl[z], rc[z][:, 2:4], neg_lam, None, ALU.mult).then_inc(v_step, 1)
                                steps += 1
                                dve.wait_ge(v_step, steps)
                                for t in range(TT):
                                    sa = slice(0, 128) if t == 0 else slice(128, 384)
                                    dve.tensor_scalar(S2[q][:, sa], S2[q][:, sa], nl[z][:, t:t + 1], None, ALU.mult).then_inc(v_step, 1)
                                    steps += 1
                                for t in range(TT):
                                    sa = slice(0, 128) if t == 0 else slice(128, 384)
                                    dve.wait_ge(v_step, steps)
                                    dve.scalar_tensor_tensor(out=S2[q][:, sa], in0=S1[q][:, sa], scalar=rc[z][:, t:t + 1],
                                                             in1=S2[q][:, sa], op0=ALU.mult, op1=ALU.add).then_inc(p_ready if t else v_step, 1)
                                    if not t:
                                        steps += 1
                        else:
                            for t in range(TT):
                                sa = slice(0, 128) if t == 0 else slice(128, 384)
                                dve.tensor_tensor_reduce(S2[q][:, sa], score_ps[0][:, sa], S1[q][:, sa], A_DH ** -0.5, 0.0,
                                                         ALU.mult, ALU.add, sm[z][:, t:t + 1]).then_inc(sc_read if t else v_step, 1)
                                if not t:
                                    steps += 1
                            dve.wait_ge(v_step, steps)
                            dve.wait_ge(sc_read, u + 1)
                            dve.wait_ge(em_ready, h + 1)
                            dve.scalar_tensor_tensor(out=rc[z][:, 0:2], in0=sm[z][:, 0:2], scalar=-1.0, in1=sm[z][:, 0:2],
                                                     op0=ALU.mult, op1=ALU.max).then_inc(v_step, 1)
                            steps += 1
                            dve.wait_ge(v_step, steps)
                            dve.tensor_tensor(rc[z][:, 0:2], rc[z][:, 0:2], em[z], ALU.max).then_inc(v_step, 1)
                            steps += 1
                            dve.wait_ge(v_step, steps)
                            dve.reciprocal(rc[z][:, 0:2], rc[z][:, 0:2]).then_inc(p_ready, 1)
                    if i == IG + 2:
                        z3 = ig_z.rearrange("p (t n) -> p t n", t=TT)
                        e3 = ig_e.rearrange("p (t n) -> p t n", t=TT)
                        lf3 = lf.rearrange("p (t n) -> p t n", t=TT)
                        iv3 = ig_v.rearrange("p (t n) -> p t n", t=TT)
                        dve.wait_ge(ig_a_step, 3)
                        dve.tensor_tensor(lf3, z3[:, :, 4:8], e3[:, :, 4:8], ALU.subtract).then_inc(ig_v_step, 1)
                        dve.tensor_scalar(e3[:, :, 0:4], e3[:, :, 0:4], 1.0, None, ALU.add).then_inc(ig_v_step, 1)
                        dve.wait_ge(ig_v_step, 5)
                        dve.reciprocal(e3[:, :, 0:4], e3[:, :, 0:4]).then_inc(ig_v_step, 1)
                        dve.wait_ge(ig_v_step, 6)
                        dve.tensor_scalar(iv3, e3[:, :, 0:4], -2.0 * GATE_CAP, GATE_CAP, ALU.mult, ALU.add).then_inc(ig_v_step, 1)
                    if i < NP:
                        kind, name, n = PIECES[i]
                        ps = piece_ps[i % 2]
                        if kind == "norm":
                            j = norm_pieces.index(i)
                            dve.wait_ge(sq_ready, j + 1)
                            if j >= 2:
                                dve.wait_ge(qk_ready, j - 1)
                            else:
                                dve.wait_ge(conv_ready, len(conv_pieces))
                            dve.tensor_scalar(ug[j % 2], ps[:, :], par[:, gain[name]:gain[name] + 1], None,
                                              ALU.mult).then_inc(bank_free[i % 2], 1)
                        elif kind == "conv":
                            j = conv_pieces.index(i)
                            dve.wait_ge(piece_done, i + 1)
                            if j >= 2:
                                dve.wait_ge(conv_ready, j - 1)
                            ch0 = (0 if name == "aq" else 4) + 2 * n
                            for w in range(4):
                                for half in range(2):
                                    ch = ch0 + half
                                    col = par[:, CONVW + 8 * w + ch:CONVW + 8 * w + ch + 1]
                                    y = ug[j % 2][:, SEQ * half:SEQ * half + SEQ]
                                    uu = ps[:, SEQ * half:SEQ * half + SEQ]
                                    if w == 0:
                                        ins = dve.tensor_scalar(y, uu, col, par[:, CONVB + ch:CONVB + ch + 1], ALU.mult, ALU.add)
                                    else:
                                        dve.wait_ge(v_step, steps - 1)
                                        ins = dve.scalar_tensor_tensor(out=y[:, w:], in0=uu[:, :SEQ - w], scalar=col,
                                                                       in1=y[:, w:], op0=ALU.mult, op1=ALU.add)
                                    if w == 3 and half == 1:
                                        ins.then_inc(bank_free[i % 2], 1)
                                    else:
                                        ins.then_inc(v_step, 1)
                                        steps += 1
                                    if w == 3 and half == 0:
                                        dve.wait_ge(v_step, steps)
                        elif kind == "igate":
                            dve.wait_ge(piece_done, i + 1)
                            z3 = ig_z.rearrange("p (t n) -> p t n", t=TT)
                            e3 = ig_e.rearrange("p (t n) -> p t n", t=TT)
                            for t in range(TT):
                                ins = dve.tensor_tensor(z3[:, t, :], ps[:, 8 * t:8 * t + 8], bc_small[:, 0:8], ALU.add)
                                ins.then_inc(bank_free[i % 2] if t else ig_v_step, 1)
                            dve.wait_ge(ig_v_step, 1)
                            dve.wait_ge(bank_free[i % 2], freed(i))
                            dve.scalar_tensor_tensor(out=e3[:, :, 4:8], in0=z3[:, :, 4:8], scalar=-1.0, in1=z3[:, :, 4:8],
                                                     op0=ALU.mult, op1=ALU.max).then_inc(ig_v_step, 1)
                            dve.tensor_scalar(z3[:, :, 4:8], z3[:, :, 4:8], 0.0, None, ALU.min).then_inc(ig_v_step, 1)

                dve.wait_ge(router_in, 16 * 5)
                dve.tensor_tensor(w_rt[:, :, :], w_rt[:, :, :], g2[:, :].unsqueeze(2).to_broadcast([P, KD, GROUPS + EXPERTS]),
                                  ALU.mult).then_inc(wrt_ready, 1)
                for j in range(12):
                    i = NP + j
                    dve.wait_ge(piece_done, i + 1)
                    p = gate_pieces[j]
                    if p in late_gates:
                        dve.wait_ge(gate_ready, late_gates.index(p) + 1)
                    else:
                        dve.wait_ge(bank_free[p % 2], freed(p))
                    dst = yT[:, 2 * j:2 * j + 2, :].rearrange("p n t -> p (n t)") if j < 4 else sq[j % 2]
                    if j >= 6:
                        dve.wait_ge(y_ready, j - 5)
                    dve.tensor_tensor(dst, piece_ps[i % 2][:, :], gate_of(j),
                                      ALU.mult).then_inc(zg_ready, 1)
                def link(ins):
                    nonlocal steps
                    ins.then_inc(v_step, 1)
                    steps += 1
                    dve.wait_ge(v_step, steps)

                def columns(t):
                    nonlocal steps
                    R = rt_of(t)
                    dve.wait_ge(pos_done, t + 1)
                    ranks, starts = pos_ps[t][:, 0:EXPERTS], pos_ps[t][:, EXPERTS:2 * EXPERTS]
                    for values, junk, found in ((ranks, R["junk"], R["rank"]), (starts, R["junk2"], R["pos"])):
                        for j, one_hot in enumerate((R["o1"], R["o2"])):
                            dve.tensor_tensor_reduce(junk[:, EXPERTS * j:EXPERTS * j + EXPERTS], one_hot, values, 1.0, 0.0,
                                                     ALU.mult, ALU.add, found[:, j:j + 1]).then_inc(v_step, 1)
                            steps += 1
                    dve.wait_ge(v_step, steps)
                    link(dve.tensor_tensor(R["pos"], R["pos"], R["rank"], ALU.add))
                    numbers = c("iota")[:, 0:2 * P]
                    link(dve.tensor_scalar(sel_g[t], numbers, R["pos"][:, 0:1], None, ALU.is_equal))
                    dve.scalar_tensor_tensor(out=sel_g[t], in0=numbers, scalar=R["pos"][:, 1:2], in1=sel_g[t],
                                             op0=ALU.is_equal, op1=ALU.add).then_inc(sel_ready, 1)

                def offsets(t):
                    nonlocal steps
                    last = TT * WINDOWS * EXPERTS
                    for j in range(WINDOWS):
                        at = EXPERTS * (WINDOWS * t + j)
                        dve.tensor_scalar(offs_f[:, at:at + EXPERTS], pos_ps[t][0:1, EXPERTS:2 * EXPERTS],
                                          float(TWIN * j + 2 * P * t), float(2 * P * (t + 1)), ALU.add, ALU.min).then_inc(v_step, 1)
                        steps += 1
                    link(dve.tensor_reduce(offs_f[:, last + t:last + t + 1], pos_ps[t][0:1, 2 * EXPERTS:3 * EXPERTS], AX_X, ALU.max))

                def add_x(j):
                    i = NP + 12 + j
                    t, half = j // 2, j % 2
                    dve.wait_ge(piece_done, i + 1)
                    o = xs[:, t, 512 * half:512 * half + 512]
                    dve.tensor_tensor(o, piece_ps[i % 2][:, :], o, ALU.add).then_inc(x1_ready, 1)

                def route(t):
                    nonlocal steps
                    R = rt_of(t)
                    dve.wait_ge(lg_done, t + 1)
                    link(dve.scalar_tensor_tensor(out=R["lg"], in0=logit_ps[t][:, 0:GROUPS + EXPERTS], scalar=rstd2[:, t:t + 1],
                                                  in1=bc_small[:, 8:44], op0=ALU.mult, op1=ALU.add))
                    link(dve.tensor_reduce(R["gm"], R["lg"][:, 0:GROUPS], AX_X, ALU.max))
                    dve.tensor_scalar(R["ngm"], R["gm"], -1.0, None, ALU.mult).then_inc(hot_ready, 1)
                    link(dve.scalar_tensor_tensor(out=R["g4"], in0=R["lg"][:, 0:GROUPS], scalar=R["gm"], in1=c("prig"),
                                                  op0=ALU.is_equal, op1=ALU.mult))
                    link(dve.tensor_reduce(R["gi"], R["g4"], AX_X, ALU.max))
                    link(dve.tensor_scalar(R["g4"], c("prig"), R["gi"], 1.0, ALU.is_equal, ALU.subtract))
                    link(dve.scalar_tensor_tensor(out=R["el"].rearrange("p (g e) -> p g e", g=GROUPS),
                                                  in0=R["g4"].unsqueeze(2).to_broadcast([P, GROUPS, PER_GROUP]), scalar=-NEG,
                                                  in1=R["lg"][:, GROUPS:].rearrange("p (g e) -> p g e", g=GROUPS),
                                                  op0=ALU.mult, op1=ALU.add))
                    for j, hot in enumerate((R["o1"], R["o2"])):
                        m, idx = R["m"][:, j:j + 1], R["i"][:, j:j + 1]
                        link(dve.tensor_reduce(m, R["el"], AX_X, ALU.max))
                        link(dve.scalar_tensor_tensor(out=hot, in0=R["el"], scalar=m, in1=c("pri"), op0=ALU.is_equal, op1=ALU.mult))
                        link(dve.tensor_reduce(idx, hot, AX_X, ALU.max))
                        link(dve.tensor_scalar(hot, c("pri"), idx, None, ALU.is_equal))
                        if j == 0:
                            link(dve.scalar_tensor_tensor(out=R["el"], in0=hot, scalar=3 * NEG, in1=R["el"], op0=ALU.mult, op1=ALU.add))
                    dve.tensor_tensor(R["d"], R["m"][:, 1:2], R["m"][:, 0:1], ALU.subtract).then_inc(hot_ready, 1)
                    dve.tensor_tensor(R["hot"], R["o1"], R["o2"], ALU.add).then_inc(v_step, 1)
                    steps += 1
                    link(dve.tensor_scalar(R["bef"], c("pri"), R["i"][:, 0:1], None, ALU.is_lt))
                    dve.scalar_tensor_tensor(out=R["bef"], in0=c("pri"), scalar=R["i"][:, 1:2], in1=R["bef"], op0=ALU.is_lt,
                                             op1=ALU.add).then_inc(hot_ready, 1)

                add_x(0)
                add_x(1)
                dve.wait_ge(xh_step, 1)
                dve.tensor_scalar(xhat[:, 0, :], xs[:, 0, :], rstd2[:, 0:1], None, ALU.mult).then_inc(xh_ready, 1)
                add_x(2)
                route(0)
                add_x(3)
                for half in range(2):
                    dve.wait_ge(th_done, 2 + half + 1)
                    dve.tensor_copy(tT[:, 4 * half:4 * half + 4, P:2 * P],
                                    turned_x_ps[1][half][:, :].rearrange("p (k n) -> p k n", k=4)).then_inc(tT_ready, 1)
                columns(0)
                dve.wait_ge(xh_step, 2)
                route(1)
                offsets(0)
                columns(1)
                offsets(1)
                at = TT * WINDOWS * EXPERTS
                link(dve.tensor_tensor(offs_f[:, at:at + 1], offs_f[:, at:at + 1], offs_f[:, at + 1:at + 2], ALU.max))
                dve.tensor_copy(offs_i[:, :], offs_f[:, :]).then_inc(offs_ready, 1)
                dve.wait_ge(offs_ready, 1)
                first_offs = [window(dve, e, j) for e, j in experts_of(0)]
                for k in (2, 3):
                    dve.wait_ge(ga_done, (KD + k) // 2 + 1)
                    dve.tensor_scalar(gathered(1, k), gather_ps(k), g2[:, k:k + 1], None, ALU.mult).then_inc(xg_ready_v, 1)
                dve.wait_ge(xg_ready_a, KD + 6)
                dve.wait_ge(xg_ready_v, 2)
                dve.wait_ge(pads_ready, 2)
                pass_tokens(dve, FAST, 0, experts_of(0), first_offs)
                W = [rt_of(t)["w"] for t in range(TT)]
                dve.wait_ge(rt_exp, 2 * TT)
                for t in range(TT):
                    R = rt_of(t)
                    dve.tensor_scalar(W[t][:, 0:1], R["e2"], 1.0, R["gs"], ALU.add, ALU.mult).then_inc(v_step, 1)
                    dve.tensor_scalar(pair_key[:, 2 * t:2 * t + 2], R["i"], -float(P), float(P * EXPERTS), ALU.mult,
                                      ALU.add).then_inc(v_step, 1)
                    steps += 2
                dve.wait_ge(v_step, steps)
                for t in range(TT):
                    dve.reciprocal(W[t][:, 0:1], W[t][:, 0:1]).then_inc(v_step, 1)
                    dve.tensor_tensor(pair_key[:, 2 * t:2 * t + 2], pair_key[:, 2 * t:2 * t + 2], rt_of(t)["rank"],
                                      ALU.add).then_inc(v_step, 1)
                    steps += 2
                dve.wait_ge(v_step, steps)
                for t in range(TT):
                    dve.tensor_tensor(W[t][:, 1:2], W[t][:, 0:1], rt_of(t)["e2"], ALU.mult).then_inc(v_step, 1)
                    steps += 1
                dve.tensor_copy(rel[:, :], pair_key[:, :]).then_inc(rel_ready, 1)
                dve.wait_ge(v_step, steps)
                dve.wait_ge(rel_ready, 1)
                for m in range(TURNS):
                    dve_pass(dve, FAST, m, P, 2 * P, experts_of(m + 1))
                with dve.Fori(1, LOOPS) as i:
                    for q in range(TURNS):
                        m = i * TURNS + q
                        dve_pass(dve, FAST, m, P, 2 * P, experts_of(m + 1))
                for m in range(LOOPS * TURNS, PASSES):
                    dve_pass(dve, FAST, m, P, 2 * P, experts_of(m + 1) if m + 1 < PASSES else None)
                results(dve, FAST)
                with general_path(dve):
                    dve.tensor_copy(rel[:, :], pair_key[:, :]).then_inc(rel_ready, 1)
                    dve.wait_ge(rel_ready, 2)
                    pass_tokens(dve, GENERAL, 0, [(0, 0), (0, 1)])

                    def expert(e):
                        dve_pass(dve, GENERAL, 2 * e, TWIN, 2 * TWIN, [(e, 2), (e, 3)])
                        is_last = isinstance(e, int) and e == EXPERTS - 1
                        dve_pass(dve, GENERAL, 2 * e + 1, TWIN, 2 * TWIN, None if is_last else [(e + 1, 0), (e + 1, 1)])

                    every_expert(dve, expert)
                    results(dve, GENERAL)

            @block.tensor
            def _(pe):
                pe.wait_ge(const_in, 16)
                pe.wait_ge(norm1_in, 16)
                pe.transpose(sum_ps[:, 0:8], small[0:8, :], c("ident", 8)[:, 0:8]).then_inc(par_ps, 1)
                for t in range(TT):
                    pe.wait_ge(xn_done, t + 1)
                    for k in range(KD):
                        ins = pe.transpose(xT_ps(k)[:, P * t:P * t + P], work[:, 2048 + 1024 * t + P * k:2048 + 1024 * t + P * k + P], ident)
                        if t == TT - 1:
                            ins.then_inc(xT_done, 1)

                def unit_steps(i):
                    u = unit_in_slot(i, 0)
                    if u is not None:
                        br, h = UNITS[u]
                        if u >= 1:
                            pe.wait_ge(sc_read, u)
                        if br in "BC":
                            pe.wait_ge(qk_ready, 4 if br == "C" else 8)
                            pairs = ([(0, score_ps[0], "cq", "ck", h), (64, score_ps[1], "cq", "ck", h)] if br == "C"
                                     else [(64 * (h % 2), score_ps[u % 2], "bq", "bk", h // 2)])
                            dk = 64
                        else:
                            pe.wait_ge(conv_ready, 4)
                            pe.wait_ge(ig_v_step, 9)
                            pairs = [(0, score_ps[0], "aq", "ak", h)]
                            dk = P
                        for r0, ps, qn, kn, ch in pairs:
                            q, k = qk[r0:r0 + dk, QK[qn] + ch, :], qk[r0:r0 + dk, QK[kn] + ch, :]
                            pe.matmul(ps[:, 0:128], q[:, 0:128], k[:, 0:128], start=True, stop=True)
                            ins = pe.matmul(ps[:, 128:384], q[:, 128:256], k[:, 0:256], start=True, stop=True)
                        if br == "A":
                            for t in range(TT):
                                ins = pe.matmul(score_ps[1][:, P * t:P * t + P], src[:, 4 * t + h:4 * t + h + 1].to_broadcast([P, P]),
                                                ident, start=True, stop=True)
                        ins.then_inc(sc_done, 1)
                    u = unit_in_slot(i, 1)
                    if u is not None:
                        pe.wait_ge(p_ready, u + 1)
                        if u >= 1:
                            pe.wait_ge(pt_ready, u)
                        S = (S1 if UNITS[u][0] == "B" else S2)[u % 2]
                        for j in range(3):
                            ins = pe.transpose(turn_ps[:, P * j:P * j + P], S[:, P * j:P * j + P], ident)
                        ins.then_inc(tp_done, 1)
                    u = unit_in_slot(i, 2)
                    if u is not None:
                        br, h = UNITS[u]
                        pe.wait_ge(pt_ready, u + 1)
                        if u >= 1:
                            pe.wait_ge(hx_ready, u)
                        name, dv = dict(A=("av", 128), B=("bv", 64), C=("cv", 128))[br]
                        if h == 0:
                            wait_values(pe, name)
                        v = vals[:, VAL[name], :, dv * h:dv * h + dv]
                        pe.matmul(value_ps[:, 0:dv], PT[0][:, 0:128], v[:, 0, :], start=True, stop=True)
                        pe.matmul(value_ps[:, dv:2 * dv], PT[0][:, 128:256], v[:, 0, :], start=True, stop=False)
                        pe.matmul(value_ps[:, dv:2 * dv], PT[0][:, 256:384], v[:, 1, :], start=False, stop=True).then_inc(pv_done, 1)
                    u = unit_in_slot(i, 3)
                    if u is not None and u in turned:
                        nx = turned.index(u)
                        pe.wait_ge(hx_ready, u + 1)
                        if nx >= 1:
                            pe.wait_ge(branch_ready, nx)
                        for t in range(TT):
                            ins = pe.transpose(outT_ps[:, P * t:P * t + P], hx[nx % 2][:, t, :], ident)
                        ins.then_inc(xt_done, 1)

                def input_gates(part):
                    for j in range(4 * part, 4 * part + 4):
                        t, k = j // KD, j % KD
                        ins = pe.matmul(piece_ps[IG % 2][:, 8 * t:8 * t + 8], hT[:, k, P * t:P * t + P], w_if[:, k, :],
                                        start=(k == 0), stop=(k == KD - 1))
                    return ins

                def head_sums(i):
                    if i >= 1 and i - 1 in norm_pieces:
                        j = norm_pieces.index(i - 1)
                        pe.wait_ge(sq_ready, j + 1)
                        if j >= 1:
                            pe.wait_ge(rs_ready, j)
                        else:
                            pe.wait_ge(par_ready, 2)
                        pe.matmul(sum_ps[:, :], c("blocks"), sq[j % 2], start=True, stop=True).then_inc(ss_done, 1)

                for i in range(NP + DRAIN + 1):
                    if i == 3:
                        pe.wait_ge(lead_in, LEAD)
                        for j in range(3):
                            ins = pe.matmul(outT_ps[:, 4 * j:4 * j + 4], t5hot[0:T5_BUCKETS, P * j:P * j + P], t5[:, :], start=True, stop=True)
                        ins.then_inc(t5_ps, 1)
                    if i == IG + 3:
                        pe.wait_ge(ig_v_step, 8)
                    unit_steps(i)
                    if i < NP:
                        kind, name, n = PIECES[i]
                        ps = piece_ps[i % 2]
                        if i >= 2 and i != IG:
                            pe.wait_ge(bank_free[i % 2], freed(i - 2))
                        b = piece_block[i]
                        if b is not None:
                            if i == 0:
                                pe.wait_ge(half_in, 16)
                            else:
                                pe.wait_ge(block_in[b % 2], 16 * (b // 2 + 1))
                            w = block_sb(b, KD)
                        if kind == "igate":
                            continue
                        if kind == "value":
                            for k in range(KD):
                                if k == KD // 2:
                                    head_sums(i)
                                    if i == IG - 1:
                                        pe.wait_ge(bank_free[IG % 2], freed(IG - 2))
                                ins = pe.matmul(ps[:, :], hT[:, k, P * n:P * n + P], w[:, k, :], start=(k == 0), stop=(k == KD - 1))
                                if i == IG - 1 and k == KD - 1:
                                    ins.then_inc(piece_done, 1)
                                if i == IG - 1 and k >= KD // 2:
                                    ins = input_gates(k - KD // 2)
                        else:
                            for half in range(2):
                                if half and i == 0:
                                    pe.wait_ge(params_in, 16 * 4)
                                    pe.wait_ge(par_ready, 1)
                                    pe.transpose(sum_ps[:, 0:52], small[0:52, :], c("ident", 52)[:, 0:52]).then_inc(par_ps, 1)
                                if half:
                                    head_sums(i)
                                ch = 2 * (n % 2) + half
                                for k in range(KD):
                                    if i == 0 and half == 0:
                                        pe.wait_ge(hT_ready[k // 4], max(k, 1) % 4 + 1)
                                    ins = pe.matmul(ps[:, SEQ * half:SEQ * half + SEQ], w[:, k, P * ch:P * ch + P], hT[:, k, :],
                                                    start=(k == 0), stop=(k == KD - 1))
                        ins.then_inc(piece_done, 1)

                    if i == IG + 2:
                        pe.wait_ge(ig_v_step, 7)
                        pe.wait_ge(t5v_ready, 1)
                        pe.matmul(outT_ps[:, 0:4], c("tri"), lf[:, 0:4], start=True, stop=True)
                        pe.matmul(outT_ps[:, 4:8], ones, lf[:, 0:4], start=True, stop=False)
                        pe.matmul(outT_ps[:, 4:8], c("tri"), lf[:, 4:8], start=False, stop=True).then_inc(ig_p_step, 1)

                for j in range(12):
                    i, b = NP + j, n_in + j // 4
                    pe.wait_ge(bank_free[i % 2], freed(i - 2)) if j < 2 else pe.wait_ge(zg_ready, j - 1)
                    pe.wait_ge(block_in[b % 2], 16 * (b // 2 + 1))
                    if j % 4 == 0:
                        pe.wait_ge(branch_ready, {0: 4, 4: 8, 8: 12}[j])
                    w = block_sb(b, 4)
                    for half in range(2):
                        ch = 2 * (j % 4) + half
                        for k in range(4):
                            ins = pe.matmul(piece_ps[i % 2][:, SEQ * half:SEQ * half + SEQ], w[:, k, P * ch:P * ch + P],
                                            branchT[:, BRANCH_ORDER[j // 4], k, :], start=(k == 0), stop=(k == 3))
                    ins.then_inc(piece_done, 1)
                def turn_tokens(t):
                    pe.wait_ge(x1_ready, 2 * t + 2)
                    for half in range(2):
                        for k in range(4 * half, 4 * half + 4):
                            ins = pe.transpose(turned_x_ps[t][half][:, P * (k % 4):P * (k % 4) + P], xs[:, t, k:D:KD], ident)
                        ins.then_inc(th_done, 1)

                def logits(t):
                    pe.wait_ge(tT_ready, 2 * t + 2)
                    for k in range(KD):
                        ins = pe.matmul(logit_ps[t][:, 0:GROUPS + EXPERTS], tT[:, k, P * t:P * t + P], w_rt[:, k, :],
                                        start=(k == 0), stop=(k == KD - 1))
                    ins.then_inc(lg_done, 1)

                pe.wait_ge(y_ready, 7)
                pe.wait_ge(wrt_ready, 1)
                pe.wait_ge(rs_ready, len(norm_pieces))
                pe.wait_ge(branch_ready, 12)
                for j in range(4):
                    i, t, half = NP + 12 + j, j // 2, j % 2
                    b = n_in + 3 + half
                    pe.wait_ge(zg_ready, 11 + j) if j < 2 else pe.wait_ge(x1_ready, j - 1)
                    pe.wait_ge(*((last_block_in, 16) if half else (block_in[b % 2], 16 * (b // 2 + 1))))
                    w = block_sb(b, KD)
                    for k in range(KD):
                        if j == 0 and k == KD - 2:
                            pe.wait_ge(y_ready, 8)
                        if j == 3 and k == 2:
                            logits(0)
                        ins = pe.matmul(piece_ps[i % 2][:, :], yT[:, k, P * t:P * t + P], w[:, k, :], start=(k == 0), stop=(k == KD - 1))
                    ins.then_inc(piece_done, 1)
                    if j == 2:
                        turn_tokens(0)

                def positions(t):
                    pe.wait_ge(hot_ready, 3 * t + 3)
                    pe.wait_ge(tT_ready, t + 1)
                    pe.matmul(pos_ps[t][:, 0:EXPERTS], c("strict"), rt_of(t)["hot"], start=True, stop=True)
                    pe.matmul(pos_ps[t][:, EXPERTS:3 * EXPERTS], ones, rt_of(t)["both"], start=True, stop=True).then_inc(pos_done, 1)

                def gather(t):
                    pe.wait_ge(xh_ready, t + 1)
                    pe.wait_ge(sel_ready, t + 1)
                    for k in range(KD):
                        if t and k % 2 == 0:
                            pe.wait_ge(xg_ready_a, k + 2)
                        ins = pe.matmul(gather_ps(k), xhat[:, t, k:D:KD], sel_g[t], start=True, stop=True)
                        if k % 2:
                            ins.then_inc(ga_done, 1)

                def keep_clock(n):
                    for _ in range(n):
                        pe.matmul(side_ps[:, :], ident, c("iota"), start=True, stop=True)

                positions(0)
                turn_tokens(1)
                keep_clock(1)
                logits(1)
                gather(0)
                keep_clock(1)
                positions(1)
                keep_clock(2)
                gather(1)
                pe.wait_ge(xg_ready_a, KD + 6)
                pe.wait_ge(xg_ready_v, 2)
                pe.wait_ge(offs_ready, 1)

                for m in range(TURNS):
                    pe_pass(pe, FAST, m, (2 * m, 2 * m + 1), before=m > 0, weights=weights_in(m, 1),
                            up=pass_up if m else pass_gate_then_up)
                with pe.Fori(1, LOOPS - 1) as i:
                    for q in range(TURNS):
                        pe_pass(pe, FAST, i * TURNS + q, (2 * q, 2 * q + 1), weights=weights_in(q, i + 1))
                for m in range((LOOPS - 1) * TURNS, PASSES):
                    q = m % TURNS
                    pe_pass(pe, FAST, m, (2 * q, 2 * q + 1), weights=weights_in(q, m // TURNS + 1),
                            up=pass_up if m < PASSES - 2 else pass_gate_then_up)
                last_combine(pe, FAST, PASSES - 1)
                with general_path(pe):
                    pe.wait_ge(FAST["out_ready"], 4)

                    def expert(e):
                        pe.wait_ge(general_in, (e + 1) * 48)
                        for j in range(2):
                            pe_pass(pe, GENERAL, 2 * e + j, (0, 0), before=j > 0 or not first(e))

                    every_expert(pe, expert)
                    last_combine(pe, GENERAL, 2 * EXPERTS - 1)


_INS = ['x', 'norm1_g', 'w_in', 'a_conv_w', 'a_conv_b', 'a_gate_bias', 'a_out_norm_g', 'b_qk_norm_g', 'b_rel_bias',
        'c_qk_norm_g', 'c_lambda', 'c_sub_norm_g', 't5_bias', 'w_branch', 'w_out', 'norm2_g', 'w_group', 'b_group',
        'w_router', 'b_router', 'w_e_gate', 'w_e_up', 'w_e_down']


def kernel(**inputs):
    import numpy as _np
    import concourse.bacc as _bacc
    from concourse import mybir as _mybir
    from concourse.bass_utils import run_bass_kernel_spmd as _run

    nc = _bacc.Bacc("TRN2", target_bir_lowering=False, num_devices=1)
    arrays, args = {}, []
    for name in _INS:
        a = _np.ascontiguousarray(inputs[name])
        arrays[f"in_{name}_dram"] = a
        args.append(nc.dram_tensor(f"in_{name}_dram", a.shape, _mybir.dt.from_np(a.dtype), kind="ExternalInput").ap())
    arrays["constants_dram"] = constants()
    consts = nc.dram_tensor("constants_dram", (P, CONST_WIDTH), F32, kind="ExternalInput").ap()
    scratch = nc.dram_tensor("t5_by_position", (3 * P * C_HEADS,), F32, kind="Internal").ap()
    out = nc.dram_tensor("out_0_dram", (1, SEQ, D), F32, kind="ExternalOutput").ap()
    build_hybrid_layer(nc, *args, consts, scratch, out)
    r = _run(nc, [arrays], core_ids=[0])
    return r.results[0]["out_0_dram"]
```
